# Optimizing a Trainium2 kernel written in Bass

```python
import jax, jax.numpy as jnp
from jax import lax
import numpy as np

D_MODEL = 1024
BATCH = 1
SEQ = 512
DEPTH = 2

GRID_W = 64
CTX_LEN = 256
MIX_WIDTH = D_MODEL
ATTN_WIDTH = MIX_WIDTH // 2
POOL_WIDTH = MIX_WIDTH // 4
CONV_WIDTH = MIX_WIDTH - ATTN_WIDTH - POOL_WIDTH
NOPE_DIM = 128
ROPE_DIM = 64
V_DIM = 128
MLA_HEADS = ATTN_WIDTH // V_DIM
Q_RANK = D_MODEL // 4
KV_RANK = D_MODEL // 8
QK_DIM = NOPE_DIM + ROPE_DIM
SOFTMAX_SCALE = QK_DIM ** -0.5
ROPE_THETA = 10000.0
POOL_WINDOWS = (2, 4, 8, 16)
POOL_GROUPS = len(POOL_WINDOWS)
POOL_CH = POOL_WIDTH // POOL_GROUPS
CONV_K = 3
D_FF = ((8 * D_MODEL // 3 + 127) // 128) * 128
Q_BLOCK = 128
EPS = 1e-6
IN_SIZES = (Q_RANK, KV_RANK, ROPE_DIM, POOL_WIDTH, CONV_WIDTH, CONV_WIDTH, CONV_WIDTH)
IN_WIDTH = sum(IN_SIZES)
IN_SPLITS = tuple(int(s) for s in np.cumsum(IN_SIZES)[:-1])

kernel_name = 'hybrid_mla_pool_shortconv_dit'

def rmsnorm(x, g):
    xf = x.astype(jnp.float32)
    y = xf * lax.rsqrt(jnp.mean(xf * xf, axis=-1, keepdims=True) + EPS)
    return (y * g.astype(jnp.float32)).astype(x.dtype)

def adaln(cvec, w, b):
    m = jax.nn.silu(cvec) @ w + b
    m = m.reshape(-1, 1, 6 * D_MODEL)
    return jnp.split(m, 6, axis=-1)

def axial_rope_tables(n_tokens):
    rows = n_tokens // GRID_W
    row = jnp.repeat(jnp.arange(rows), GRID_W).astype(jnp.float32)
    col = jnp.tile(jnp.arange(GRID_W), rows).astype(jnp.float32)
    n_freq = ROPE_DIM // 4
    inv = ROPE_THETA ** (-jnp.arange(n_freq, dtype=jnp.float32) / n_freq)
    ar = row[:, None] * inv
    ac = col[:, None] * inv
    ang = jnp.concatenate([ar, ar, ac, ac], axis=-1)
    return jnp.cos(ang), jnp.sin(ang)

def apply_axial_rope(x, cos, sin):
    n_freq = ROPE_DIM // 4
    xr = x.reshape(x.shape[:-1] + (2, 2, n_freq))
    rot = jnp.stack([-xr[..., 1, :], xr[..., 0, :]], axis=-2).reshape(x.shape)
    return x * cos.astype(x.dtype) + rot * sin.astype(x.dtype)

def dwconv3(u, w):
    up = jnp.pad(u, ((0, 0), (1, 1), (0, 0)))
    return up[:, :-2] * w[0] + up[:, 1:-1] * w[1] + up[:, 2:] * w[2]

def mixer_features(h, w_in, qc_g, kvc_g, w_q_up, w_kv_up, qn_g, qr_g, kn_g, kr_g, rope):
    b, n, _ = h.shape
    q_lat, kv_lat, k_rope, pool_in, gate_b, gate_c, conv_in = jnp.split(h @ w_in, IN_SPLITS, axis=-1)
    q = (rmsnorm(q_lat, qc_g) @ w_q_up).reshape(b, n, MLA_HEADS, QK_DIM)
    kv = (rmsnorm(kv_lat, kvc_g) @ w_kv_up).reshape(b, n, MLA_HEADS, NOPE_DIM + V_DIM)
    q_nope = rmsnorm(q[..., :NOPE_DIM], qn_g)
    q_rope = rmsnorm(q[..., NOPE_DIM:], qr_g)
    k_nope = rmsnorm(kv[..., :NOPE_DIM], kn_g)
    v = kv[..., NOPE_DIM:]
    k_rope = rmsnorm(k_rope, kr_g)
    if rope is not None:
        cos, sin = rope
        q_rope = apply_axial_rope(q_rope, cos[:, None, :], sin[:, None, :])
        k_rope = apply_axial_rope(k_rope, cos, sin)
    attn_in = (q_nope * SOFTMAX_SCALE, q_rope * SOFTMAX_SCALE, k_nope, k_rope, v)
    return attn_in, (pool_in, gate_b, gate_c, conv_in)

def attend(q_nope, q_rope, k_nope, k_rope, v):
    s = jnp.einsum('bqhd,bkhd->bhqk', q_nope, k_nope) + jnp.einsum('bqhr,bkr->bhqk', q_rope, k_rope)
    p = jax.nn.softmax(s.astype(jnp.float32), axis=-1).astype(v.dtype)
    o = jnp.einsum('bhqk,bkhd->bqhd', p, v)
    return o.reshape(o.shape[0], o.shape[1], ATTN_WIDTH)

def blocked_attention(q_nope, q_rope, k_nope, k_rope, v):
    b, n = q_nope.shape[:2]
    nblk = n // Q_BLOCK
    qn = q_nope.reshape(b, nblk, Q_BLOCK, MLA_HEADS, NOPE_DIM).swapaxes(0, 1)
    qr = q_rope.reshape(b, nblk, Q_BLOCK, MLA_HEADS, ROPE_DIM).swapaxes(0, 1)
    o = lax.map(lambda qs: attend(qs[0], qs[1], k_nope, k_rope, v), (qn, qr))
    return o.swapaxes(0, 1).reshape(b, n, ATTN_WIDTH)

def multiscale_pool(p, w, scale):
    b, n, _ = p.shape
    cs = jnp.pad(jnp.cumsum(p.astype(jnp.float32), axis=1), ((0, 0), (1, 0), (0, 0)))
    t = jnp.arange(n)
    means = []
    for g, win in enumerate(POOL_WINDOWS):
        lo = jnp.clip(t - win // 2, 0, n)
        hi = jnp.clip(t + win // 2, 0, n)
        csg = cs[..., g * POOL_CH:(g + 1) * POOL_CH]
        total = jnp.take(csg, hi, axis=1) - jnp.take(csg, lo, axis=1)
        means.append(total / (hi - lo).astype(jnp.float32)[None, :, None])
    pooled = jnp.stack(means, axis=2).astype(p.dtype)
    diff = pooled - p.reshape(b, n, POOL_GROUPS, POOL_CH)
    y = jnp.einsum('bngc,gcd->bngd', diff, w).reshape(b, n, POOL_WIDTH)
    return y * scale

def mixer_output(attn, other, pool_w, pool_scale, sconv_w, w_o):
    pool_in, gate_b, gate_c, conv_in = other
    pool_out = multiscale_pool(pool_in, pool_w, pool_scale)
    conv_out = gate_b * dwconv3(gate_c * conv_in, sconv_w)
    return jnp.concatenate([attn, pool_out, conv_out], axis=-1) @ w_o

def conv_ffn(h, w_up, w_conv, w_down):
    g, u = jnp.split(h @ w_up, 2, axis=-1)
    return (jax.nn.silu(dwconv3(g, w_conv)) * u) @ w_down

def setup_inputs(seed: int = 0) -> dict:
    key = jax.random.key(seed)
    ks = jax.random.split(key, 24)

    def nrm(k, shape, s):
        return jax.random.normal(k, shape, jnp.float32) * s

    def gain(k, shape):
        return 1.0 + 0.1 * jax.random.normal(k, shape, jnp.float32)

    return {
        'x': nrm(ks[0], (BATCH, SEQ, D_MODEL), 1.0),
        'c': nrm(ks[1], (BATCH, D_MODEL), 1.0),
        'ctx': nrm(ks[2], (BATCH, CTX_LEN, D_MODEL), 1.0),
        'c_ctx': nrm(ks[3], (D_MODEL,), 1.0),
        'ada_w': nrm(ks[4], (DEPTH, D_MODEL, 6 * D_MODEL), 0.5 * D_MODEL ** -0.5),
        'ada_b': nrm(ks[5], (DEPTH, 6 * D_MODEL), 0.02),
        'norm1_g': gain(ks[6], (DEPTH, D_MODEL)),
        'norm2_g': gain(ks[7], (DEPTH, D_MODEL)),
        'w_in': nrm(ks[8], (DEPTH, D_MODEL, IN_WIDTH), D_MODEL ** -0.5),
        'qc_g': gain(ks[9], (DEPTH, Q_RANK)),
        'kvc_g': gain(ks[10], (DEPTH, KV_RANK)),
        'w_q_up': nrm(ks[11], (DEPTH, Q_RANK, MLA_HEADS * QK_DIM), Q_RANK ** -0.5),
        'w_kv_up': nrm(ks[12], (DEPTH, KV_RANK, MLA_HEADS * (NOPE_DIM + V_DIM)), KV_RANK ** -0.5),
        'qn_g': gain(ks[13], (DEPTH, NOPE_DIM)),
        'qr_g': gain(ks[14], (DEPTH, ROPE_DIM)),
        'kn_g': gain(ks[15], (DEPTH, NOPE_DIM)),
        'kr_g': gain(ks[16], (DEPTH, ROPE_DIM)),
        'pool_w': nrm(ks[17], (DEPTH, POOL_GROUPS, POOL_CH, POOL_CH), POOL_CH ** -0.5),
        'pool_scale': gain(ks[18], (DEPTH, POOL_WIDTH)),
        'sconv_w': nrm(ks[19], (DEPTH, CONV_K, CONV_WIDTH), CONV_K ** -0.5),
        'w_o': nrm(ks[20], (DEPTH, MIX_WIDTH, D_MODEL), MIX_WIDTH ** -0.5),
        'ff_up': nrm(ks[21], (DEPTH, D_MODEL, 2 * D_FF), D_MODEL ** -0.5),
        'ff_conv': nrm(ks[22], (DEPTH, CONV_K, D_FF), CONV_K ** -0.5),
        'ff_down': nrm(ks[23], (DEPTH, D_FF, D_MODEL), D_FF ** -0.5),
    }

def reference(x, c, ctx, c_ctx, ada_w, ada_b, norm1_g, norm2_g, w_in, qc_g, kvc_g, w_q_up, w_kv_up,
              qn_g, qr_g, kn_g, kr_g, pool_w, pool_scale, sconv_w, w_o, ff_up, ff_conv, ff_down):
    n = x.shape[1]
    rope = axial_rope_tables(n)
    for i in range(DEPTH):
        feat_w = (w_in[i], qc_g[i], kvc_g[i], w_q_up[i], w_kv_up[i], qn_g[i], qr_g[i], kn_g[i], kr_g[i])
        out_w = (pool_w[i], pool_scale[i], sconv_w[i], w_o[i])
        ffn_w = (ff_up[i], ff_conv[i], ff_down[i])
        sh1x, sc1x, g1x, sh2x, sc2x, g2x = adaln(c, ada_w[i], ada_b[i])
        sh1c, sc1c, g1c, sh2c, sc2c, g2c = adaln(c_ctx, ada_w[i], ada_b[i])

        hx = rmsnorm(x, norm1_g[i]) * (1 + sc1x) + sh1x
        hc = rmsnorm(ctx, norm1_g[i]) * (1 + sc1c) + sh1c
        (qn_x, qr_x, kn_x, kr_x, v_x), rest_x = mixer_features(hx, *feat_w, rope)
        (qn_c, qr_c, kn_c, kr_c, v_c), rest_c = mixer_features(hc, *feat_w, None)

        k_nope = jnp.concatenate([kn_x, kn_c], axis=1)
        k_rope = jnp.concatenate([kr_x, kr_c], axis=1)
        v = jnp.concatenate([v_x, v_c], axis=1)
        attn_x = blocked_attention(qn_x, qr_x, k_nope, k_rope, v)
        x = x + g1x * mixer_output(attn_x, rest_x, *out_w)
        x = x + g2x * conv_ffn(rmsnorm(x, norm2_g[i]) * (1 + sc2x) + sh2x, *ffn_w)

        if i < DEPTH - 1:
            attn_c = attend(qn_c, qr_c, kn_c, kr_c, v_c)
            ctx = ctx + g1c * mixer_output(attn_c, rest_c, *out_w)
            ctx = ctx + g2c * conv_ffn(rmsnorm(ctx, norm2_g[i]) * (1 + sc2c) + sh2c, *ffn_w)
    return x


_drawn_inputs = setup_inputs


def setup_inputs(seed=0):
    import zlib

    import numpy as np

    out = dict(_drawn_inputs(seed))
    spreads = {}
    factors = {'ctx': 5.397,
     'qc_g': 8.0,
     'kvc_g': 6.173,
     'qn_g': 8.0,
     'qr_g': 8.0,
     'kn_g': 8.0,
     'kr_g': 8.0,
     'pool_scale': 3.074}
    for name, (base, spread) in spreads.items():
        noise = np.random.default_rng([zlib.crc32(name.encode()), seed]).standard_normal(out[name].shape)
        drawn = base * np.exp(spread * noise) if base else spread * noise
        out[name] = __import__('jax').numpy.asarray(drawn.astype(out[name].dtype))
    for name, factor in factors.items():
        out[name] = (out[name] * factor).astype(out[name].dtype)
    return out
```

```python
import numpy as np
import concourse.bass as bass
from concourse import mybir
from contextlib import ExitStack

F32 = mybir.dt.float32
F32R = mybir.dt.float32r
ALU = mybir.AluOpType
ACT = mybir.ActivationFunctionType
AX = mybir.AxisListType

P = 128
D = 1024
KD = D // P
DEPTH = 2
NX, NC = 512, 256
NT = NX + NC
TOK = NT // P
XTOK = NX // P
GRID_W = 64
HEADS = 4
NOPE, ROPE = 128, 64
SCALE = (NOPE + ROPE) ** -0.5
QR, KVR = 256, 128
LATW = QR + KVR + ROPE
HQ = NOPE + ROPE
QKW = HQ + NOPE
DFF = 2816
FT = DFF // P
FP = FT // 2
EPS = 1e-6
CH = 1024
ADC = 512
ADB = 6 * D // ADC
PAD = 8

C_LAT, C_A2, C_WO, C_FF = 0, 4, 12, 20
NCH = C_FF + 6 * FP
SPARE = 4
V_N1, V_N2, V_ADAB, V_QC, V_KVC, V_QN, V_KN, V_PS, V_SC, V_FC = 0, 8, 16, 64, 66, 67, 68, 69, 71, 77
V_LAYER = V_FC + 3 * FT
V_C = DEPTH * V_LAYER
V_INVW = V_C + 16
V_RATIO = V_INVW + 2
V_EPS = V_RATIO + 32
NV = V_EPS + 1


def job_plan():
    plan, n = {}, 0
    for name, count in [("ada", 4)]:
        plan[name] = n
        n += count
    for L in range(DEPTH):
        for name, count in [("norm1", 1), ("lat", 3), ("a2", 8), ("latT", 4), ("pool", 2), ("b0", 7),
                            ("heads", 16 * (HEADS - 1)), ("last", 9), ("wo", 8), ("norm2", 1), ("u0", 4),
                            ("ff", 24 * ((FP - 1) // 2)), ("dlast", 8)]:
            plan[name, L] = n
            n += count
    return plan


JOB = job_plan()


def build(nc, dram):
    ctx = ExitStack()
    base = (nc.sbuf_base + 31) // 32 * 32

    def at(name, off, shape, dt=F32):
        return nc.alloc_sbuf_tensor_at(name, shape, dt, offset=base + off)

    class Place:
        def __init__(self, off):
            self.off = off

        def __call__(self, name, shape, dt=F32, extra=0):
            t = at(name, self.off, shape, dt)
            self.off += (4 * int(np.prod(shape[1:])) + extra + 31) // 32 * 32
            return t

    sb = Place(0)
    X = sb("X", [P, KD, NT])
    vec = sb("vec", [P, NV + (-NV) % 8])
    mod = [sb(f"mod{L}", [P, 2, 48]) for L in range(DEPTH)]
    csil = sb("csil", [P, 16])
    amul = sb("amul", [P, 2, 8])
    qg = sb("qg", [P, 8])
    lat_ss = sb("lat_ss", [P, 3, TOK])
    head_ss = sb("head_ss", [P, 3, TOK])
    nmax = sb("nmax", [P, 8])
    rsum = sb("rsum", [P, 8])
    ident = sb("ident", [P, P])
    ones = sb("ones", [P, P])
    poolw = sb("poolw", [P, 2, P])
    rgain = sb("rgain", [P, 4, ROPE])
    junk = rgain[:].rearrange("p n f -> p (n f)")
    rtab = sb("rtab", [P, 4, TOK, ROPE])
    w_raw = [sb(f"w_raw{s}", [P, CH]) for s in range(2)]
    w_hi = [sb(f"w_hi{s}", [P, CH], F32R) for s in range(4)]
    w_lo = [sb(f"w_lo{s}", [P, CH], F32R) for s in range(4)]
    HWC = 2 * HQ + 2 * NOPE
    hw_raw = sb("hw_raw", [P, HWC])
    hw_hi = sb("hw_hi", [P, HWC], F32R)
    hw_lo = sb("hw_lo", [P, HWC], F32R)
    mid = Place(sb.off)
    ql = [mid(f"ql_{x}", [P, 2, NT], F32R) for x in ("hi", "lo")]
    kvl = [mid(f"kvl_{x}", [P, NT], F32R) for x in ("hi", "lo")]
    kr = [mid(f"kr_{x}", [P, NT], F32R) for x in ("hi", "lo")]
    ymix = [None] * 4
    for j in (0, 2, 3):
        ymix[j] = mid(f"ymix{j}", [P, NT])
    win_a = at("win_a", mid.off, [P, NT + 4 * PAD])
    ymix[1] = mid("ymix1", [P, NT], F32, extra=4 * 4 * PAD)
    cat_y = [at(f"cat_y_{x}", sb.off + 4 * 4 * NT * n, [P, 4, NT], F32R) for n, x in enumerate(("hi", "lo"))]
    ph = Place(mid.off)
    ada_raw = [ph(f"ada_raw{s}", [P, ADC]) for s in range(4)]
    ada_acc = ph("ada_acc", [P, 2, ADC])
    ada_end = ph.off
    tmp = [ph(f"tmp{s}", [P, NT]) for s in range(2)]
    ss = ph("ss", [P, NT])
    lo_free = ph.off
    H = [ph(f"H_{x}", [P, KD, NT], F32R) for x in ("hi", "lo")]
    latr = ph("latr", [P, TOK, LATW])
    win_p = ph("win_p", [P, NT + 4 * PAD])
    win_r = ph("win_r", [P, NT + 4 * PAD])
    hd = Place(mid.off)
    q = [hd(f"q_{x}", [P, NT], F32R) for x in ("hi", "lo")]
    qr = [hd(f"qr_{x}", [P, NT], F32R) for x in ("hi", "lo")]
    k = [hd(f"k_{x}", [P, NT], F32R) for x in ("hi", "lo")]
    v = [hd(f"v_{x}", [P, NT], F32R) for x in ("hi", "lo")]
    pt = [[hd(f"pt_{x}{s}", [P, NX], F32R) for s in range(4)] for x in ("hi", "lo")]
    prob = hd("prob", [P, XTOK, NT])
    probc = hd("probc", [P, 2, NC])
    qkt = hd("qkt", [P, TOK, QKW])
    rt = [hd(f"rt{s}", [P, TOK, ROPE]) for s in range(2)]
    assert hd.off >= lo_free
    cat_a = [hd(f"cat_a_{x}", [P, 4, NT], F32R) for x in ("hi", "lo")]
    ff = Place(sb.off)
    inner = [[ff(f"inner_{x}{b}", [P, 2, NT], F32R) for b in range(2)] for x in ("hi", "lo")]
    ff_v = ff("ff_v", [P, NT])
    assert ff.off <= mid.off

    ps_t = ctx.enter_context(nc.psum_tensor("ps", [P, 8, 512], F32))
    ps_all = ps_t[:].rearrange("p b n -> p (b n)")

    def sem(name):
        return ctx.enter_context(nc.semaphore(name))

    def sems(name, n=DEPTH):
        return [sem(f"{name}{i}") for i in range(n)]

    full, free = sems("psum_full", 4), sems("psum_free", 4)
    chunk_in = sems("chunk_in", 2)
    chunk_hi, chunk_lo, lat_used = sem("chunk_hi"), sem("chunk_lo"), sem("lat_used")
    hw_in, hw_hid, hw_lod = sem("hw_in"), sem("hw_hi_done"), sem("hw_lo_done")
    ada_in = sems("ada_in", 4)
    ada_op, mod_done = sem("ada_op"), sem("mod_done")
    vec_in, x_in, tab_in, csil_done = sem("vec_in"), sem("x_in"), sem("tab_in"), sem("csil_done")
    consts, poolw_zero, poolw_in, out_in = sem("consts"), sem("poolw_zero"), sem("poolw_in"), sem("out_in")
    sq_done, ss_done, scale_ok, t_done, h_hi, h_lo = (
        sems(n, 4) for n in ("sq_done", "ss_done", "scale_ok", "t_done", "h_hi", "h_lo"))
    (lat_sq, lat_ms, lat_rt, lat_nm, lat_hi, kr_rot, tab_ok, win_st, win_ok, pdiff, cv, b_sq, b_ms, b_rt, b_rot, b_hi,
     s_max, s_rec, s_p, pt_hi, pv_used, ca_hi, cy_hi, cy_lo, ff_mid, ff_conv, ff_silu, ff_hi, ff_lo) = (
        sems(n) for n in ("lat_sq", "lat_ms", "lat_rt", "lat_nm", "lat_hi", "kr_rot", "tab_ok", "win_st", "win_ok",
                          "pdiff", "cv", "b_sq", "b_ms", "b_rt", "b_rot", "b_hi", "s_max", "s_rec", "s_p", "pt_hi",
                          "pv_used", "ca_hi", "cy_hi", "cy_lo", "ff_mid", "ff_conv", "ff_silu", "ff_hi", "ff_lo"))

    block = ctx.enter_context(nc.Block())

    ALL = [(0, 0, NX), (1, NX, NT)]

    def segs(L):
        return ALL if L == 0 else ALL[:1]

    def nsegs(nn):
        return ALL if nn < 3 else ALL[:1]

    def width(L):
        return NT if L == 0 else NX

    def qtok(L):
        return TOK if L == 0 else XTOK

    class Job:
        def __init__(self, n, i=0, per=0):
            self.slot, self.count, self.i, self.step = n % 4, n // 4, i, per // 4
            assert per % 4 == 0

        def times(self, extra):
            n = self.count + extra
            return n + self.i * self.step if self.step else n

        def ps(self, a=0, b=1024):
            return ps_all[:, self.slot * 1024 + a:self.slot * 1024 + b]

        def open(self, pe):
            if self.count:
                pe.wait_ge(free[self.slot], self.times(0))

        def filled(self, ins):
            ins.then_inc(full[self.slot], 1)

        def ready(self, eng):
            eng.wait_ge(full[self.slot], self.times(1))

        def last_read(self, ins):
            ins.then_inc(free[self.slot], 1)

        def taken(self, eng):
            eng.wait_ge(free[self.slot], self.times(1))

    def V(L, off, n=1):
        return vec[:, L * V_LAYER + off:L * V_LAYER + off + n]

    TJOBS = [[(0, 1), (2, 3), (4, 5), (6,)], [(0, 1), (2, 3), (4,), (5,)]]
    ENTRIES = [7, 6]
    LAT_SQ = [3 * qtok(L) + 2 * (TOK - qtok(L)) for L in range(DEPTH)]
    B_SQ = [3 * qtok(L) + (TOK - qtok(L)) for L in range(DEPTH)]
    J_S, J_B, J_BT, J_T, J_PV, J_V, J_HEAD = 0, 4, 7, (10, 11, 13, 14), 12, 15, 16
    ROLES = ("pool", "gate_c", "conv_in", "gate_b")

    @block.sync
    def _(sp):
        def load(c, i=0, per=0):
            if c >= 2:
                sp.wait_ge(chunk_lo, c - 1 + per * i if per else c - 1)
            src = dram["w_main"][c + per * i] if per else dram["w_main"][c]
            sp.dma_start(w_raw[c % 2][:], src).then_inc(chunk_in[c % 2], 16)

        def load_head(n):
            if n >= 1:
                sp.wait_ge(hw_lod, n)
            sp.dma_start(hw_raw[:], dram["w_head"][n]).then_inc(hw_in, 16)

        def load_ada(c, i=0, per=0):
            if c >= 4:
                sp.wait_ge(ada_op, 2 * c - 6 + 2 * per * i if per else 2 * c - 6)
            src = dram["w_ada"][c + per * i] if per else dram["w_ada"][c]
            sp.dma_start(ada_raw[c % 4][:], src).then_inc(ada_in[c % 4], 16)

        def load_tables(L):
            for n in (0, 2):
                sp.dma_start(rtab[:, n:n + 2], dram["rope"]).then_inc(tab_in, 16)
            sp.dma_start(rgain[:], dram["rgain"][L].partition_broadcast(P)).then_inc(tab_in, 16)
            for g in range(4):
                p0 = 64 * (g % 2)
                sp.dma_start(poolw[p0:p0 + 64, g // 2, p0:p0 + 64], dram["pool_w"][L, g]).then_inc(poolw_in, 16)

        sp.dma_start(vec[:, 0:NV], dram["vec"]).then_inc(vec_in, 16)
        for c in range(4):
            load_ada(c)
        sp.dma_start(X[:, :, 0:NX], dram["x"]).then_inc(x_in, 16)
        sp.dma_start(X[:, :, NX:NT], dram["ctx"]).then_inc(x_in, 16)
        load(0)
        load(1)
        load_head(0)
        sp.wait_ge(poolw_zero, 1)
        load_tables(0)
        for c in range(32):
            load_ada(c + 4)
        for c in range(4):
            load(c + 2)
        for L in range(DEPTH):
            c0 = NCH * L
            load_head(HEADS * L + 1)
            for j in range(4):
                load(c0 + 6 + j)
            if L == 0:
                for m in range(8):
                    load_ada(8 * 4 + m + 4)
            for j in range(8):
                if L == 0 and j in (2, 4, 6):
                    for m in range(8):
                        if 8 * (4 + j // 2) + m + 4 < 64:
                            load_ada(8 * (4 + j // 2) + m + 4)
                load(c0 + 10 + j)
            load_head(HEADS * L + 2)
            load_head(HEADS * L + 3)
            if L == 0:
                load_head(HEADS)
                Job(JOB["last", 0] + 3).ready(sp)
                for c in range(64, 68):
                    load_ada(c)
            with sp.Fori(0, 2) as i:
                for j in range(4):
                    if L == 0:
                        for m in range(4):
                            load_ada(8 * (8 + j // 2) + 4 * (j % 2) + m + 4, i, 16)
                    load(c0 + 18 + j, i, 4)
            if L == 0:
                for m in range(8):
                    load_ada(8 * 12 + m + 4)
            for j in range(4):
                load(c0 + 26 + j)
            if L == 0:
                b_rot_done = 3 * HEADS
                sp.wait_ge(b_rot[0], b_rot_done)
                load_tables(1)
            with sp.Fori(0, (FP - 1) // 2) as i:
                for d in range(2):
                    c = c0 + 30 + 6 * d
                    for t in range(2):
                        for x in range(2):
                            load(c + 2 * t + x, i, 12)
                        if L == 0:
                            for m in (2 * t, 2 * t + 1):
                                load_ada(8 * (13 + d) + m + 4, i, 16)
                    if L == 0:
                        for m in range(4, 8):
                            load_ada(8 * (13 + d) + m + 4, i, 16)
                    for x in range(2):
                        load(c + 4 + x, i, 12)
            if L == 0:
                for c in range(8 * 23 + 4, 8 * 24):
                    load_ada(c)
                for j in range(2):
                    load(c0 + NCH + 4 + j)
        for m in range(KD):
            Job(JOB["dlast", 1] + m).taken(sp)
            sp.dma_start(dram["out"][m], X[:, m, 0:NX]).then_inc(out_in, 16)
        sp.wait_ge(out_in, 16 * KD)
        for s in range(2):
            sp.wait_ge(chunk_in[s], 8 * (DEPTH * NCH + SPARE))

    @block.gpsimd
    def _(pool):
        pool.memset(poolw[:], 0.0).then_inc(poolw_zero, 1)
        pool.memset(ones[:], 1.0).then_inc(consts, 1)
        pool.memset(ident[:], 0.0).then_inc(consts, 1)
        pool.memset(lat_ss[:], 1.0).then_inc(consts, 1)
        pool.memset(head_ss[:], 1.0).then_inc(consts, 1)
        pool.wait_ge(consts, 4)
        pool.affine_select(out=ident[:], in_=ident[:], compare_op=ALU.not_equal, fill=1.0, base=0,
                           pattern=[[-1, P]], channel_multiplier=1).then_inc(consts, 1)

        def rotate(src, n, tab, done, before, scratch):
            def halves(x):
                return x.rearrange("p t (a h f) -> p t a h f", a=2, h=2)
            a, b = scratch[0][:, 0:n], scratch[1][:, 0:n]
            pool.tensor_tensor(a, src, rtab[:, tab, 0:n], ALU.mult).then_inc(done, 1)
            for h in range(2):
                for ax in range(2):
                    last = pool.tensor_tensor(halves(b)[:, :, ax, h], halves(src)[:, :, ax, 1 - h],
                                              halves(rtab[:, tab + 1, 0:n])[:, :, ax, h], ALU.mult)
            last.then_inc(done, 1)
            pool.wait_ge(done, before + 2)
            pool.tensor_tensor(src, a, b, ALU.add).then_inc(done, 1)

        for L in range(DEPTH):
            W = width(L) + (4 if L == 0 else 2) * PAD
            streams = [(PAD, NX)] + ([(NX + 3 * PAD, NC)] if L == 0 else [])
            st = 0

            def step(ins):
                nonlocal st
                st += 1
                ins.then_inc(win_st[L], 1)
            pool.wait_ge(h_lo[2 * L], KD)
            for o, n in streams:
                pool.memset(win_p[:, o - PAD:o], 0.0)
                last = pool.memset(win_p[:, o + n:o + n + PAD], 0.0)
            step(last)
            for m in range(2):
                if m == 1:
                    pool.wait_ge(pdiff[L], 1)
                Job(JOB["a2", L] + 4 * m).taken(pool)
                pool.wait_ge(win_st[L], st)
                if m == 0:
                    pool.tensor_tensor(win_r[0:64, 1:W], win_p[0:64, 0:W - 1], win_p[0:64, 1:W], ALU.add)
                    step(pool.tensor_tensor(win_a[64:P, 1:W], win_p[64:P, 0:W - 1], win_p[64:P, 1:W], ALU.add))
                    pool.wait_ge(win_st[L], st)
                    step(pool.tensor_tensor(win_r[64:P, 2:W - 1], win_a[64:P, 1:W - 2], win_a[64:P, 3:W], ALU.add))
                else:
                    step(pool.tensor_tensor(win_a[:, 1:W], win_p[:, 0:W - 1], win_p[:, 1:W], ALU.add))
                    pool.wait_ge(win_st[L], st)
                    step(pool.tensor_tensor(win_r[:, 2:W - 1], win_a[:, 1:W - 2], win_a[:, 3:W], ALU.add))
                    pool.wait_ge(win_st[L], st)
                    step(pool.tensor_tensor(win_a[:, 4:W - 3], win_r[:, 2:W - 5], win_r[:, 6:W - 1], ALU.add))
                    pool.wait_ge(win_st[L], st)
                    pool.tensor_copy(win_r[0:64, 8:W - 8], win_a[0:64, 8:W - 8])
                    step(pool.tensor_tensor(win_r[64:P, 8:W - 7], win_a[64:P, 4:W - 11], win_a[64:P, 12:W - 3],
                                            ALU.add))
                pool.wait_ge(win_st[L], st)
                for o, n in streams:
                    for e, c in ((0, o), (1, o + n - PAD)):
                        r = V_RATIO + 16 * m + 8 * e
                        last = pool.tensor_tensor(win_r[:, c:c + 8], win_r[:, c:c + 8], vec[:, r:r + 8], ALU.mult)
                last.then_inc(win_ok[L], 1)
            pool.wait_ge(pdiff[L], 2)
            pool.wait_ge(lat_nm[L], 3)
            pool.wait_ge(tab_ok[L], 5)
            scratch = [x[:, 0:TOK * ROPE].rearrange("p (t f) -> p t f", t=TOK) for x in (win_p, win_r)]
            rotate(latr[:, :, QR + KVR:LATW], TOK, 2, kr_rot[L], 0, scratch)

            def head_rope(j, i, per, h):
                Job(j, i, per).taken(pool)
                rotate(qkt[:, 0:qtok(L), NOPE:HQ], qtok(L), 0, b_rot[L], 3 * h, rt)
            head_rope(JOB["b0", L] + 2, 0, 0, 0)
            with pool.Fori(0, HEADS - 1) as h:
                head_rope(JOB["heads", L] + J_B + 2, h, J_HEAD, h + 1)

    @block.tensor
    def _(pe):
        def mm3(out, w, wsl, x, xsl, first, last):
            (wh, wl), (xh, xl) = w, x
            pe.matmul(out, wh[wsl], xh[xsl], start=first, stop=False)
            pe.matmul(out, wh[wsl], xl[xsl], start=False, stop=False)
            return pe.matmul(out, wl[wsl], xh[xsl], start=False, stop=last)

        def ada_reduce(job, b_op):
            pe.wait_ge(ada_op, b_op)
            for s in range(2):
                for c in range(4):
                    o = 768 + 4 * s + c
                    last = pe.matmul(job.ps(o, o + 1), ada_acc[:, s, P * c:P * (c + 1)], ones[:, 0:1],
                                     start=True, stop=True)
            return last

        def norm_sum(nn, job):
            job.open(pe)
            pe.wait_ge(ss_done[nn], KD + 2)
            for _, a, b in nsegs(nn):
                last = pe.matmul(job.ps(a, b), ones[:], ss[:, a:b], start=True, stop=True)
            job.filled(last)

        def part(job, sg, w, wc, x, xk, first, last):
            wsl = slice(wc, wc + P)
            for n, (ww, xx) in enumerate(((w[0], x[0]), (w[0], x[1]), (w[1], x[0]))):
                for _, a, b in sg:
                    ins = pe.matmul(job.ps(a, b), ww[:, wsl], xx[:, xk, a:b], start=first and n == 0,
                                    stop=last and n == 2)
            return ins

        def slot(c):
            return w_hi[c % 4], w_lo[c % 4]

        pe.wait_ge(consts, 5)
        for b in range(4):
            job = Job(JOB["ada"] + b)
            job.filled(ada_reduce(job, 16 * (b + 1)))
        for L in range(DEPTH):
            sg, c0 = segs(L), NCH * L
            norm_sum(2 * L, Job(JOB["norm1", L]))
            jobs = [Job(JOB["lat", L] + j) for j in range(3)]
            for j in jobs:
                j.open(pe)
            for kk in range(KD):
                if kk % 2 == 0:
                    pe.wait_ge(chunk_lo, c0 + kk // 2 + 1)
                pe.wait_ge(h_lo[2 * L], kk + 1)
                wo = (kk % 2) * LATW
                for t in range(TOK):
                    a = 0 if t < qtok(L) else QR
                    o = 512 * (t % 2)
                    last = mm3(jobs[t // 2].ps(o + a, o + LATW), H, (slice(None), kk, slice(P * t, P * (t + 1))),
                               slot(c0 + kk // 2), (slice(None), slice(wo + a, wo + LATW)), kk == 0, kk == KD - 1)
                    if kk == KD - 1 and t % 2 == 1:
                        jobs[t // 2].filled(last)
                if kk % 2 == 1 and kk < KD - 1:
                    last.then_inc(lat_used, 1)
            with pe.Fori(0, 2) as i:
                for j in range(4):
                    job = Job(JOB["a2", L] + j, i, 4)
                    c = c0 + C_A2 + j
                    pe.wait_ge(chunk_lo, c + 1 + 4 * i)
                    job.open(pe)
                    for kk in range(KD):
                        last = part(job, sg, slot(c), P * kk, H, kk, kk == 0, kk == KD - 1)
                    if L == 0 and j % 2 == 1:
                        last = ada_reduce(job, 16 * (5 + j // 2) + 32 * i)
                    job.filled(last)
            for n, (a, b) in enumerate(((0, P), (P, QR), (QR, QR + KVR), (QR + KVR, LATW))):
                job = Job(JOB["latT", L] + n)
                job.open(pe)
                if n == 0:
                    pe.wait_ge(lat_nm[L], 3)
                if n == 3:
                    pe.wait_ge(kr_rot[L], 3)
                for t in range(qtok(L) if n < 2 else TOK):
                    last = pe.transpose(job.ps(P * t, P * (t + 1))[0:b - a], latr[:, t, a:b], ident[:])
                job.filled(last)
            pe.wait_ge(poolw_in, 64 * (L + 1))
            for m in range(2):
                job = Job(JOB["pool", L] + m)
                job.open(pe)
                pe.wait_ge(pdiff[L], m + 1)
                for _, a, b in sg:
                    last = pe.matmul(job.ps(a, b), poolw[:, m], ymix[m][:, a:b], start=True, stop=True)
                job.filled(last)

            def b_tokens(j0, i, per, h):
                pe.wait_ge(hw_lod, HEADS * L + 1 + h)
                for j in range(3):
                    job = Job(j0 + j, i, per)
                    job.open(pe)
                    for t in (2 * j, 2 * j + 1):
                        o, tsl = 512 * (t % 2), slice(P * t, P * (t + 1))
                        for kk in range(2 if t < qtok(L) else 0):
                            mm3(job.ps(o, o + HQ), ql, (slice(None), kk, tsl), (hw_hi, hw_lo),
                                (slice(None), slice(HQ * kk, HQ * (kk + 1))), kk == 0, kk == 1)
                        last = mm3(job.ps(o + HQ, o + QKW), kvl, (slice(None), tsl), (hw_hi, hw_lo),
                                   (slice(None), slice(2 * HQ, 2 * HQ + NOPE)), True, True)
                    job.filled(last)

            def b_turn(j0, jt, i, per, h):
                for n, (a, b, nt) in enumerate(((0, NOPE, qtok(L)), (HQ, QKW, TOK), (NOPE, NOPE + P, qtok(L)))):
                    job = Job(jt + n, i, per)
                    job.open(pe)
                    if n == 0:
                        Job(j0 + 2, i, per).taken(pe)
                    if n == 2:
                        pe.wait_ge(b_rot[L], 3 * h + 3)
                    for t in range(nt):
                        last = pe.transpose(job.ps(P * t, P * (t + 1)), qkt[:, t, a:b], ident[:])
                    job.filled(last)

            def b_v(j, i, per):
                job = Job(j, i, per)
                job.open(pe)
                for t in range(TOK):
                    last = mm3(job.ps(P * t, P * (t + 1)), kvl, (slice(None), slice(P * t, P * (t + 1))),
                               (hw_hi, hw_lo), (slice(None), slice(2 * HQ + NOPE, HWC)), True, True)
                job.filled(last)

            def scores(j0, i, per):
                for t in range(XTOK):
                    job = Job(j0 + t, i, per)
                    job.open(pe)
                    parts = [(t, 0, NX, 0), (t, NX, NT, NX)]
                    if L == 0 and t < 2:
                        parts.append((XTOK + t, NX, NT, NT))
                    for qt, ka, kb, o in parts:
                        qs = slice(P * qt, P * (qt + 1))
                        mm3(job.ps(o, o + kb - ka), q, (slice(None), qs), k, (slice(None), slice(ka, kb)), True, False)
                        last = mm3(job.ps(o, o + kb - ka), qr, (slice(0, ROPE), qs), kr,
                                   (slice(0, ROPE), slice(ka, kb)), False, True)
                    job.filled(last)

            def attend(js, jpv, i, per, h):
                pv = Job(jpv, i, per)

                def turn(n):
                    job = Job(js[n], i, per)
                    job.open(pe)
                    for m, e in enumerate(TJOBS[L][n]):
                        if e < 6:
                            for t in range(XTOK):
                                if n == 0 and m == 0:
                                    pe.wait_ge(s_p[L], 4 * h + (t + 1))
                                o = 512 * m + P * t
                                last = pe.transpose(job.ps(o, o + P), prob[:, t, P * e:P * (e + 1)], ident[:])
                        else:
                            for kt in range(2):
                                for t in range(2):
                                    o = NC * kt + P * t
                                    last = pe.transpose(job.ps(o, o + P), probc[:, t, P * kt:P * (kt + 1)], ident[:])
                    job.filled(last)

                def values(n):
                    Job(js[n], i, per).taken(pe)
                    for e in TJOBS[L][n]:
                        if e == 0:
                            pv.open(pe)
                        p = (pt[0][e % 4], pt[1][e % 4])
                        if e < 6:
                            last = mm3(pv.ps(0, NX), v, (slice(None), slice(P * e, P * (e + 1))), p,
                                       (slice(None), slice(0, NX)), e == 0, e == 5)
                        else:
                            for kt in range(2):
                                last = mm3(pv.ps(NX, NT), v, (slice(None), slice(P * (4 + kt), P * (5 + kt))), p,
                                           (slice(None), slice(NC * kt, NC * (kt + 1))), kt == 0, kt == 1)
                        if e < ENTRIES[L] - 1:
                            last.then_inc(pv_used[L], 1)
                        else:
                            pv.filled(last)
                turn(0)
                turn(1)
                values(0)
                turn(2)
                values(1)
                turn(3)
                values(2)
                values(3)

            b0 = JOB["b0", L]
            Job(JOB["latT", L] + 3).taken(pe)
            b_tokens(b0, 0, 0, 0)
            b_turn(b0, b0 + 3, 0, 0, 0)
            b_v(b0 + 6, 0, 0)
            Job(b0 + 6).taken(pe)
            j0 = JOB["heads", L]
            with pe.Fori(0, HEADS - 1) as h:
                scores(j0 + J_S, h, J_HEAD)
                b_tokens(j0 + J_B, h, J_HEAD, h + 1)
                b_turn(j0 + J_B, j0 + J_BT, h, J_HEAD, h + 1)
                attend([j0 + x for x in J_T], j0 + J_PV, h, J_HEAD, h)
                b_v(j0 + J_V, h, J_HEAD)
                Job(j0 + J_V, h, J_HEAD).taken(pe)
            j0 = JOB["last", L]
            scores(j0, 0, 0)
            attend([j0 + 4, j0 + 5, j0 + 7, j0 + 8], j0 + 6, 0, 0, HEADS - 1)
            pe.wait_ge(cy_lo[L], 4)
            Job(j0 + 6).taken(pe)
            with pe.Fori(0, 2) as i:
                for j in range(4):
                    job = Job(JOB["wo", L] + j, i, 4)
                    c = c0 + C_WO + j
                    pe.wait_ge(chunk_lo, c + 1 + 4 * i)
                    job.open(pe)
                    for n, kk in enumerate((4, 5, 6, 7, 0, 1, 2, 3)):
                        last = part(job, sg, slot(c), P * kk, cat_a if kk < 4 else cat_y, kk % 4, n == 0, n == 7)
                    if L == 0 and j % 2 == 1:
                        last = ada_reduce(job, 16 * (9 + j // 2) + 32 * i)
                    job.filled(last)
            norm_sum(2 * L + 1, Job(JOB["norm2", L]))

            def up_first(jn, c):
                jobs = [Job(jn + n) for n in range(4)]
                for j in jobs:
                    j.open(pe)
                pe.wait_ge(chunk_lo, c + 4)
                for kk in range(KD):
                    pe.wait_ge(h_lo[2 * L + 1], kk + 1)
                    for n in range(4):
                        last = part(jobs[n], sg, slot(c + n), P * kk, H, kk, kk == 0, kk == KD - 1)
                        if kk == KD - 1:
                            if L == 0 and n == 3:
                                last = ada_reduce(jobs[3], 16 * 13)
                            jobs[n].filled(last)

            def up(jn, c, i):
                for n in range(4):
                    job = Job(jn + n, i, 24)
                    pe.wait_ge(chunk_lo, c + n + 1 + 12 * i)
                    job.open(pe)
                    for kk in range(KD):
                        last = part(job, sg, slot(c + n), P * kk, H, kk, kk == 0, kk == KD - 1)
                    job.filled(last)

            def down(jn, c, p, buf, i, per_j, per_c, ada=None):
                pe.wait_ge(ff_lo[L], 2 * p + 2)
                pe.wait_ge(chunk_lo, c + 2 + per_c * i if per_c else c + 2)
                x = (inner[0][buf], inner[1][buf])
                for m in range(KD):
                    job = Job(jn + m, i, per_j)
                    job.open(pe)
                    for kk in range(2):
                        last = part(job, sg, slot(c + kk), P * m, x, kk, kk == 0, kk == 1)
                    if ada is not None and m == KD - 1:
                        last = ada_reduce(job, ada)
                    job.filled(last)

            up_first(JOB["u0", L], c0 + C_FF)
            jf = JOB["ff", L]
            with pe.Fori(0, (FP - 1) // 2) as i:
                for d in range(2):
                    c = c0 + C_FF + 4 + 6 * d
                    up(jf + 12 * d, c, i)
                    down(jf + 12 * d + 4, c + 4, 2 * i + d, d, i, 24, 12, 16 * (14 + d) + 32 * i if L == 0 else None)
            down(JOB["dlast", L], c0 + NCH - 2, FP - 1, 0, 0, 0, 0, 16 * 24 if L == 0 else None)

    @block.scalar
    def _(act):
        def split_hi(c, user=None, i=0, per=0):
            if user is not None:
                user.ready(act)
            n = 16 * (c // 2 + 1)
            act.wait_ge(chunk_in[c % 2], n + 8 * per * i if per else n)
            act.activation(w_hi[c % 4][:], w_raw[c % 2][:], ACT.Copy).then_inc(chunk_hi, 1)

        def head_hi(n):
            act.wait_ge(hw_in, 16 * n + 16)
            act.activation(hw_hi[:], hw_raw[:], ACT.Copy).then_inc(hw_hid, 1)

        def square(nn, m, par, job=None):
            w = NT if nn < 3 else NX
            if job is not None:
                job.taken(act)
            act.wait_ge(ss_done[nn], m + 1)
            act.activation(tmp[par][:, 0:w], X[:, m, 0:w], ACT.Square).then_inc(sq_done[nn], 1)

        def norm(nn, job):
            L, which, w = nn // 2, nn % 2, NT if nn < 3 else NX
            job.ready(act)
            job.last_read(act.activation(ss[:, 0:w], job.ps(0, w), ACT.Sqrt, bias=vec[:, V_EPS:V_EPS + 1],
                                         scale=1.0 / D))
            for kk in range(KD):
                act.wait_ge(t_done[nn], kk + 1)
                for s, a, b in nsegs(nn):
                    m = 24 * which + kk
                    last = act.activation(H[0][:, kk, a:b], tmp[kk % 2][:, a:b], ACT.Identity,
                                          bias=mod[L][:, s, m:m + 1])
                last.then_inc(h_hi[nn], 1)

        act.wait_ge(vec_in, 16)
        act.activation(csil[:], vec[:, V_C:V_C + 16], ACT.Silu).then_inc(csil_done, 1)
        act.wait_ge(x_in, 32)
        for m in range(KD):
            square(0, m, m % 2)
        for c in range(4):
            split_hi(c)
        head_hi(0)
        for L in range(DEPTH):
            c0, w = NCH * L, width(L)
            norm(2 * L, Job(JOB["norm1", L]))
            for j in range(4):
                if j < 3:
                    act.wait_ge(lat_used, 3 * L + j + 1)
                split_hi(c0 + 4 + j, Job(JOB["lat", L] + 2) if j == 3 else None)
            n = 0
            for t in range(TOK):
                if t % 2 == 0:
                    Job(JOB["lat", L] + t // 2).taken(act)
                for g, (a, b) in enumerate(((0, QR), (QR, QR + KVR), (QR + KVR, LATW))):
                    if g > 0 or t < qtok(L):
                        if n:
                            act.wait_ge(lat_sq[L], n)
                        act.activation(tmp[1][:, 0:b - a], latr[:, t, a:b], ACT.Square,
                                       accum_out=lat_ss[:, g, t:t + 1]).then_inc(lat_sq[L], 1)
                        n += 1
            assert n == LAT_SQ[L]
            act.wait_ge(lat_ms[L], 4)
            act.activation(lat_ss[:], lat_ss[:], ACT.Sqrt).then_inc(lat_rt[L], 1)
            for j in range(8):
                job = Job(JOB["a2", L] + j)
                if j % 4 == 0:
                    pdone = j // 4
                    if pdone:
                        act.wait_ge(pdiff[L], 1)
                    job.ready(act)
                    for s, a, b in segs(L):
                        o = PAD + a + 2 * PAD * s
                        last = act.activation(win_p[:, o:o + b - a], job.ps(a, b), ACT.Copy)
                    job.last_read(last)
                split_hi(c0 + 8 + j, job)
            for n in range(4):
                job = Job(JOB["latT", L] + n)
                job.ready(act)
                if n < 2:
                    ins = act.activation(ql[0][:, n, 0:w], job.ps(0, w), ACT.Copy, scale=V(L, V_QC + n))
                elif n == 2:
                    ins = act.activation(kvl[0][:], job.ps(0, NT), ACT.Copy, scale=V(L, V_KVC))
                else:
                    ins = act.activation(kr[0][0:ROPE], job.ps(0, NT)[0:ROPE], ACT.Copy)
                ins.then_inc(lat_hi[L], 1)
            for m in range(2):
                job = Job(JOB["pool", L] + m)
                job.ready(act)
                job.last_read(act.activation(ymix[m][:, 0:w], job.ps(0, w), ACT.Copy, scale=V(L, V_PS + m)))

            def b_stats(j0, i, per, h):
                n = 0
                for t in range(TOK):
                    job = Job(j0 + t // 2, i, per)
                    if t % 2 == 0:
                        job.ready(act)
                    for g, (a, b) in enumerate(((0, NOPE), (NOPE, HQ), (HQ, QKW))):
                        if g == 2 or t < qtok(L):
                            if n:
                                act.wait_ge(b_sq[L], B_SQ[L] * h + n)
                            o = 512 * (t % 2)
                            act.activation(junk[:, 0:b - a], job.ps(o + a, o + b), ACT.Square,
                                           accum_out=head_ss[:, g, t:t + 1]).then_inc(b_sq[L], 1)
                            n += 1
                assert n == B_SQ[L]
                act.wait_ge(b_ms[L], 4 * h + 4)
                act.activation(head_ss[:], head_ss[:], ACT.Sqrt).then_inc(b_rt[L], 1)

            def b_halves(j0, i, per):
                for n, (dst, rows, wn) in enumerate(((q, P, w), (k, P, NT), (qr, ROPE, w))):
                    job = Job(j0 + n, i, per)
                    job.ready(act)
                    kw = ({"scale": qg[:, 0:1]}, {"scale": V(L, V_KN)}, {})[n]
                    act.activation(dst[0][0:rows, 0:wn], job.ps(0, wn)[0:rows], ACT.Copy, **kw).then_inc(b_hi[L], 1)

            def v_half(j, i, per):
                job = Job(j, i, per)
                job.ready(act)
                act.activation(v[0][:], job.ps(0, NT), ACT.Copy).then_inc(b_hi[L], 1)

            def softmax(j0, i, per, h):
                for t in range(XTOK):
                    job = Job(j0 + t, i, per)
                    act.wait_ge(s_max[L], 4 * h + (t + 1))
                    ins = act.activation(prob[:, t], job.ps(0, NT), ACT.Exp, bias=nmax[:, t:t + 1],
                                         accum_out=rsum[:, t:t + 1])
                    if L == 0 and t < 2:
                        ins = act.activation(probc[:, t], job.ps(NT, 1024), ACT.Exp, bias=nmax[:, 4 + t:5 + t],
                                             accum_out=rsum[:, 4 + t:5 + t])
                    job.last_read(ins)

            def attend(js, jpv, i, per, h):
                for n in range(4):
                    job = Job(js[n], i, per)
                    job.ready(act)
                    for m, e in enumerate(TJOBS[L][n]):
                        if e >= 4:
                            act.wait_ge(pv_used[L], (ENTRIES[L] - 1) * h + (e - 3))
                        act.activation(pt[0][e % 4][:], job.ps(512 * m, 512 * (m + 1)),
                                       ACT.Copy).then_inc(pt_hi[L], 1)

            def attended(jpv, i, per, h):
                job = Job(jpv, i, per)
                job.ready(act)
                act.activation(cat_a[0][:, h, 0:w], job.ps(0, w), ACT.Copy).then_inc(ca_hi[L], 1)

            b0 = JOB["b0", L]
            b_stats(b0, 0, 0, 0)
            b_halves(b0 + 3, 0, 0)
            v_half(b0 + 6, 0, 0)
            j0 = JOB["heads", L]
            with act.Fori(0, HEADS - 1) as h:
                head_hi(h + (HEADS * L + 1))
                softmax(j0 + J_S, h, J_HEAD, h)
                b_stats(j0 + J_B, h, J_HEAD, h + 1)
                b_halves(j0 + J_BT, h, J_HEAD)
                attend([j0 + x for x in J_T], j0 + J_PV, h, J_HEAD, h)
                attended(j0 + J_PV, h, J_HEAD, h)
                v_half(j0 + J_V, h, J_HEAD)
            if L == 0:
                head_hi(HEADS)
            j0 = JOB["last", L]
            softmax(j0, 0, 0, HEADS - 1)
            attend([j0 + 4, j0 + 5, j0 + 7, j0 + 8], j0 + 6, 0, 0, HEADS - 1)
            Job(JOB["a2", L] + 7).taken(act)
            Job(JOB["pool", L] + 1).taken(act)
            for j in range(4):
                act.activation(cat_y[0][:, j, 0:w], ymix[j][:, 0:w], ACT.Copy).then_inc(cy_hi[L], 1)
            attended(j0 + 6, 0, 0, HEADS - 1)
            with act.Fori(0, 2) as i:
                for j in range(4):
                    job = Job(JOB["wo", L] + j, i, 4)
                    split_hi(c0 + 16 + j, job, i, 4)
                    square(2 * L + 1, 4 * i + j, j % 2, job)
            norm(2 * L + 1, Job(JOB["norm2", L]))

            def ff_tile(t, jn, c, par, buf, i, per_j, per_c):
                g, u = Job(jn, i, per_j), Job(jn + 1, i, per_j)
                g.ready(act)
                tap = vec[:, bass.ds(L * V_LAYER + V_FC + FT + t, 1)]
                act.activation(tmp[par][:, 0:w], g.ps(0, w), ACT.Copy, scale=tap).then_inc(ff_mid[L], 1)
                split_hi(c, g, i, per_c)
                g.taken(act)
                act.activation(tmp[par][:, 0:w], tmp[par][:, 0:w], ACT.Silu).then_inc(ff_silu[L], 1)
                split_hi(c + 1, u, i, per_c)
                u.taken(act)
                act.activation(inner[0][buf][:, par, 0:w], ff_v[:, 0:w], ACT.Copy).then_inc(ff_hi[L], 1)

            for t in range(2):
                ff_tile(t, JOB["u0", L] + 2 * t, c0 + C_FF + 4 + 2 * t, t, 0, 0, 0, 0)
            jf = JOB["ff", L]
            with act.Fori(0, (FP - 1) // 2) as i:
                for d in range(2):
                    c = c0 + C_FF + 4 + 6 * d
                    for t in range(2):
                        ff_tile(4 * i + (2 * (d + 1) + t), jf + 12 * d + 2 * t, c + 4 + 2 * t, t, 1 - d, i, 24, 12)
                    for x in range(2):
                        split_hi(c + 8 + x, Job(jf + 12 * d + 11, i, 24), i, 12)
            if L == 0:
                for m in range(KD):
                    square(2, m, m % 2, Job(JOB["dlast", 0] + m))
                for x in range(2):
                    split_hi(c0 + NCH + 2 + x, Job(JOB["dlast", 0] + 7))

    @block.vector
    def _(dve):
        def split_lo(c, i=0, per=0):
            dve.wait_ge(chunk_hi, c + 1 + per * i if per else c + 1)
            dve.tensor_tensor(w_lo[c % 4][:], w_raw[c % 2][:], w_hi[c % 4][:].bitcast(F32),
                              ALU.subtract).then_inc(chunk_lo, 1)

        def head_lo(n):
            dve.wait_ge(hw_hid, n + 1)
            dve.tensor_tensor(hw_lo[:], hw_raw[:], hw_hi[:].bitcast(F32), ALU.subtract).then_inc(hw_lod, 1)

        def ada_chunks(b, ks, i=0, per=0):
            for kk in ks:
                c = 8 * b + kk
                n = 16 * (c // 4 + 1)
                dve.wait_ge(ada_in[c % 4], n + 32 * per * i if per else n)
                for s in range(2):
                    cs = csil[:, 8 * s + kk:8 * s + kk + 1]
                    if kk == 0:
                        ins = dve.tensor_scalar(ada_acc[:, s], ada_raw[c % 4][:], cs, None, ALU.mult)
                    else:
                        done = 2 * c + s - 1
                        dve.wait_ge(ada_op, done + 16 * per * i if per else done)
                        ins = dve.scalar_tensor_tensor(ada_acc[:, s], ada_raw[c % 4][:], cs, ada_acc[:, s],
                                                       ALU.mult, ALU.add)
                    ins.then_inc(ada_op, 1)

        def ada_out(L, b, job):
            bias = vec[:, bass.ds(L * V_LAYER + V_ADAB + 4 * b, 4)].unsqueeze(1).to_broadcast([P, 2, 4])
            return dve.tensor_tensor(mod[L][:, :, bass.ds(4 * b, 4)],
                                     job.ps(768, 776).rearrange("p (s c) -> p s c", s=2), bias, ALU.add)

        def clear_ss(nn):
            dve.memset(ss[:, 0:NT if nn < 3 else NX], 0.0).then_inc(ss_done[nn], 2)

        def add_squares(nn, m, par):
            w = NT if nn < 3 else NX
            dve.wait_ge(sq_done[nn], m + 1)
            dve.wait_ge(ss_done[nn], m + 2)
            dve.tensor_tensor(ss[:, 0:w], ss[:, 0:w], tmp[par][:, 0:w], ALU.add).then_inc(ss_done[nn], 1)

        def norm(nn, job):
            L, which, w = nn // 2, nn % 2, NT if nn < 3 else NX
            if nn == 0:
                Job(JOB["ada"] + 3).taken(dve)
            else:
                dve.wait_ge(mod_done, ADB * L + (4 if which == 0 else 10) - 4)
            g = V(L, V_N1 if which == 0 else V_N2, 8).unsqueeze(1).to_broadcast([P, 2, 8])
            dve.scalar_tensor_tensor(amul[:], mod[L][:, :, 24 * which + 8:24 * which + 16], 1.0, g, ALU.add,
                                     ALU.mult).then_inc(scale_ok[nn], 1)
            job.taken(dve)
            dve.reciprocal(ss[:, 0:w], ss[:, 0:w]).then_inc(scale_ok[nn], 1)
            dve.wait_ge(scale_ok[nn], 2)

            def scaled(kk):
                if kk >= 2:
                    dve.wait_ge(h_lo[nn], kk - 1)
                for s, a, b in nsegs(nn):
                    last = dve.scalar_tensor_tensor(tmp[kk % 2][:, a:b], X[:, kk, a:b], amul[:, s, kk:kk + 1],
                                                    ss[:, a:b], ALU.mult, ALU.mult)
                last.then_inc(t_done[nn], 1)
            scaled(0)
            for kk in range(KD):
                if kk + 1 < KD:
                    scaled(kk + 1)
                dve.wait_ge(h_hi[nn], kk + 1)
                for s, a, b in nsegs(nn):
                    m = 24 * which + kk
                    last = dve.scalar_tensor_tensor(H[1][:, kk, a:b], tmp[kk % 2][:, a:b], mod[L][:, s, m:m + 1],
                                                    H[0][:, kk, a:b].bitcast(F32), ALU.add, ALU.subtract)
                last.then_inc(h_lo[nn], 1)

        def lo_half(dst, src, hi, scale=None):
            if scale is None:
                return dve.tensor_tensor(dst, src, hi.bitcast(F32), ALU.subtract)
            return dve.scalar_tensor_tensor(dst, src, scale, hi.bitcast(F32), ALU.mult, ALU.subtract)

        def update_x(m, L, job, gate, loop=False):
            for s, a, b in segs(L):
                xo = X[:, m, a:b]
                last = dve.scalar_tensor_tensor(xo, job.ps(a, b), mod[L][:, s, bass.ds(gate + m, 1)], xo,
                                                ALU.mult, ALU.add)
            job.last_read(last)

        clear_ss(0)
        dve.wait_ge(vec_in, 16)
        dve.wait_ge(csil_done, 1)
        for b in range(4):
            ada_chunks(b, range(8))
            for m in (2 * b, 2 * b + 1):
                add_squares(0, m, m % 2)
            job = Job(JOB["ada"] + b)
            job.ready(dve)
            job.last_read(ada_out(0, b, job))
        for c in range(4):
            split_lo(c)
        head_lo(0)
        for L in range(DEPTH):
            c0, w, sg = NCH * L, width(L), segs(L)
            norm(2 * L, Job(JOB["norm1", L]))
            for j in range(4):
                split_lo(c0 + 4 + j)
            dve.wait_ge(tab_in, 48 * (L + 1))
            for n in range(4):
                gb = rgain[:, n:n + 1].to_broadcast([P, TOK, ROPE])
                dve.scalar_tensor_tensor(rtab[:, n], rtab[:, n], SCALE if n < 2 else 1.0, gb, ALU.mult,
                                         ALU.mult).then_inc(tab_ok[L], 1)
            dve.tensor_scalar(qg[:, 0:1], V(L, V_QN), SCALE, None, ALU.mult).then_inc(tab_ok[L], 1)
            for j in range(3):
                job = Job(JOB["lat", L] + j)
                job.ready(dve)
                a = 0 if 2 * j < qtok(L) else QR
                src = job.ps().rearrange("p (t c) -> p t c", t=2)[:, :, a:LATW]
                job.last_read(dve.tensor_copy(latr[:, 2 * j:2 * j + 2, a:LATW], src))
            if L == 0:
                ada_chunks(4, range(8))
            dve.wait_ge(lat_sq[L], LAT_SQ[L])
            for g, n in enumerate((QR, KVR, ROPE)):
                dve.tensor_scalar(lat_ss[:, g], lat_ss[:, g], 1.0 / n, EPS, ALU.mult, ALU.add).then_inc(lat_ms[L], 1)
            dve.wait_ge(lat_ms[L], 3)
            dve.reciprocal(lat_ss[:], lat_ss[:]).then_inc(lat_ms[L], 1)
            dve.wait_ge(lat_rt[L], 1)
            for g, (a, b) in enumerate(((0, QR), (QR, QR + KVR), (QR + KVR, LATW))):
                nt = TOK if g > 0 else qtok(L)
                r = lat_ss[:, g, 0:nt].unsqueeze(2).to_broadcast([P, nt, b - a])
                dve.tensor_tensor(latr[:, 0:nt, a:b], latr[:, 0:nt, a:b], r, ALU.mult).then_inc(lat_nm[L], 1)
            ncv = 1 + 2 * len(sg)
            for j in range(8):
                job, m, role = Job(JOB["a2", L] + j), j // 4, ROLES[j % 4]
                y = ymix[2 + m]
                if L == 0 and j in (2, 4, 6):
                    ada_chunks(4 + j // 2, range(8))
                if role != "pool":
                    job.ready(dve)
                if L == 0 and j % 2 == 1:
                    ada_out(0, 4 + j // 2, job).then_inc(mod_done, 1)
                if role == "gate_c":
                    job.last_read(dve.tensor_copy(tmp[0][:, 0:w], job.ps(0, w)))
                elif role == "conv_in":
                    Job(JOB["a2", L] + j - 1).taken(dve)
                    job.last_read(dve.tensor_tensor(tmp[1][:, 0:w], tmp[0][:, 0:w], job.ps(0, w), ALU.mult))
                    job.taken(dve)
                    dve.tensor_scalar(y[:, 0:w], tmp[1][:, 0:w], V(L, V_SC + 3 * m + 1), None,
                                      ALU.mult).then_inc(cv[L], 1)
                    n = ncv * m + 1
                    for tap, d0, s0 in ((0, 1, 0), (2, 0, 1)):
                        for _, a, b in sg:
                            dve.wait_ge(cv[L], n)
                            yo = y[:, a + d0:b - 1 + d0]
                            dve.scalar_tensor_tensor(yo, tmp[1][:, a + s0:b - 1 + s0], V(L, V_SC + 3 * m + tap), yo,
                                                     ALU.mult, ALU.add).then_inc(cv[L], 1)
                            n += 1
                elif role == "gate_b":
                    dve.wait_ge(cv[L], ncv * (m + 1))
                    job.last_read(dve.tensor_tensor(y[:, 0:w], y[:, 0:w], job.ps(0, w), ALU.mult))
                    dve.wait_ge(win_ok[L], m + 1)
                    for s, a, b in sg:
                        o = PAD + a + 2 * PAD * s
                        last = dve.scalar_tensor_tensor(ymix[m][:, a:b], win_r[:, o:o + b - a],
                                                        vec[:, V_INVW + m:V_INVW + m + 1], win_p[:, o:o + b - a],
                                                        ALU.mult, ALU.subtract)
                    last.then_inc(pdiff[L], 1)
                split_lo(c0 + 8 + j)
            for n in range(4):
                job = Job(JOB["latT", L] + n)
                dve.wait_ge(lat_hi[L], n + 1)
                if n < 2:
                    ins = lo_half(ql[1][:, n, 0:w], job.ps(0, w), ql[0][:, n, 0:w], V(L, V_QC + n))
                elif n == 2:
                    ins = lo_half(kvl[1][:], job.ps(0, NT), kvl[0][:], V(L, V_KVC))
                else:
                    ins = lo_half(kr[1][0:ROPE], job.ps(0, NT)[0:ROPE], kr[0][0:ROPE])
                job.last_read(ins)

            def b_norm(j0, i, per, h):
                dve.wait_ge(b_sq[L], B_SQ[L] * (h + 1))
                for g, n in enumerate((NOPE, ROPE, NOPE)):
                    dve.tensor_scalar(head_ss[:, g], head_ss[:, g], 1.0 / n, EPS, ALU.mult,
                                      ALU.add).then_inc(b_ms[L], 1)
                dve.wait_ge(b_ms[L], 4 * h + 3)
                dve.reciprocal(head_ss[:], head_ss[:]).then_inc(b_ms[L], 1)
                dve.wait_ge(b_rt[L], h + 1)
                for j in range(3):
                    job = Job(j0 + j, i, per)
                    src = job.ps().rearrange("p (t c) -> p t c", t=2)
                    for g, (a, b) in enumerate(((0, NOPE), (NOPE, HQ), (HQ, QKW))):
                        if g == 2 or 2 * j < qtok(L):
                            r = head_ss[:, g, 2 * j:2 * j + 2].unsqueeze(2).to_broadcast([P, 2, b - a])
                            last = dve.tensor_tensor(qkt[:, 2 * j:2 * j + 2, a:b], src[:, :, a:b], r, ALU.mult)
                    job.last_read(last)

            def b_halves(j0, i, per, h):
                for n, (dst, rows, wn) in enumerate(((q, P, w), (k, P, NT), (qr, ROPE, w))):
                    job = Job(j0 + n, i, per)
                    dve.wait_ge(b_hi[L], 4 * h + (n + 1))
                    scale = (qg[:, 0:1], V(L, V_KN), None)[n]
                    job.last_read(lo_half(dst[1][0:rows, 0:wn], job.ps(0, wn)[0:rows], dst[0][0:rows, 0:wn], scale))

            def v_half(j, i, per, h):
                dve.wait_ge(b_hi[L], 4 * h + 4)
                job = Job(j, i, per)
                job.last_read(lo_half(v[1][:], job.ps(0, NT), v[0][:]))

            def softmax(j0, i, per, h):
                for t in range(XTOK):
                    job = Job(j0 + t, i, per)
                    job.ready(dve)
                    last = dve.tensor_reduce(nmax[:, t:t + 1], job.ps(0, NT), AX.X, ALU.max, negate=True)
                    if L == 0 and t < 2:
                        last = dve.tensor_reduce(nmax[:, 4 + t:5 + t], job.ps(NT, 1024), AX.X, ALU.max, negate=True)
                    last.then_inc(s_max[L], 1)
                for t in range(XTOK):
                    Job(j0 + t, i, per).taken(dve)
                    if L == 0 and t < 2:
                        dve.reciprocal(rsum[:, 4 + t:5 + t], rsum[:, 4 + t:5 + t])
                    dve.reciprocal(rsum[:, t:t + 1], rsum[:, t:t + 1]).then_inc(s_rec[L], 1)
                    dve.wait_ge(s_rec[L], 4 * h + (t + 1))
                    if L == 0 and t < 2:
                        dve.tensor_scalar(probc[:, t], probc[:, t], rsum[:, 4 + t:5 + t], None, ALU.mult)
                    dve.tensor_scalar(prob[:, t], prob[:, t], rsum[:, t:t + 1], None, ALU.mult).then_inc(s_p[L], 1)

            def attend(js, i, per, h):
                for n in range(4):
                    job = Job(js[n], i, per)
                    for m, e in enumerate(TJOBS[L][n]):
                        dve.wait_ge(pt_hi[L], ENTRIES[L] * h + (e + 1))
                        ins = lo_half(pt[1][e % 4][:], job.ps(512 * m, 512 * (m + 1)), pt[0][e % 4][:])
                    job.last_read(ins)

            def attended(jpv, i, per, h):
                job = Job(jpv, i, per)
                dve.wait_ge(ca_hi[L], h + 1)
                job.last_read(lo_half(cat_a[1][:, h, 0:w], job.ps(0, w), cat_a[0][:, h, 0:w]))

            b0 = JOB["b0", L]
            b_norm(b0, 0, 0, 0)
            b_halves(b0 + 3, 0, 0, 0)
            v_half(b0 + 6, 0, 0, 0)
            j0 = JOB["heads", L]
            with dve.Fori(0, HEADS - 1) as h:
                head_lo(h + (HEADS * L + 1))
                softmax(j0 + J_S, h, J_HEAD, h)
                b_norm(j0 + J_B, h, J_HEAD, h + 1)
                b_halves(j0 + J_BT, h, J_HEAD, h + 1)
                attend([j0 + x for x in J_T], h, J_HEAD, h)
                attended(j0 + J_PV, h, J_HEAD, h)
                v_half(j0 + J_V, h, J_HEAD, h + 1)
            if L == 0:
                head_lo(HEADS)
            j0 = JOB["last", L]
            softmax(j0, 0, 0, HEADS - 1)
            attend([j0 + 4, j0 + 5, j0 + 7, j0 + 8], 0, 0, HEADS - 1)
            for j in range(4):
                dve.wait_ge(cy_hi[L], j + 1)
                lo_half(cat_y[1][:, j, 0:w], ymix[j][:, 0:w], cat_y[0][:, j, 0:w]).then_inc(cy_lo[L], 1)
            attended(j0 + 6, 0, 0, HEADS - 1)
            nn = 2 * L + 1
            clear_ss(nn)
            with dve.Fori(0, 2) as i:
                for j in range(4):
                    job = Job(JOB["wo", L] + j, i, 4)
                    if L == 0:
                        ada_chunks(8 + j // 2, range(4 * (j % 2), 4 * (j % 2) + 4), i, 2)
                    job.ready(dve)
                    if L == 0 and j % 2 == 1:
                        ada_out(0, 2 * i + (8 + j // 2), job).then_inc(mod_done, 1)
                    update_x(4 * i + j, L, job, 16)
                    split_lo(c0 + 16 + j, i, 4)
                    add_squares(nn, 4 * i + j, j % 2)
            norm(nn, Job(JOB["norm2", L]))
            if L == 0:
                ada_chunks(12, range(8))

            def ff_tile(t, jn, c, par, buf, i, per_j, per_c):
                g, u = Job(jn, i, per_j), Job(jn + 1, i, per_j)
                dve.wait_ge(ff_mid[L], t + 1)
                n, per_tile = 0, 2 * len(sg) - 1
                for tap, d0, s0 in ((0, 1, 0), (2, 0, 1)):
                    for _, a, b in sg:
                        if n:
                            dve.wait_ge(ff_conv[L], per_tile * t + n)
                        y = tmp[par][:, a + d0:b - 1 + d0]
                        ins = dve.scalar_tensor_tensor(y, g.ps(a + s0, b - 1 + s0),
                                                       vec[:, bass.ds(L * V_LAYER + V_FC + FT * tap + t, 1)], y,
                                                       ALU.mult, ALU.add)
                        n += 1
                        if n <= per_tile:
                            ins.then_inc(ff_conv[L], 1)
                        else:
                            g.last_read(ins)
                split_lo(c, i, per_c)
                u.ready(dve)
                dve.wait_ge(ff_silu[L], t + 1)
                return u

            def ff_value(t, u, c, par, buf, i, per_c):
                u.last_read(dve.tensor_tensor(ff_v[:, 0:w], tmp[par][:, 0:w], u.ps(0, w), ALU.mult))
                split_lo(c + 1, i, per_c)
                dve.wait_ge(ff_hi[L], t + 1)
                lo_half(inner[1][buf][:, par, 0:w], ff_v[:, 0:w],
                        inner[0][buf][:, par, 0:w]).then_inc(ff_lo[L], 1)

            for t in range(2):
                u = ff_tile(t, JOB["u0", L] + 2 * t, c0 + C_FF + 4 + 2 * t, t, 0, 0, 0, 0)
                if L == 0 and t == 1:
                    ada_out(1, 0, u).then_inc(mod_done, 1)
                ff_value(t, u, c0 + C_FF + 4 + 2 * t, t, 0, 0, 0)
            jf = JOB["ff", L]
            with dve.Fori(0, (FP - 1) // 2) as i:
                for d in range(2):
                    c = c0 + C_FF + 4 + 6 * d
                    for t in range(2):
                        tile, cc = 4 * i + (2 * (d + 1) + t), c + 4 + 2 * t
                        u = ff_tile(tile, jf + 12 * d + 2 * t, cc, t, 1 - d, i, 24, 12)
                        ff_value(tile, u, cc, t, 1 - d, i, 12)
                        if L == 0:
                            ada_chunks(13 + d, (2 * t, 2 * t + 1), i, 2)
                    for m in range(KD):
                        job = Job(jf + 12 * d + 4 + m, i, 24)
                        if L == 0 and m < 4:
                            ada_chunks(13 + d, (4 + m,), i, 2)
                        job.ready(dve)
                        if L == 0 and m == KD - 1:
                            ada_out(1, 2 * i + (1 + d), job).then_inc(mod_done, 1)
                        update_x(m, L, job, 40)
                    for x in range(2):
                        split_lo(c + 8 + x, i, 12)
            if L == 0:
                ada_chunks(23, range(8))
                clear_ss(2)
            for m in range(KD):
                job = Job(JOB["dlast", L] + m)
                job.ready(dve)
                if L == 0 and m == KD - 1:
                    ada_out(1, 11, job).then_inc(mod_done, 1)
                update_x(m, L, job, 40)
                if L == 0 and m:
                    add_squares(2, m - 1, (m - 1) % 2)
            if L == 0:
                add_squares(2, KD - 1, (KD - 1) % 2)
                for x in range(2):
                    split_lo(c0 + NCH + 2 + x)

    ctx.close()


def pack_vectors(a):
    cols = np.zeros((P, NV), np.float32)

    def put(c, x):
        x = np.asarray(x, np.float32).reshape(-1, P).T
        cols[:, c:c + x.shape[1]] = x
    for L in range(DEPTH):
        o = L * V_LAYER
        for c, name in ((V_N1, "norm1_g"), (V_N2, "norm2_g"), (V_ADAB, "ada_b"), (V_QC, "qc_g"), (V_KVC, "kvc_g"),
                        (V_QN, "qn_g"), (V_KN, "kn_g"), (V_PS, "pool_scale")):
            put(o + c, a[name][L])
        for m in range(2):
            for tap in range(3):
                put(o + V_SC + 3 * m + tap, a["sconv_w"][L][tap, P * m:P * (m + 1)])
        for tap in range(3):
            put(o + V_FC + FT * tap, a["ff_conv"][L][tap])
    put(V_C, a["c"][0])
    put(V_C + 8, a["c_ctx"])
    for m, pair in enumerate(((2, 4), (8, 16))):
        for half, win in enumerate(pair):
            rows = slice(64 * half, 64 * half + 64)
            cols[rows, V_INVW + m] = 1.0 / win
            for t in range(PAD):
                left = min(t + win // 2, NC) - max(t - win // 2, 0)
                right = min(NC - PAD + t + win // 2, NC) - (NC - PAD + t - win // 2)
                cols[rows, V_RATIO + 16 * m + t] = win / left
                cols[rows, V_RATIO + 16 * m + 8 + t] = win / right
    cols[:, V_EPS] = EPS
    return cols


def rope_tables():
    t = np.arange(NX)
    nf = ROPE // 4
    inv = (10000.0 ** (-np.arange(nf, dtype=np.float32) / nf)).astype(np.float32)
    ar = (t // GRID_W).astype(np.float32)[:, None] * inv
    ac = (t % GRID_W).astype(np.float32)[:, None] * inv
    ang = np.concatenate([ar, ar, ac, ac], axis=-1)
    sign = np.tile(np.repeat(np.array([-1.0, 1.0], np.float32), nf), 2)
    tab = np.zeros((2, NT, ROPE), np.float32)
    tab[0] = 1.0
    tab[0, :NX] = np.cos(ang)
    tab[1, :NX] = np.sin(ang) * sign
    return np.ascontiguousarray(tab.reshape(2, TOK, P, ROPE).transpose(2, 0, 1, 3))


def tiles(w):
    n = w.shape[1] // P
    return w.reshape(KD, P, n, P).transpose(2, 1, 0, 3).reshape(n, P, CH)


def layout(a):
    a = {n: np.asarray(x) for n, x in a.items()}
    main = np.zeros((DEPTH * NCH + SPARE, P, CH), np.float32)
    heads = np.zeros((DEPTH * HEADS, P, 2 * HQ + 2 * NOPE), np.float32)
    rgain = np.zeros((DEPTH, 4, ROPE), np.float32)
    partner = np.arange(ROPE).reshape(2, 2, ROPE // 4)[:, ::-1].reshape(-1)
    for L in range(DEPTH):
        w_in, m = a["w_in"][L], main[NCH * L:NCH * (L + 1)]
        lat = w_in[:, :LATW].reshape(4, 2, P, LATW).transpose(0, 2, 1, 3).reshape(4, P, 2 * LATW)
        m[C_LAT:C_LAT + 4, :, :2 * LATW] = lat
        rest = tiles(np.ascontiguousarray(w_in[:, LATW:]))
        m[C_A2:C_A2 + 8] = rest[[0, 4, 6, 2, 1, 5, 7, 3]]
        m[C_WO:C_WO + 8] = tiles(a["w_o"][L])
        up = tiles(a["ff_up"][L])
        down = a["ff_down"][L].reshape(FT, P, D)
        c = C_FF
        for p in range(FP + 1):
            if p < FP:
                m[c:c + 4] = up[[2 * p, FT + 2 * p, 2 * p + 1, FT + 2 * p + 1]]
                c += 4
            if p:
                m[c:c + 2] = down[2 * p - 2:2 * p]
                c += 2
        wq = a["w_q_up"][L].reshape(2, P, HEADS, HQ)
        wkv = a["w_kv_up"][L].reshape(P, HEADS, NOPE + P)
        for h in range(HEADS):
            w = heads[HEADS * L + h]
            w[:, :2 * HQ] = wq[:, :, h].transpose(1, 0, 2).reshape(P, 2 * HQ)
            w[:, 2 * HQ:] = wkv[:, h]
        rgain[L] = [a["qr_g"][L], a["qr_g"][L][partner], a["kr_g"][L], a["kr_g"][L][partner]]
    ada = a["ada_w"].reshape(DEPTH, KD, P, ADB, ADC).transpose(0, 3, 1, 2, 4).reshape(DEPTH * ADB * KD, P, ADC)
    return {
        "x": a["x"][0].T.reshape(KD, P, NX).transpose(1, 0, 2), "ctx": a["ctx"][0].T.reshape(KD, P, NC).transpose(1, 0, 2),
        "vec": pack_vectors(a), "rope": rope_tables(), "rgain": rgain, "pool_w": a["pool_w"],
        "w_main": main, "w_head": heads, "w_ada": ada,
    }


def kernel(**inputs):
    import concourse.bacc as bacc
    from concourse.bass_utils import run_bass_kernel_spmd

    nc = bacc.Bacc("TRN2", target_bir_lowering=False, num_devices=1)
    arrays, dram = {}, {}
    for name, x in layout(inputs).items():
        arrays[f"in_{name}"] = np.ascontiguousarray(x)
        dram[name] = nc.dram_tensor(f"in_{name}", x.shape, F32, kind="ExternalInput").ap()
    dram["out"] = nc.dram_tensor("out_x", (KD, P, NX), F32, kind="ExternalOutput").ap()
    build(nc, dram)
    r = run_bass_kernel_spmd(nc, [arrays], core_ids=[0])
    return np.ascontiguousarray(r.results[0]["out_x"].reshape(D, NX).T)[None]
```

```python
import numpy as np
import concourse.bass as bass
from concourse import mybir
from contextlib import ExitStack

F32 = mybir.dt.float32
F32R = mybir.dt.float32r
ALU = mybir.AluOpType
ACT = mybir.ActivationFunctionType
AX = mybir.AxisListType

P = 128
D = 1024
KD = D // P
DEPTH = 2
NX, NC = 512, 256
NT = NX + NC
TOK = NT // P
XTOK = NX // P
GRID_W = 64
HEADS = 4
NOPE, ROPE = 128, 64
SCALE = (NOPE + ROPE) ** -0.5
QR, KVR = 256, 128
LATW = QR + KVR + ROPE
HQ = NOPE + ROPE
QKW = HQ + NOPE
DFF = 2816
FT = DFF // P
FP = FT // 2
EPS = 1e-6
CH = 1024
ADC = 512
ADB = 6 * D // ADC
PAD = 8

C_LAT, C_A2, C_WO, C_FF = 0, 4, 12, 20
NCH = C_FF + 6 * FP
SPARE = 4
ADA0 = 4
ADA_SPARE = 4
V_N1, V_N2, V_ADAB, V_QC, V_KVC, V_QN, V_KN, V_PS, V_SC, V_FC = 0, 8, 16, 64, 66, 67, 68, 69, 71, 77
V_LAYER = V_FC + 3 * FT
V_C = DEPTH * V_LAYER
V_INVW = V_C + 16
V_RATIO = V_INVW + 2
V_EPS = V_RATIO + 32
NV = V_EPS + 1


ADA_FIRST, ADA_ROWS, ADA_TURN, ADA_NORM = (2, 3, 0, 1), (0, 1, 3, 7), (2, 4, 8, 9), 5


def job_plan():
    plan, n = {"ada": 0}, 2 * ADA0 + 2
    for L in range(DEPTH):
        for name, count in [("norm1", 2 * L), ("lat", 3), ("a2", 8), ("latT", 3), ("pool", 2), ("b0", 3), ("krT", 1), ("v0", 1),
                            ("b0T", 3),
                            ("heads", 16 * (HEADS - 1)), ("last", 9), ("wo", 8), ("norm2", 2 - L), ("u0", 4),
                            ("ff", 24 * ((FP - 1) // 2)), ("dlast", 8)]:
            plan[name, L] = n
            n += count
    plan["norm1", 0] = ADA_NORM
    return plan


JOB = job_plan()


def build(nc, dram):
    ctx = ExitStack()
    base = (nc.sbuf_base + 31) // 32 * 32

    def at(name, off, shape, dt=F32):
        return nc.alloc_sbuf_tensor_at(name, shape, dt, offset=base + off)

    class Place:
        def __init__(self, off):
            self.off = off

        def __call__(self, name, shape, dt=F32, extra=0):
            t = at(name, self.off, shape, dt)
            self.off += (4 * int(np.prod(shape[1:])) + extra + 31) // 32 * 32
            return t

    sb = Place(0)
    X = sb("X", [P, KD, NT])
    vec = sb("vec", [P, NV + (-NV) % 8])
    mod = [sb(f"mod{L}", [P, 2, 48]) for L in range(DEPTH)]
    csil = sb("csil", [P, 16])
    amul = sb("amul", [P, 2, 8])
    qg = sb("qg", [P, 8])
    lat_ss = sb("lat_ss", [P, 3, TOK])
    head_ss = sb("head_ss", [P, 3, TOK])
    head_sq = sb("head_sq", [P, TOK, 5])
    warm = sb("warm", [P, 8])
    nmax = sb("nmax", [P, 8])
    rsum = sb("rsum", [P, 8])
    ident = sb("ident", [P, P])
    ones = sb("ones", [P, P])
    poolw = sb("poolw", [P, 2, P])
    rgain = sb("rgain", [P, 4, ROPE])
    rtab = sb("rtab", [P, 4, TOK, ROPE])
    w_raw = [sb(f"w_raw{s}", [P, CH]) for s in range(2)]
    w_hi = [sb(f"w_hi{s}", [P, CH], F32R) for s in range(4)]
    w_lo = [sb(f"w_lo{s}", [P, CH], F32R) for s in range(4)]
    HWC = 2 * HQ + 2 * NOPE
    hw_raw = sb("hw_raw", [P, HWC])
    hw_hi = sb("hw_hi", [P, HWC], F32R)
    hw_lo = sb("hw_lo", [P, HWC], F32R)
    mid = Place(sb.off)
    ql = [mid(f"ql_{x}", [P, 2, NT], F32R) for x in ("hi", "lo")]
    kvl = [mid(f"kvl_{x}", [P, NT], F32R) for x in ("hi", "lo")]
    kr = [mid(f"kr_{x}", [P, NT], F32R) for x in ("hi", "lo")]
    ymix = [None] * 4
    for j in (0, 2, 3):
        ymix[j] = mid(f"ymix{j}", [P, NT])
    win_a = at("win_a", mid.off, [P, NT + 4 * PAD])
    ymix[1] = mid("ymix1", [P, NT], F32, extra=4 * 4 * PAD)
    cat_y = [at(f"cat_y_{x}", sb.off + 4 * 4 * NT * n, [P, 4, NT], F32R) for n, x in enumerate(("hi", "lo"))]
    ph = Place(mid.off)
    ada_raw = [ph(f"ada_raw{s}", [P, ADC]) for s in range(4)]
    ada_acc = ph("ada_acc", [P, 2, ADC])
    ada_end = ph.off
    tmp = [ph(f"tmp{s}", [P, NT]) for s in range(2)]
    ss = ph("ss", [P, NT])
    lo_free = ph.off
    H = [ph(f"H_{x}", [P, KD, NT], F32R) for x in ("hi", "lo")]
    ada_acc2 = at("ada_acc2", ph.off, [P, 1, ADC])
    latr = ph("latr", [P, TOK, LATW])
    ada_first = [at(f"ada_first{b}", (sb.off, lo_free)[b // 2] + 4 * KD * ADC * (b % 2), [P, KD, ADC])
                 for b in range(ADA0)]
    assert 2 * 4 * KD * ADC <= min(mid.off - sb.off, 2 * 4 * KD * NT)
    win_p = ph("win_p", [P, NT + 4 * PAD])
    win_r = ph("win_r", [P, NT + 4 * PAD])
    hd = Place(mid.off)
    q = [hd(f"q_{x}", [P, NT], F32R) for x in ("hi", "lo")]
    qr = [hd(f"qr_{x}", [P, NT], F32R) for x in ("hi", "lo")]
    k = [hd(f"k_{x}", [P, NT], F32R) for x in ("hi", "lo")]
    v = [hd(f"v_{x}", [P, NT], F32R) for x in ("hi", "lo")]
    pt = [[hd(f"pt_{x}{s}", [P, NX], F32R) for s in range(4)] for x in ("hi", "lo")]
    prob = hd("prob", [P, XTOK, NT])
    probc = hd("probc", [P, 2, NC])
    qkt = hd("qkt", [P, TOK, QKW])
    rt = [hd(f"rt{s}", [P, TOK, ROPE]) for s in range(2)]
    assert hd.off >= lo_free
    cat_a = [hd(f"cat_a_{x}", [P, 4, NT], F32R) for x in ("hi", "lo")]
    ff = Place(sb.off)
    inner = [[ff(f"inner_{x}{b}", [P, 2, NT], F32R) for b in range(2)] for x in ("hi", "lo")]
    ff_v = ff("ff_v", [P, NT])
    assert ff.off <= mid.off

    ps_t = ctx.enter_context(nc.psum_tensor("ps", [P, 8, 512], F32))
    ps_all = ps_t[:].rearrange("p b n -> p (b n)")

    def sem(name):
        return ctx.enter_context(nc.semaphore(name))

    def sems(name, n=DEPTH):
        return [sem(f"{name}{i}") for i in range(n)]

    full, free = sems("psum_full", 4), sems("psum_free", 4)
    chunk_in = sems("chunk_in", 2)
    chunk_hi, chunk_lo, lat_used = sem("chunk_hi"), sem("chunk_lo"), sem("lat_used")
    hw_in, hw_hid, hw_lod = sem("hw_in"), sem("hw_hi_done"), sem("hw_lo_done")
    ada_in = sems("ada_in", 4)
    ada_first_in = sems("ada_first_in", 2 * ADA0)
    ada_op, mod_done = sem("ada_op"), sem("mod_done")
    vec_in, x_in, tab_in, csil_done = sem("vec_in"), sem("x_in"), sem("tab_in"), sem("csil_done")
    consts, poolw_zero, poolw_in, out_in = sem("consts"), sem("poolw_zero"), sem("poolw_in"), sem("out_in")
    sq_done, ss_done, scale_ok, rms_ok, t_done, h_hi, h_lo = (
        sems(n, 4) for n in ("sq_done", "ss_done", "scale_ok", "rms_ok", "t_done", "h_hi", "h_lo"))
    (lat_sq, lat_ms, lat_rt, lat_nm, lat_hi, kr_rot, tab_ok, win_st, win_ok, pdiff, cv, b_sq, b_ms, b_rt, b_rc, b_rot, b_hi, v_hi,
     s_max, s_rec, s_p, pt_hi, pv_used, ca_hi, cy_hi, cy_lo, ff_mid, ff_conv, ff_silu, ff_hi, ff_lo) = (
        sems(n) for n in ("lat_sq", "lat_ms", "lat_rt", "lat_nm", "lat_hi", "kr_rot", "tab_ok", "win_st", "win_ok",
                          "pdiff", "cv", "b_sq", "b_ms", "b_rt", "b_rc", "b_rot", "b_hi", "v_hi", "s_max", "s_rec", "s_p", "pt_hi",
                          "pv_used", "ca_hi", "cy_hi", "cy_lo", "ff_mid", "ff_conv", "ff_silu", "ff_hi", "ff_lo"))

    block = ctx.enter_context(nc.Block())

    ALL = [(0, 0, NX), (1, NX, NT)]

    def segs(L):
        return ALL if L == 0 else ALL[:1]

    def nsegs(nn):
        return ALL if nn < 3 else ALL[:1]

    def width(L):
        return NT if L == 0 else NX

    def qtok(L):
        return TOK if L == 0 else XTOK

    class Job:
        def __init__(self, n, i=0, per=0):
            self.slot, self.count, self.i, self.step = n % 4, n // 4, i, per // 4
            assert per % 4 == 0

        def times(self, extra):
            n = self.count + extra
            return n + self.i * self.step if self.step else n

        def ps(self, a=0, b=1024):
            return ps_all[:, self.slot * 1024 + a:self.slot * 1024 + b]

        def open(self, pe):
            if self.count:
                pe.wait_ge(free[self.slot], self.times(0))

        def filled(self, ins):
            ins.then_inc(full[self.slot], 1)

        def ready(self, eng):
            eng.wait_ge(full[self.slot], self.times(1))

        def last_read(self, ins):
            ins.then_inc(free[self.slot], 1)

        def taken(self, eng):
            eng.wait_ge(free[self.slot], self.times(1))

    def V(L, off, n=1):
        return vec[:, L * V_LAYER + off:L * V_LAYER + off + n]

    TJOBS = [[(0, 1), (2, 3), (4, 5), (6,)], [(0, 1), (2, 3), (4,), (5,)]]
    ENTRIES = [7, 6]
    LAT_SQ = [3 * qtok(L) + 2 * (TOK - qtok(L)) for L in range(DEPTH)]
    J_S, J_B, J_BT, J_T, J_PV, J_V, J_HEAD = (0, 4, 5, 6), 1, 7, (10, 11, 12, 14), 13, 15, 16
    J_LS = (0, 1, 2, 3)
    ROLES = ("pool", "gate_c", "conv_in", "gate_b")

    def spare_landed(eng):
        for n in range(4):
            eng.wait_ge(ada_in[n], 4 * ((DEPTH * ADB - ADA0) * KD + ADA_SPARE))

    def pieces(nn):
        if nn == 3:
            return [(kk, ALL[0]) for kk in range(KD)]
        return ([(0, ALL[0]), (1, ALL[0]), (0, ALL[1]), (1, ALL[1])]
                + [(kk, sg) for kk in range(2, KD) for sg in ALL])

    NORM_BREAK = 3

    ADA_WO = (range(6), range(6, 8))
    ADA_UP = (((0, 1, 2), (3,)), ((4, 5), (6, 7)))

    @block.sync
    def _(sp):
        def load(c, i=0, per=0):
            if c >= 2:
                sp.wait_ge(chunk_lo, c - 1 + per * i if per else c - 1)
            src = dram["w_main"][c + per * i] if per else dram["w_main"][c]
            sp.dma_start(w_raw[c % 2][:], src).then_inc(chunk_in[c % 2], 16)

        def load_head(n):
            if n >= 1:
                sp.wait_ge(hw_lod, n)
            sp.dma_start(hw_raw[:], dram["w_head"][n]).then_inc(hw_in, 16)

        def load_ada(c, i=0, per=0):
            c -= ADA0 * KD
            if c >= 4:
                sp.wait_ge(ada_op, 2 * c - 6 + 2 * per * i if per else 2 * c - 6)
            n = c + ADA0 * KD
            src = dram["w_ada"][n + per * i] if per else dram["w_ada"][n]
            sp.dma_start(ada_raw[c % 4][:], src).then_inc(ada_in[c % 4], 16)

        def load_tables(L):
            for n in (0, 2):
                sp.dma_start(rtab[:, n:n + 2], dram["rope"]).then_inc(tab_in, 16)
            sp.dma_start(rgain[:], dram["rgain"][L].partition_broadcast(P)).then_inc(tab_in, 16)
            for g in range(4):
                p0 = 64 * (g % 2)
                sp.dma_start(poolw[p0:p0 + 64, g // 2, p0:p0 + 64], dram["pool_w"][L, g]).then_inc(poolw_in, 16)

        sp.dma_start(vec[:, 0:NV], dram["vec"]).then_inc(vec_in, 16)
        def load_first(n):
            b = ADA_FIRST[n]
            for kk in (0, KD // 2):
                src = dram["w_ada"][KD * b + kk:KD * b + kk + KD // 2].rearrange("k p n -> p k n")
                sp.dma_start(ada_first[b][:, kk:kk + KD // 2], src).then_inc(ada_first_in[2 * b + 2 * kk // KD], 16)
        load_first(0)
        sp.dma_start(X[:, :, 0:NX], dram["x"]).then_inc(x_in, 16)
        sp.dma_start(X[:, :, NX:NT], dram["ctx"]).then_inc(x_in, 16)
        load_first(1)
        load(0)
        load(1)
        load_first(2)
        load_first(3)
        load(2)
        load(3)
        load_head(0)
        for m in range(4):
            load_ada(ADA0 * KD + m)
        sp.wait_ge(poolw_zero, 1)
        load_tables(0)
        for L in range(DEPTH):
            c0 = NCH * L
            if L == 0:
                load(4)
                load(5)
            load_head(HEADS * L + 1)
            for j in range(4):
                load(c0 + 6 + j)
            if L == 0:
                for m in range(8):
                    load_ada(8 * 4 + m + 4)
            for j in range(8):
                if L == 0 and j in (2, 4, 6):
                    for m in range(8):
                        if 8 * (4 + j // 2) + m + 4 < 64:
                            load_ada(8 * (4 + j // 2) + m + 4)
                load(c0 + 10 + j)
            load_head(HEADS * L + 2)
            load_head(HEADS * L + 3)
            if L == 0:
                load_head(HEADS)
                Job(JOB["last", 0] + 3).ready(sp)
                for c in range(64, 68):
                    load_ada(c)
            with sp.Fori(0, 2) as i:
                for j in range(4):
                    if L == 0:
                        for m in ADA_WO[j % 2]:
                            load_ada(8 * (8 + j // 2) + m + 4, i, 16)
                    load(c0 + 18 + j, i, 4)
            if L == 0:
                for m in range(8):
                    load_ada(8 * 12 + m + 4)
            for j in range(4):
                if L == 0 and j == 0:
                    for m in range(8):
                        load_ada(8 * 13 + m + 4)
                load(c0 + 26 + j)
            if L == 0:
                b_rot_done = 3 * HEADS
                sp.wait_ge(b_rot[0], b_rot_done)
                load_tables(1)
            with sp.Fori(0, (FP - 1) // 2) as i:
                for d in range(2):
                    c = c0 + 30 + 6 * d
                    for t in range(2):
                        for x in range(2):
                            if L == 0:
                                for m in ADA_UP[t][x]:
                                    load_ada(8 * (14 + d) + m + 4, i, 16)
                            load(c + 2 * t + x, i, 12)
                    for x in range(2):
                        load(c + 4 + x, i, 12)
            if L == 0:
                for j in range(2):
                    load(c0 + NCH + 4 + j)
        for m in range(KD):
            Job(JOB["dlast", 1] + m).taken(sp)
            sp.dma_start(dram["out"][m], X[:, m, 0:NX]).then_inc(out_in, 16)
        sp.wait_ge(out_in, 16 * KD)
        for s in range(2):
            sp.wait_ge(chunk_in[s], 8 * (DEPTH * NCH + SPARE))

    @block.gpsimd
    def _(pool):
        pool.memset(poolw[:], 0.0).then_inc(poolw_zero, 1)
        pool.memset(ones[:], 1.0).then_inc(consts, 1)
        pool.memset(ident[:], 0.0).then_inc(consts, 1)
        pool.memset(lat_ss[:], 1.0).then_inc(consts, 1)
        pool.memset(head_sq[:], 1.0).then_inc(consts, 1)
        pool.wait_ge(consts, 4)
        pool.affine_select(out=ident[:], in_=ident[:], compare_op=ALU.not_equal, fill=1.0, base=0,
                           pattern=[[-1, P]], channel_multiplier=1).then_inc(consts, 1)

        def rotate(src, n, tab, done, before, scratch):
            def halves(x):
                return x.rearrange("p t (a h f) -> p t a h f", a=2, h=2)
            a, b = scratch[0][:, 0:n], scratch[1][:, 0:n]
            pool.tensor_tensor(a, src, rtab[:, tab, 0:n], ALU.mult).then_inc(done, 1)
            for h in range(2):
                for ax in range(2):
                    last = pool.tensor_tensor(halves(b)[:, :, ax, h], halves(src)[:, :, ax, 1 - h],
                                              halves(rtab[:, tab + 1, 0:n])[:, :, ax, h], ALU.mult)
            last.then_inc(done, 1)
            pool.wait_ge(done, before + 2)
            pool.tensor_tensor(src, a, b, ALU.add).then_inc(done, 1)

        for L in range(DEPTH):
            W = width(L) + (4 if L == 0 else 2) * PAD
            streams = [(PAD, NX)] + ([(NX + 3 * PAD, NC)] if L == 0 else [])
            st = 0

            def step(ins):
                nonlocal st
                st += 1
                ins.then_inc(win_st[L], 1)
            pool.wait_ge(h_lo[2 * L], len(pieces(2 * L)))
            for o, n in streams:
                pool.memset(win_p[:, o - PAD:o], 0.0)
                last = pool.memset(win_p[:, o + n:o + n + PAD], 0.0)
            step(last)
            for m in range(2):
                if m == 1:
                    pool.wait_ge(pdiff[L], 1)
                Job(JOB["a2", L] + 4 * m).taken(pool)
                pool.wait_ge(win_st[L], st)
                if m == 0:
                    pool.tensor_tensor(win_r[0:64, 1:W], win_p[0:64, 0:W - 1], win_p[0:64, 1:W], ALU.add)
                    step(pool.tensor_tensor(win_a[64:P, 1:W], win_p[64:P, 0:W - 1], win_p[64:P, 1:W], ALU.add))
                    pool.wait_ge(win_st[L], st)
                    step(pool.tensor_tensor(win_r[64:P, 2:W - 1], win_a[64:P, 1:W - 2], win_a[64:P, 3:W], ALU.add))
                else:
                    step(pool.tensor_tensor(win_a[:, 1:W], win_p[:, 0:W - 1], win_p[:, 1:W], ALU.add))
                    pool.wait_ge(win_st[L], st)
                    step(pool.tensor_tensor(win_r[:, 2:W - 1], win_a[:, 1:W - 2], win_a[:, 3:W], ALU.add))
                    pool.wait_ge(win_st[L], st)
                    step(pool.tensor_tensor(win_a[:, 4:W - 3], win_r[:, 2:W - 5], win_r[:, 6:W - 1], ALU.add))
                    pool.wait_ge(win_st[L], st)
                    pool.tensor_copy(win_r[0:64, 8:W - 8], win_a[0:64, 8:W - 8])
                    step(pool.tensor_tensor(win_r[64:P, 8:W - 7], win_a[64:P, 4:W - 11], win_a[64:P, 12:W - 3],
                                            ALU.add))
                pool.wait_ge(win_st[L], st)
                for o, n in streams:
                    for e, c in ((0, o), (1, o + n - PAD)):
                        r = V_RATIO + 16 * m + 8 * e
                        last = pool.tensor_tensor(win_r[:, c:c + 8], win_r[:, c:c + 8], vec[:, r:r + 8], ALU.mult)
                last.then_inc(win_ok[L], 1)
            pool.wait_ge(pdiff[L], 2)
            pool.wait_ge(lat_nm[L], 3)
            pool.wait_ge(tab_ok[L], 5)
            scratch = [x[:, 0:TOK * ROPE].rearrange("p (t f) -> p t f", t=TOK) for x in (win_p, win_r)]
            rotate(latr[:, :, QR + KVR:LATW], TOK, 2, kr_rot[L], 0, scratch)

            def head_rope(j, i, per, h):
                Job(j, i, per).taken(pool)
                rotate(qkt[:, 0:qtok(L), NOPE:HQ], qtok(L), 0, b_rot[L], 3 * h, rt)
            head_rope(JOB["b0", L] + 2, 0, 0, 0)
            with pool.Fori(0, HEADS - 1) as h:
                head_rope(JOB["heads", L] + J_B + 2, h, J_HEAD, h + 1)

    @block.tensor
    def _(pe):
        def mm3(out, w, wsl, x, xsl, first, last):
            (wh, wl), (xh, xl) = w, x
            pe.matmul(out, wh[wsl], xh[xsl], start=first, stop=False)
            pe.matmul(out, wh[wsl], xl[xsl], start=False, stop=False)
            return pe.matmul(out, wl[wsl], xh[xsl], start=False, stop=last)

        def ada_rows(n):
            job, b = Job(JOB["ada"] + ADA_ROWS[n]), ADA_FIRST[n]
            job.open(pe)
            cs = csil[:].rearrange("p (s k) -> p k s", s=2)
            for kk in range(KD):
                if kk % (KD // 2) == 0:
                    pe.wait_ge(ada_first_in[2 * b + 2 * kk // KD], 16)
                last = pe.matmul(job.ps(0, ADC)[0:2], cs[:, kk], ada_first[b][:, kk], start=kk == 0,
                                 stop=kk == KD - 1)
            job.filled(last)

        def ada_turn(n):
            job = Job(JOB["ada"] + ADA_TURN[n])
            job.open(pe)
            Job(JOB["ada"] + ADA_ROWS[n]).taken(pe)
            for c in range(4):
                last = pe.transpose(job.ps(2 * c, 2 * c + 2), ada_acc[0:2, n % 2, P * c:P * (c + 1)],
                                    ident[0:2, 0:2])
            job.filled(last)

        def ada_reduce(job, b_op, acc=ada_acc, ns=2):
            pe.wait_ge(ada_op, b_op - 2 * KD * ADA0)
            for s in range(ns):
                for c in range(4):
                    o = 768 + 4 * s + c
                    last = pe.matmul(job.ps(o, o + 1), acc[:, s, P * c:P * (c + 1)], ones[:, 0:1],
                                     start=True, stop=True)
            return last

        def norm_sum(nn, j):
            for sg, a, b in nsegs(nn):
                job = Job(j + sg)
                job.open(pe)
                pe.wait_ge(ss_done[nn], KD + 2)
                job.filled(pe.matmul(job.ps(a, b), ones[:], ss[:, a:b], start=True, stop=True))

        def part(job, sg, w, wc, x, xk, first, last):
            wsl = slice(wc, wc + P)
            for n, (ww, xx) in enumerate(((w[0], x[0]), (w[0], x[1]), (w[1], x[0]))):
                for _, a, b in sg:
                    ins = pe.matmul(job.ps(a, b), ww[:, wsl], xx[:, xk, a:b], start=first and n == 0,
                                    stop=last and n == 2)
            return ins

        def slot(c):
            return w_hi[c % 4], w_lo[c % 4]

        pe.wait_ge(consts, 5)
        pe.wait_ge(csil_done, 1)
        ada_rows(0)
        ada_rows(1)
        ada_turn(0)
        ada_rows(2)
        ada_turn(1)
        norm_sum(0, ADA_NORM)
        ada_rows(3)
        ada_turn(2)
        ada_turn(3)
        for L in range(DEPTH):
            sg, c0 = segs(L), NCH * L
            if L == 1:
                norm_sum(2 * L, JOB["norm1", L])
            jobs = [Job(JOB["lat", L] + j) for j in range(3)]
            for j in jobs:
                j.open(pe)
            for n, (kk, (sgn, ta, tb)) in enumerate(pieces(2 * L)):
                if sgn == 0 and kk % 2 == 0:
                    pe.wait_ge(chunk_lo, c0 + kk // 2 + 1)
                pe.wait_ge(h_lo[2 * L], n + 1)
                wo = (kk % 2) * LATW
                for t in range(ta // P, tb // P):
                    a = 0 if t < qtok(L) else QR
                    o = 512 * (t % 2)
                    last = mm3(jobs[t // 2].ps(o + a, o + LATW), H, (slice(None), kk, slice(P * t, P * (t + 1))),
                               slot(c0 + kk // 2), (slice(None), slice(wo + a, wo + LATW)), kk == 0, kk == KD - 1)
                    if kk == KD - 1 and t % 2 == 1:
                        jobs[t // 2].filled(last)
                if sgn == 1 and kk % 2 == 1 and kk < KD - 1:
                    last.then_inc(lat_used, 1)
            with pe.Fori(0, 2) as i:
                for j in range(4):
                    job = Job(JOB["a2", L] + j, i, 4)
                    c = c0 + C_A2 + j
                    pe.wait_ge(chunk_lo, c + 1 + 4 * i)
                    job.open(pe)
                    for kk in range(KD):
                        last = part(job, sg, slot(c), P * kk, H, kk, kk == 0, kk == KD - 1)
                    if L == 0 and j % 2 == 1:
                        last = ada_reduce(job, 16 * (5 + j // 2) + 32 * i)
                    job.filled(last)
            def lat_turn(job, a, b, nt):
                job.open(pe)
                for t in range(nt):
                    last = pe.transpose(job.ps(P * t, P * (t + 1))[0:b - a], latr[:, t, a:b], ident[:])
                job.filled(last)
            pe.wait_ge(lat_nm[L], 3)
            for n, nt in enumerate((qtok(L), qtok(L), TOK)):
                lat_turn(Job(JOB["latT", L] + n), P * n, P * (n + 1), nt)
            pe.wait_ge(poolw_in, 64 * (L + 1))
            for m in range(2):
                job = Job(JOB["pool", L] + m)
                job.open(pe)
                pe.wait_ge(pdiff[L], m + 1)
                for _, a, b in sg:
                    last = pe.matmul(job.ps(a, b), poolw[:, m], ymix[m][:, a:b], start=True, stop=True)
                job.filled(last)

            def b_tokens(j0, i, per, h):
                pe.wait_ge(hw_lod, HEADS * L + 1 + h)
                for j in range(3):
                    job = Job(j0 + j, i, per)
                    job.open(pe)
                    for t in (2 * j, 2 * j + 1):
                        o, tsl = 512 * (t % 2), slice(P * t, P * (t + 1))
                        for kk in range(2 if t < qtok(L) else 0):
                            mm3(job.ps(o, o + HQ), ql, (slice(None), kk, tsl), (hw_hi, hw_lo),
                                (slice(None), slice(HQ * kk, HQ * (kk + 1))), kk == 0, kk == 1)
                        last = mm3(job.ps(o + HQ, o + QKW), kvl, (slice(None), tsl), (hw_hi, hw_lo),
                                   (slice(None), slice(2 * HQ, 2 * HQ + NOPE)), True, True)
                    job.filled(last)

            def b_turn(j0, jt, i, per, h):
                for n, (a, b, nt) in enumerate(((0, NOPE, qtok(L)), (HQ, QKW, TOK), (NOPE, NOPE + P, qtok(L)))):
                    job = Job(jt + n, i, per)
                    job.open(pe)
                    if n == 0:
                        Job(j0 + 2, i, per).taken(pe)
                    if n == 2:
                        pe.wait_ge(b_rot[L], 3 * h + 3)
                    for t in range(nt):
                        last = pe.transpose(job.ps(P * t, P * (t + 1)), qkt[:, t, a:b], ident[:])
                    job.filled(last)

            def b_v(j, i, per):
                job = Job(j, i, per)
                job.open(pe)
                for t in range(TOK):
                    last = mm3(job.ps(P * t, P * (t + 1)), kvl, (slice(None), slice(P * t, P * (t + 1))),
                               (hw_hi, hw_lo), (slice(None), slice(2 * HQ + NOPE, HWC)), True, True)
                job.filled(last)

            def score(t, j, i, per):
                job = Job(j, i, per)
                job.open(pe)
                parts = [(t, 0, NX, 0), (t, NX, NT, NX)]
                if L == 0 and t < 2:
                    parts.append((XTOK + t, NX, NT, NT))
                for qt, ka, kb, o in parts:
                    qs = slice(P * qt, P * (qt + 1))
                    mm3(job.ps(o, o + kb - ka), q, (slice(None), qs), k, (slice(None), slice(ka, kb)), True, False)
                    last = mm3(job.ps(o, o + kb - ka), qr, (slice(0, ROPE), qs), kr,
                               (slice(0, ROPE), slice(ka, kb)), False, True)
                job.filled(last)

            def attend(js, jpv, i, per, h):
                pv = Job(jpv, i, per)

                def turn(n):
                    job = Job(js[n], i, per)
                    job.open(pe)
                    for m, e in enumerate(TJOBS[L][n]):
                        if e < 6:
                            for t in range(XTOK):
                                if n == 0 and m == 0:
                                    pe.wait_ge(s_p[L], 4 * h + (t + 1))
                                o = 512 * m + P * t
                                last = pe.transpose(job.ps(o, o + P), prob[:, t, P * e:P * (e + 1)], ident[:])
                        else:
                            for kt in range(2):
                                for t in range(2):
                                    o = NC * kt + P * t
                                    last = pe.transpose(job.ps(o, o + P), probc[:, t, P * kt:P * (kt + 1)], ident[:])
                    job.filled(last)

                def values(n):
                    Job(js[n], i, per).taken(pe)
                    for e in TJOBS[L][n]:
                        if e == 0:
                            pv.open(pe)
                        p = (pt[0][e % 4], pt[1][e % 4])
                        if e < 6:
                            last = mm3(pv.ps(0, NX), v, (slice(None), slice(P * e, P * (e + 1))), p,
                                       (slice(None), slice(0, NX)), e == 0, e == 5)
                        else:
                            for kt in range(2):
                                last = mm3(pv.ps(NX, NT), v, (slice(None), slice(P * (4 + kt), P * (5 + kt))), p,
                                           (slice(None), slice(NC * kt, NC * (kt + 1))), kt == 0, kt == 1)
                        if e < ENTRIES[L] - 1:
                            last.then_inc(pv_used[L], 1)
                        else:
                            pv.filled(last)
                turn(0)
                turn(1)
                values(0)
                turn(2)
                values(1)
                turn(3)
                values(2)
                values(3)

            b0, b0t = JOB["b0", L], JOB["b0T", L]
            Job(JOB["latT", L] + 2).taken(pe)
            b_tokens(b0, 0, 0, 0)
            pe.wait_ge(kr_rot[L], 3)
            lat_turn(Job(JOB["krT", L]), QR + KVR, LATW, TOK)
            b_v(JOB["v0", L], 0, 0)
            b_turn(b0, b0t, 0, 0, 0)
            Job(b0t + 2).taken(pe)
            j0 = JOB["heads", L]
            with pe.Fori(0, HEADS - 1) as h:
                score(0, j0 + J_S[0], h, J_HEAD)
                b_tokens(j0 + J_B, h, J_HEAD, h + 1)
                for t in range(1, XTOK):
                    score(t, j0 + J_S[t], h, J_HEAD)
                b_turn(j0 + J_B, j0 + J_BT, h, J_HEAD, h + 1)
                attend([j0 + x for x in J_T], j0 + J_PV, h, J_HEAD, h)
                b_v(j0 + J_V, h, J_HEAD)
                Job(j0 + J_BT + 2, h, J_HEAD).taken(pe)
            j0 = JOB["last", L]
            for t in range(XTOK):
                score(t, j0 + J_LS[t], 0, 0)
            attend([j0 + 4, j0 + 5, j0 + 7, j0 + 8], j0 + 6, 0, 0, HEADS - 1)
            pe.wait_ge(cy_lo[L], 4)
            with pe.Fori(0, 2) as i:
                for j in range(4):
                    job = Job(JOB["wo", L] + j, i, 4)
                    c = c0 + C_WO + j
                    pe.wait_ge(chunk_lo, c + 1 + 4 * i)
                    job.open(pe)
                    for n, kk in enumerate((4, 5, 6, 7, 0, 1, 2, 3)):
                        if j == 0 and n == 4:
                            Job(JOB["last", L] + 6).taken(pe)
                        last = part(job, sg, slot(c), P * kk, cat_a if kk < 4 else cat_y, kk % 4, n == 0, n == 7)
                    if L == 0 and j % 2 == 1:
                        last = ada_reduce(job, 16 * (9 + j // 2) + 32 * i)
                    job.filled(last)
            norm_sum(2 * L + 1, JOB["norm2", L])

            def up_first(jn, c):
                jobs = [Job(jn + n) for n in range(4)]
                for j in jobs:
                    j.open(pe)
                pe.wait_ge(chunk_lo, c + 4)
                for m, (kk, stream) in enumerate(pieces(2 * L + 1)):
                    pe.wait_ge(h_lo[2 * L + 1], m + 1)
                    for n in range(4):
                        last = part(jobs[n], [stream], slot(c + n), P * kk, H, kk, kk == 0, kk == KD - 1)
                        if m == len(pieces(2 * L + 1)) - 1:
                            if L == 0 and n % 2 == 1:
                                last = ada_reduce(jobs[n], 16 * (13 + n // 2), (ada_acc, ada_acc2)[n // 2], 1)
                            jobs[n].filled(last)

            def up(jn, c, i):
                for n in range(4):
                    job = Job(jn + n, i, 24)
                    pe.wait_ge(chunk_lo, c + n + 1 + 12 * i)
                    job.open(pe)
                    for kk in range(KD):
                        last = part(job, sg, slot(c + n), P * kk, H, kk, kk == 0, kk == KD - 1)
                    job.filled(last)

            def down(jn, c, p, buf, i, per_j, per_c, ada=None):
                pe.wait_ge(ff_lo[L], 2 * p + 2)
                pe.wait_ge(chunk_lo, c + 2 + per_c * i if per_c else c + 2)
                x = (inner[0][buf], inner[1][buf])
                for m in range(KD):
                    job = Job(jn + m, i, per_j)
                    job.open(pe)
                    for kk in range(2):
                        last = part(job, sg, slot(c + kk), P * m, x, kk, kk == 0, kk == 1)
                    if ada is not None and m == KD - 1:
                        last = ada_reduce(job, ada)
                    job.filled(last)

            up_first(JOB["u0", L], c0 + C_FF)
            jf = JOB["ff", L]
            with pe.Fori(0, (FP - 1) // 2) as i:
                for d in range(2):
                    c = c0 + C_FF + 4 + 6 * d
                    up(jf + 12 * d, c, i)
                    down(jf + 12 * d + 4, c + 4, 2 * i + d, d, i, 24, 12, 16 * (15 + d) + 32 * i if L == 0 else None)
            down(JOB["dlast", L], c0 + NCH - 2, FP - 1, 0, 0, 0, 0)

    @block.scalar
    def _(act):
        def split_hi(c, user=None, i=0, per=0):
            if user is not None:
                user.ready(act)
            n = 16 * (c // 2 + 1)
            act.wait_ge(chunk_in[c % 2], n + 8 * per * i if per else n)
            act.activation(w_hi[c % 4][:], w_raw[c % 2][:], ACT.Copy).then_inc(chunk_hi, 1)

        def head_hi(n):
            act.wait_ge(hw_in, 16 * n + 16)
            act.activation(hw_hi[:], hw_raw[:], ACT.Copy).then_inc(hw_hid, 1)

        def square(nn, m, par, job=None):
            w = NT if nn < 3 else NX
            if job is not None:
                job.taken(act)
            act.wait_ge(ss_done[nn], m + 1)
            act.activation(tmp[par][:, 0:w], X[:, m, 0:w], ACT.Square).then_inc(sq_done[nn], 1)

        def norm_roots(nn, j):
            for sg, a, b in nsegs(nn):
                job = Job(j + sg)
                job.ready(act)
                job.last_read(act.activation(ss[:, a:b], job.ps(a, b), ACT.Sqrt, bias=vec[:, V_EPS:V_EPS + 1],
                                             scale=1.0 / D))

        def norm(nn, between=None):
            L, which = nn // 2, nn % 2
            for n, (kk, (sg, a, b)) in enumerate(pieces(nn)):
                act.wait_ge(t_done[nn], n + 1)
                m = 24 * which + kk
                act.activation(H[0][:, kk, a:b], tmp[kk % 2][:, a:b], ACT.Identity,
                               bias=mod[L][:, sg, m:m + 1]).then_inc(h_hi[nn], 1)
                if n == NORM_BREAK and between:
                    between()

        act.wait_ge(vec_in, 16)
        act.activation(csil[:], vec[:, V_C:V_C + 16], ACT.Silu).then_inc(csil_done, 1)
        act.wait_ge(x_in, 32)
        for m in range(KD):
            square(0, m, m % 2)
        for c in range(2):
            split_hi(c)
        for n in range(ADA0):
            if n == 3:
                norm_roots(0, ADA_NORM)
            if n >= 2:
                Job(JOB["ada"] + ADA_TURN[n - 2]).ready(act)
            job = Job(JOB["ada"] + ADA_ROWS[n])
            job.ready(act)
            job.last_read(act.activation(ada_acc[0:2, n % 2], job.ps(0, ADC)[0:2], ACT.Copy))
        for L in range(DEPTH):
            c0, w = NCH * L, width(L)
            if L == 0:
                def between():
                    split_hi(2)
                    split_hi(3)
                norm(0, between)
                head_hi(0)
            else:
                norm_roots(2, JOB["norm1", 1])
                norm(2)
            for j in range(4):
                if j < 3:
                    act.wait_ge(lat_used, 3 * L + j + 1)
                split_hi(c0 + 4 + j, Job(JOB["lat", L] + 2) if j == 3 else None)
            n = 0
            for t in range(TOK):
                if t % 2 == 0:
                    Job(JOB["lat", L] + t // 2).taken(act)
                for g, (a, b) in enumerate(((0, QR), (QR, QR + KVR), (QR + KVR, LATW))):
                    if g > 0 or t < qtok(L):
                        if n:
                            act.wait_ge(lat_sq[L], n)
                        act.activation(tmp[1][:, 0:b - a], latr[:, t, a:b], ACT.Square,
                                       accum_out=lat_ss[:, g, t:t + 1]).then_inc(lat_sq[L], 1)
                        n += 1
            assert n == LAT_SQ[L]
            act.wait_ge(lat_ms[L], 4)
            act.activation(lat_ss[:], lat_ss[:], ACT.Sqrt).then_inc(lat_rt[L], 1)
            for j in range(8):
                job = Job(JOB["a2", L] + j)
                if j % 4 == 0:
                    pdone = j // 4
                    if pdone:
                        act.wait_ge(pdiff[L], 1)
                    job.ready(act)
                    for s, a, b in segs(L):
                        o = PAD + a + 2 * PAD * s
                        last = act.activation(win_p[:, o:o + b - a], job.ps(a, b), ACT.Copy)
                    job.last_read(last)
                split_hi(c0 + 8 + j, job)
            for n in range(3):
                job = Job(JOB["latT", L] + n)
                job.ready(act)
                if n < 2:
                    ins = act.activation(ql[0][:, n, 0:w], job.ps(0, w), ACT.Copy, scale=V(L, V_QC + n))
                else:
                    ins = act.activation(kvl[0][:], job.ps(0, NT), ACT.Copy, scale=V(L, V_KVC))
                ins.then_inc(lat_hi[L], 1)
            for m in range(2):
                job = Job(JOB["pool", L] + m)
                job.ready(act)
                job.last_read(act.activation(ymix[m][:, 0:w], job.ps(0, w), ACT.Copy, scale=V(L, V_PS + m)))

            def b_stats(j0, i, per, h):
                act.activation(warm[:, 0:1], ones[:, 0:1], ACT.Sqrt)
                for j in range(3):
                    job = Job(j0 + j, i, per)
                    job.ready(act)
                    a = 0 if 2 * j < qtok(L) else HQ
                    src = job.ps().rearrange("p (t c) -> p t c", t=2)[:, :, a:QKW]
                    act.activation(qkt[:, 2 * j:2 * j + 2, a:QKW], src, ACT.Square).then_inc(b_sq[L], 1)
                act.wait_ge(b_ms[L], 4 * h + 4)
                eps = vec[:, V_EPS:V_EPS + 1]
                act.activation(head_ss[:, 0:2], head_ss[:, 0:2], ACT.Sqrt, bias=eps,
                               scale=1.0 / NOPE).then_inc(b_rt[L], 1)
                act.activation(head_ss[:, 2], head_sq[:, :, 2], ACT.Sqrt, bias=eps,
                               scale=1.0 / ROPE).then_inc(b_rt[L], 1)

            def b_halves(j0, i, per):
                for n, (dst, rows, wn) in enumerate(((q, P, w), (k, P, NT), (qr, ROPE, w))):
                    job = Job(j0 + n, i, per)
                    job.ready(act)
                    kw = ({"scale": qg[:, 0:1]}, {"scale": V(L, V_KN)}, {})[n]
                    act.activation(dst[0][0:rows, 0:wn], job.ps(0, wn)[0:rows], ACT.Copy, **kw).then_inc(b_hi[L], 1)

            def v_half(j, i, per):
                job = Job(j, i, per)
                job.ready(act)
                act.activation(v[0][:], job.ps(0, NT), ACT.Copy).then_inc(v_hi[L], 1)

            def exponentials(t, j, i, per, h):
                job = Job(j, i, per)
                act.wait_ge(s_max[L], 4 * h + (t + 1))
                ins = act.activation(prob[:, t], job.ps(0, NT), ACT.Exp, bias=nmax[:, t:t + 1],
                                     accum_out=rsum[:, t:t + 1])
                if L == 0 and t < 2:
                    ins = act.activation(probc[:, t], job.ps(NT, 1024), ACT.Exp, bias=nmax[:, 4 + t:5 + t],
                                         accum_out=rsum[:, 4 + t:5 + t])
                job.last_read(ins)

            def attend(js, jpv, i, per, h):
                for n in range(4):
                    job = Job(js[n], i, per)
                    job.ready(act)
                    for m, e in enumerate(TJOBS[L][n]):
                        if e >= 4:
                            act.wait_ge(pv_used[L], (ENTRIES[L] - 1) * h + (e - 3))
                        act.activation(pt[0][e % 4][:], job.ps(512 * m, 512 * (m + 1)),
                                       ACT.Copy).then_inc(pt_hi[L], 1)

            def attended(jpv, i, per, h):
                job = Job(jpv, i, per)
                job.ready(act)
                act.activation(cat_a[0][:, h, 0:w], job.ps(0, w), ACT.Copy).then_inc(ca_hi[L], 1)

            b0 = JOB["b0", L]
            if L == 1:
                spare_landed(act)
            b_stats(b0, 0, 0, 0)
            job = Job(JOB["krT", L])
            job.ready(act)
            act.activation(kr[0][0:ROPE], job.ps(0, NT)[0:ROPE], ACT.Copy).then_inc(lat_hi[L], 1)
            v_half(JOB["v0", L], 0, 0)
            b_halves(JOB["b0T", L], 0, 0)
            j0 = JOB["heads", L]
            with act.Fori(0, HEADS - 1) as h:
                head_hi(h + (HEADS * L + 1))
                exponentials(0, j0 + J_S[0], h, J_HEAD, h)
                b_stats(j0 + J_B, h, J_HEAD, h + 1)
                for t in range(1, XTOK):
                    exponentials(t, j0 + J_S[t], h, J_HEAD, h)
                b_halves(j0 + J_BT, h, J_HEAD)
                attend([j0 + x for x in J_T], j0 + J_PV, h, J_HEAD, h)
                attended(j0 + J_PV, h, J_HEAD, h)
                v_half(j0 + J_V, h, J_HEAD)
            if L == 0:
                head_hi(HEADS)
            j0 = JOB["last", L]
            for t in range(XTOK):
                exponentials(t, j0 + J_LS[t], 0, 0, HEADS - 1)
            attend([j0 + 4, j0 + 5, j0 + 7, j0 + 8], j0 + 6, 0, 0, HEADS - 1)
            Job(JOB["a2", L] + 7).taken(act)
            Job(JOB["pool", L] + 1).taken(act)
            for j in range(4):
                act.activation(cat_y[0][:, j, 0:w], ymix[j][:, 0:w], ACT.Copy).then_inc(cy_hi[L], 1)
            attended(j0 + 6, 0, 0, HEADS - 1)
            with act.Fori(0, 2) as i:
                for j in range(4):
                    job = Job(JOB["wo", L] + j, i, 4)
                    split_hi(c0 + 16 + j, job, i, 4)
                    square(2 * L + 1, 4 * i + j, j % 2, job)
            norm_roots(2 * L + 1, JOB["norm2", L])
            norm(2 * L + 1)

            def ff_tile(t, jn, c, par, buf, i, per_j, per_c):
                g, u = Job(jn, i, per_j), Job(jn + 1, i, per_j)
                g.ready(act)
                tap = vec[:, bass.ds(L * V_LAYER + V_FC + FT + t, 1)]
                act.activation(tmp[par][:, 0:w], g.ps(0, w), ACT.Copy, scale=tap).then_inc(ff_mid[L], 1)
                split_hi(c, g, i, per_c)
                g.taken(act)
                act.activation(tmp[par][:, 0:w], tmp[par][:, 0:w], ACT.Silu).then_inc(ff_silu[L], 1)
                split_hi(c + 1, u, i, per_c)
                u.taken(act)
                act.activation(inner[0][buf][:, par, 0:w], ff_v[:, 0:w], ACT.Copy).then_inc(ff_hi[L], 1)

            for t in range(2):
                ff_tile(t, JOB["u0", L] + 2 * t, c0 + C_FF + 4 + 2 * t, t, 0, 0, 0, 0)
            jf = JOB["ff", L]
            with act.Fori(0, (FP - 1) // 2) as i:
                for d in range(2):
                    c = c0 + C_FF + 4 + 6 * d
                    for t in range(2):
                        ff_tile(4 * i + (2 * (d + 1) + t), jf + 12 * d + 2 * t, c + 4 + 2 * t, t, 1 - d, i, 24, 12)
                    for x in range(2):
                        split_hi(c + 8 + x, Job(jf + 12 * d + 11, i, 24), i, 12)
            if L == 0:
                for m in range(KD):
                    square(2, m, m % 2, Job(JOB["dlast", 0] + m))
                for x in range(2):
                    split_hi(c0 + NCH + 2 + x, Job(JOB["dlast", 0] + 7))

    @block.vector
    def _(dve):
        def split_lo(c, i=0, per=0):
            dve.wait_ge(chunk_hi, c + 1 + per * i if per else c + 1)
            dve.tensor_tensor(w_lo[c % 4][:], w_raw[c % 2][:], w_hi[c % 4][:].bitcast(F32),
                              ALU.subtract).then_inc(chunk_lo, 1)

        def head_lo(n):
            dve.wait_ge(hw_hid, n + 1)
            dve.tensor_tensor(hw_lo[:], hw_raw[:], hw_hi[:].bitcast(F32), ALU.subtract).then_inc(hw_lod, 1)

        def ada_chunks(b, ks, i=0, per=0, acc=ada_acc, ns=2):
            for kk in ks:
                c = 8 * (b - ADA0) + kk
                n = 16 * (c // 4 + 1)
                dve.wait_ge(ada_in[c % 4], n + 32 * per * i if per else n)
                for s in range(ns):
                    cs = csil[:, 8 * s + kk:8 * s + kk + 1]
                    if kk == 0:
                        ins = dve.tensor_scalar(acc[:, s], ada_raw[c % 4][:], cs, None, ALU.mult)
                    else:
                        done = 2 * c + s - (ns - 1)
                        dve.wait_ge(ada_op, done + 16 * per * i if per else done)
                        ins = dve.scalar_tensor_tensor(acc[:, s], ada_raw[c % 4][:], cs, acc[:, s],
                                                       ALU.mult, ALU.add)
                    ins.then_inc(ada_op, 2 // ns)

        def ada_out(L, b, job, ns=2):
            bias = vec[:, bass.ds(L * V_LAYER + V_ADAB + 4 * b, 4)].unsqueeze(1).to_broadcast([P, ns, 4])
            return dve.tensor_tensor(mod[L][:, 0:ns, bass.ds(4 * b, 4)],
                                     job.ps(768, 768 + 4 * ns).rearrange("p (s c) -> p s c", s=ns), bias, ALU.add)

        def clear_ss(nn):
            dve.memset(ss[:, 0:NT if nn < 3 else NX], 0.0).then_inc(ss_done[nn], 2)

        def add_squares(nn, m, par):
            w = NT if nn < 3 else NX
            dve.wait_ge(sq_done[nn], m + 1)
            dve.wait_ge(ss_done[nn], m + 2)
            dve.tensor_tensor(ss[:, 0:w], ss[:, 0:w], tmp[par][:, 0:w], ALU.add).then_inc(ss_done[nn], 1)

        def norm_inverse(nn, j, sg):
            _, a, b = ALL[sg]
            Job(j + sg).taken(dve)
            dve.reciprocal(ss[:, a:b], ss[:, a:b]).then_inc(rms_ok[nn], 1)

        def norm(nn, j=None, between=None):
            L, which = nn // 2, nn % 2
            if nn == 0:
                Job(JOB["ada"] + ADA_TURN[ADA0 - 1]).taken(dve)
            else:
                dve.wait_ge(mod_done, ADB - 6 if L == 0 else 2 * ADB - 4)
            g = V(L, V_N1 if which == 0 else V_N2, 8).unsqueeze(1).to_broadcast([P, 2, 8])
            dve.scalar_tensor_tensor(amul[:], mod[L][:, :, 24 * which + 8:24 * which + 16], 1.0, g, ALU.add,
                                     ALU.mult).then_inc(scale_ok[nn], 1)
            if j is not None:
                norm_inverse(nn, j, 0)
            dve.wait_ge(scale_ok[nn], 1)
            work = pieces(nn)

            def scaled(n):
                kk, (sg, a, b) = work[n]
                if j is not None and (kk, sg) == (0, 1):
                    norm_inverse(nn, j, 1)
                dve.wait_ge(rms_ok[nn], 1 + sg)
                if n >= 2:
                    dve.wait_ge(h_lo[nn], n - 1)
                dve.scalar_tensor_tensor(tmp[kk % 2][:, a:b], X[:, kk, a:b], amul[:, sg, kk:kk + 1], ss[:, a:b],
                                         ALU.mult, ALU.mult).then_inc(t_done[nn], 1)
            scaled(0)
            for n, (kk, (sg, a, b)) in enumerate(work):
                if n + 1 < len(work):
                    scaled(n + 1)
                dve.wait_ge(h_hi[nn], n + 1)
                m = 24 * which + kk
                dve.scalar_tensor_tensor(H[1][:, kk, a:b], tmp[kk % 2][:, a:b], mod[L][:, sg, m:m + 1],
                                         H[0][:, kk, a:b].bitcast(F32), ALU.add, ALU.subtract).then_inc(h_lo[nn], 1)
                if n == NORM_BREAK and between:
                    between()

        def lo_half(dst, src, hi, scale=None):
            if scale is None:
                return dve.tensor_tensor(dst, src, hi.bitcast(F32), ALU.subtract)
            return dve.scalar_tensor_tensor(dst, src, scale, hi.bitcast(F32), ALU.mult, ALU.subtract)

        def update_x(m, L, job, gate, loop=False):
            for s, a, b in segs(L):
                xo = X[:, m, a:b]
                last = dve.scalar_tensor_tensor(xo, job.ps(a, b), mod[L][:, s, bass.ds(gate + m, 1)], xo,
                                                ALU.mult, ALU.add)
            job.last_read(last)

        clear_ss(0)
        dve.wait_ge(vec_in, 16)
        dve.wait_ge(csil_done, 1)
        for m in range(KD):
            add_squares(0, m, m % 2)
        for c in range(2):
            split_lo(c)
        for n, b in enumerate(ADA_FIRST):
            if n == 2:
                norm_inverse(0, ADA_NORM, 0)
                norm_inverse(0, ADA_NORM, 1)
            job = Job(JOB["ada"] + ADA_TURN[n])
            job.ready(dve)
            bias = V(0, V_ADAB + 4 * b, 4).unsqueeze(1).to_broadcast([P, 2, 4])
            job.last_read(dve.tensor_tensor(mod[0][:, :, 4 * b:4 * b + 4],
                                            job.ps(0, 8).rearrange("p (c s) -> p s c", s=2), bias, ALU.add))
        for L in range(DEPTH):
            c0, w, sg = NCH * L, width(L), segs(L)
            if L == 0:
                def between():
                    split_lo(2)
                    split_lo(3)
                norm(0, None, between)
                head_lo(0)
            else:
                norm(2, JOB["norm1", 1])
            for j in range(4):
                split_lo(c0 + 4 + j)
            dve.wait_ge(tab_in, 48 * (L + 1))
            for n in range(4):
                gb = rgain[:, n:n + 1].to_broadcast([P, TOK, ROPE])
                dve.scalar_tensor_tensor(rtab[:, n], rtab[:, n], SCALE if n < 2 else 1.0, gb, ALU.mult,
                                         ALU.mult).then_inc(tab_ok[L], 1)
            dve.tensor_scalar(qg[:, 0:1], V(L, V_QN), SCALE, None, ALU.mult).then_inc(tab_ok[L], 1)
            for j in range(3):
                job = Job(JOB["lat", L] + j)
                job.ready(dve)
                a = 0 if 2 * j < qtok(L) else QR
                src = job.ps().rearrange("p (t c) -> p t c", t=2)[:, :, a:LATW]
                job.last_read(dve.tensor_copy(latr[:, 2 * j:2 * j + 2, a:LATW], src))
            if L == 0:
                ada_chunks(4, range(8))
            dve.wait_ge(lat_sq[L], LAT_SQ[L])
            for g, n in enumerate((QR, KVR, ROPE)):
                dve.tensor_scalar(lat_ss[:, g], lat_ss[:, g], 1.0 / n, EPS, ALU.mult, ALU.add).then_inc(lat_ms[L], 1)
            dve.wait_ge(lat_ms[L], 3)
            dve.reciprocal(lat_ss[:], lat_ss[:]).then_inc(lat_ms[L], 1)
            dve.wait_ge(lat_rt[L], 1)
            for g, (a, b) in enumerate(((0, QR), (QR, QR + KVR), (QR + KVR, LATW))):
                nt = TOK if g > 0 else qtok(L)
                r = lat_ss[:, g, 0:nt].unsqueeze(2).to_broadcast([P, nt, b - a])
                dve.tensor_tensor(latr[:, 0:nt, a:b], latr[:, 0:nt, a:b], r, ALU.mult).then_inc(lat_nm[L], 1)
            ncv = 1 + 2 * len(sg)
            for j in range(8):
                job, m, role = Job(JOB["a2", L] + j), j // 4, ROLES[j % 4]
                y = ymix[2 + m]
                if L == 0 and j in (2, 4, 6):
                    ada_chunks(4 + j // 2, range(8))
                if role != "pool":
                    job.ready(dve)
                if L == 0 and j % 2 == 1:
                    ada_out(0, 4 + j // 2, job).then_inc(mod_done, 1)
                if role == "gate_c":
                    job.last_read(dve.tensor_copy(tmp[0][:, 0:w], job.ps(0, w)))
                elif role == "conv_in":
                    Job(JOB["a2", L] + j - 1).taken(dve)
                    job.last_read(dve.tensor_tensor(tmp[1][:, 0:w], tmp[0][:, 0:w], job.ps(0, w), ALU.mult))
                    job.taken(dve)
                    dve.tensor_scalar(y[:, 0:w], tmp[1][:, 0:w], V(L, V_SC + 3 * m + 1), None,
                                      ALU.mult).then_inc(cv[L], 1)
                    n = ncv * m + 1
                    for tap, d0, s0 in ((0, 1, 0), (2, 0, 1)):
                        for _, a, b in sg:
                            dve.wait_ge(cv[L], n)
                            yo = y[:, a + d0:b - 1 + d0]
                            dve.scalar_tensor_tensor(yo, tmp[1][:, a + s0:b - 1 + s0], V(L, V_SC + 3 * m + tap), yo,
                                                     ALU.mult, ALU.add).then_inc(cv[L], 1)
                            n += 1
                elif role == "gate_b":
                    dve.wait_ge(cv[L], ncv * (m + 1))
                    job.last_read(dve.tensor_tensor(y[:, 0:w], y[:, 0:w], job.ps(0, w), ALU.mult))
                    dve.wait_ge(win_ok[L], m + 1)
                    for s, a, b in sg:
                        o = PAD + a + 2 * PAD * s
                        last = dve.scalar_tensor_tensor(ymix[m][:, a:b], win_r[:, o:o + b - a],
                                                        vec[:, V_INVW + m:V_INVW + m + 1], win_p[:, o:o + b - a],
                                                        ALU.mult, ALU.subtract)
                    last.then_inc(pdiff[L], 1)
                split_lo(c0 + 8 + j)
            for n in range(3):
                job = Job(JOB["latT", L] + n)
                dve.wait_ge(lat_hi[L], n + 1)
                if n < 2:
                    ins = lo_half(ql[1][:, n, 0:w], job.ps(0, w), ql[0][:, n, 0:w], V(L, V_QC + n))
                else:
                    ins = lo_half(kvl[1][:], job.ps(0, NT), kvl[0][:], V(L, V_KVC))
                job.last_read(ins)

            def b_norm(j0, i, per, h):
                for j in range(3):
                    dve.wait_ge(b_sq[L], 3 * h + (j + 1))
                    a = 0 if 2 * j < qtok(L) else HQ
                    sq = qkt[:, 2 * j:2 * j + 2, a:QKW].rearrange("p t (g f) -> p t g f", f=ROPE)
                    dve.tensor_reduce(head_sq[:, 2 * j:2 * j + 2, a // ROPE:], sq, AX.X, ALU.add).then_inc(b_ms[L], 1)
                dve.wait_ge(b_ms[L], 4 * h + 3)
                parts = head_sq[:].rearrange("p t g -> p g t")
                dve.tensor_tensor(head_ss[:, 0:2], parts[:, 0:4:3], parts[:, 1:5:3], ALU.add).then_inc(b_ms[L], 1)
                dve.wait_ge(b_rt[L], 2 * h + 2)
                dve.reciprocal(head_ss[:], head_ss[:]).then_inc(b_rc[L], 1)
                dve.wait_ge(b_rc[L], h + 1)
                for j in range(3):
                    job = Job(j0 + j, i, per)
                    src = job.ps().rearrange("p (t c) -> p t c", t=2)
                    for g, a, b in ((0, 0, NOPE), (2, NOPE, HQ), (1, HQ, QKW)):
                        if g == 1 or 2 * j < qtok(L):
                            r = head_ss[:, g, 2 * j:2 * j + 2].unsqueeze(2).to_broadcast([P, 2, b - a])
                            last = dve.tensor_tensor(qkt[:, 2 * j:2 * j + 2, a:b], src[:, :, a:b], r, ALU.mult)
                    job.last_read(last)

            def b_halves(j0, i, per, h):
                for n, (dst, rows, wn) in enumerate(((q, P, w), (k, P, NT), (qr, ROPE, w))):
                    job = Job(j0 + n, i, per)
                    dve.wait_ge(b_hi[L], 3 * h + (n + 1))
                    scale = (qg[:, 0:1], V(L, V_KN), None)[n]
                    job.last_read(lo_half(dst[1][0:rows, 0:wn], job.ps(0, wn)[0:rows], dst[0][0:rows, 0:wn], scale))

            def v_half(j, i, per, h):
                dve.wait_ge(v_hi[L], h + 1)
                job = Job(j, i, per)
                job.last_read(lo_half(v[1][:], job.ps(0, NT), v[0][:]))

            def maxima(t, j, i, per):
                job = Job(j, i, per)
                job.ready(dve)
                last = dve.tensor_reduce(nmax[:, t:t + 1], job.ps(0, NT), AX.X, ALU.max, negate=True)
                if L == 0 and t < 2:
                    last = dve.tensor_reduce(nmax[:, 4 + t:5 + t], job.ps(NT, 1024), AX.X, ALU.max, negate=True)
                last.then_inc(s_max[L], 1)

            def probabilities(t, j, i, per, h):
                Job(j, i, per).taken(dve)
                if L == 0 and t < 2:
                    dve.reciprocal(rsum[:, 4 + t:5 + t], rsum[:, 4 + t:5 + t])
                dve.reciprocal(rsum[:, t:t + 1], rsum[:, t:t + 1]).then_inc(s_rec[L], 1)
                dve.wait_ge(s_rec[L], 4 * h + (t + 1))
                if L == 0 and t < 2:
                    dve.tensor_scalar(probc[:, t], probc[:, t], rsum[:, 4 + t:5 + t], None, ALU.mult)
                dve.tensor_scalar(prob[:, t], prob[:, t], rsum[:, t:t + 1], None, ALU.mult).then_inc(s_p[L], 1)

            def attend(js, i, per, h):
                for n in range(4):
                    job = Job(js[n], i, per)
                    for m, e in enumerate(TJOBS[L][n]):
                        dve.wait_ge(pt_hi[L], ENTRIES[L] * h + (e + 1))
                        ins = lo_half(pt[1][e % 4][:], job.ps(512 * m, 512 * (m + 1)), pt[0][e % 4][:])
                    job.last_read(ins)

            def attended(jpv, i, per, h):
                job = Job(jpv, i, per)
                dve.wait_ge(ca_hi[L], h + 1)
                job.last_read(lo_half(cat_a[1][:, h, 0:w], job.ps(0, w), cat_a[0][:, h, 0:w]))

            b0 = JOB["b0", L]
            if L == 1:
                spare_landed(dve)
            b_norm(b0, 0, 0, 0)
            dve.wait_ge(lat_hi[L], 4)
            job = Job(JOB["krT", L])
            job.last_read(lo_half(kr[1][0:ROPE], job.ps(0, NT)[0:ROPE], kr[0][0:ROPE]))
            v_half(JOB["v0", L], 0, 0, 0)
            b_halves(JOB["b0T", L], 0, 0, 0)
            j0 = JOB["heads", L]
            with dve.Fori(0, HEADS - 1) as h:
                head_lo(h + (HEADS * L + 1))
                maxima(0, j0 + J_S[0], h, J_HEAD)
                b_norm(j0 + J_B, h, J_HEAD, h + 1)
                for t in range(1, XTOK):
                    maxima(t, j0 + J_S[t], h, J_HEAD)
                    probabilities(t - 1, j0 + J_S[t - 1], h, J_HEAD, h)
                probabilities(XTOK - 1, j0 + J_S[XTOK - 1], h, J_HEAD, h)
                b_halves(j0 + J_BT, h, J_HEAD, h + 1)
                attend([j0 + x for x in J_T], h, J_HEAD, h)
                attended(j0 + J_PV, h, J_HEAD, h)
                v_half(j0 + J_V, h, J_HEAD, h + 1)
            if L == 0:
                head_lo(HEADS)
            j0 = JOB["last", L]
            for t in range(XTOK):
                maxima(t, j0 + J_LS[t], 0, 0)
                if t:
                    probabilities(t - 1, j0 + J_LS[t - 1], 0, 0, HEADS - 1)
            probabilities(XTOK - 1, j0 + J_LS[XTOK - 1], 0, 0, HEADS - 1)
            attend([j0 + 4, j0 + 5, j0 + 7, j0 + 8], 0, 0, HEADS - 1)
            for j in range(4):
                dve.wait_ge(cy_hi[L], j + 1)
                lo_half(cat_y[1][:, j, 0:w], ymix[j][:, 0:w], cat_y[0][:, j, 0:w]).then_inc(cy_lo[L], 1)
            attended(j0 + 6, 0, 0, HEADS - 1)
            nn = 2 * L + 1
            clear_ss(nn)
            with dve.Fori(0, 2) as i:
                for j in range(4):
                    job = Job(JOB["wo", L] + j, i, 4)
                    if L == 0:
                        ada_chunks(8 + j // 2, ADA_WO[j % 2], i, 2)
                    job.ready(dve)
                    if L == 0 and j % 2 == 1:
                        ada_out(0, 2 * i + (8 + j // 2), job).then_inc(mod_done, 1)
                    update_x(4 * i + j, L, job, 16)
                    split_lo(c0 + 16 + j, i, 4)
                    add_squares(nn, 4 * i + j, j % 2)
            norm(nn, JOB["norm2", L])
            if L == 0:
                ada_chunks(12, range(8), ns=1)
                ada_chunks(13, range(8), acc=ada_acc2, ns=1)

            def ff_tile(t, jn, c, par, buf, i, per_j, per_c, ada=None):
                g, u = Job(jn, i, per_j), Job(jn + 1, i, per_j)
                if ada is not None:
                    ada_chunks(ada, ADA_UP[par][0], i, 2)
                dve.wait_ge(ff_mid[L], t + 1)
                n, per_tile = 0, 2 * len(sg) - 1
                for tap, d0, s0 in ((0, 1, 0), (2, 0, 1)):
                    for _, a, b in sg:
                        if n:
                            dve.wait_ge(ff_conv[L], per_tile * t + n)
                        y = tmp[par][:, a + d0:b - 1 + d0]
                        ins = dve.scalar_tensor_tensor(y, g.ps(a + s0, b - 1 + s0),
                                                       vec[:, bass.ds(L * V_LAYER + V_FC + FT * tap + t, 1)], y,
                                                       ALU.mult, ALU.add)
                        n += 1
                        if n <= per_tile:
                            ins.then_inc(ff_conv[L], 1)
                        else:
                            g.last_read(ins)
                split_lo(c, i, per_c)
                if ada is not None:
                    ada_chunks(ada, ADA_UP[par][1], i, 2)
                u.ready(dve)
                dve.wait_ge(ff_silu[L], t + 1)
                return u

            def ff_value(t, u, c, par, buf, i, per_c):
                u.last_read(dve.tensor_tensor(ff_v[:, 0:w], tmp[par][:, 0:w], u.ps(0, w), ALU.mult))
                split_lo(c + 1, i, per_c)
                dve.wait_ge(ff_hi[L], t + 1)
                lo_half(inner[1][buf][:, par, 0:w], ff_v[:, 0:w],
                        inner[0][buf][:, par, 0:w]).then_inc(ff_lo[L], 1)

            for t in range(2):
                u = ff_tile(t, JOB["u0", L] + 2 * t, c0 + C_FF + 4 + 2 * t, t, 0, 0, 0, 0)
                if L == 0:
                    ada_out(1, ADB - 2 + t, u, 1).then_inc(mod_done, 1)
                ff_value(t, u, c0 + C_FF + 4 + 2 * t, t, 0, 0, 0)
            jf = JOB["ff", L]
            with dve.Fori(0, (FP - 1) // 2) as i:
                for d in range(2):
                    c = c0 + C_FF + 4 + 6 * d
                    for t in range(2):
                        tile, cc = 4 * i + (2 * (d + 1) + t), c + 4 + 2 * t
                        u = ff_tile(tile, jf + 12 * d + 2 * t, cc, t, 1 - d, i, 24, 12, 14 + d if L == 0 else None)
                        ff_value(tile, u, cc, t, 1 - d, i, 12)
                    for m in range(KD):
                        job = Job(jf + 12 * d + 4 + m, i, 24)
                        job.ready(dve)
                        if L == 0 and m == KD - 1:
                            ada_out(1, 2 * i + d, job).then_inc(mod_done, 1)
                        update_x(m, L, job, 40)
                    for x in range(2):
                        split_lo(c + 8 + x, i, 12)
            if L == 0:
                clear_ss(2)
            for m in range(KD):
                job = Job(JOB["dlast", L] + m)
                job.ready(dve)
                update_x(m, L, job, 40)
                if L == 0 and m:
                    add_squares(2, m - 1, (m - 1) % 2)
            if L == 0:
                add_squares(2, KD - 1, (KD - 1) % 2)
                for x in range(2):
                    split_lo(c0 + NCH + 2 + x)

    ctx.close()


def pack_vectors(a):
    cols = np.zeros((P, NV), np.float32)

    def put(c, x):
        x = np.asarray(x, np.float32).reshape(-1, P).T
        cols[:, c:c + x.shape[1]] = x
    for L in range(DEPTH):
        o = L * V_LAYER
        for c, name in ((V_N1, "norm1_g"), (V_N2, "norm2_g"), (V_ADAB, "ada_b"), (V_QC, "qc_g"), (V_KVC, "kvc_g"),
                        (V_QN, "qn_g"), (V_KN, "kn_g"), (V_PS, "pool_scale")):
            put(o + c, a[name][L])
        for m in range(2):
            for tap in range(3):
                put(o + V_SC + 3 * m + tap, a["sconv_w"][L][tap, P * m:P * (m + 1)])
        for tap in range(3):
            put(o + V_FC + FT * tap, a["ff_conv"][L][tap])
    put(V_C, a["c"][0])
    put(V_C + 8, a["c_ctx"])
    for m, pair in enumerate(((2, 4), (8, 16))):
        for half, win in enumerate(pair):
            rows = slice(64 * half, 64 * half + 64)
            cols[rows, V_INVW + m] = 1.0 / win
            for t in range(PAD):
                left = min(t + win // 2, NC) - max(t - win // 2, 0)
                right = min(NC - PAD + t + win // 2, NC) - (NC - PAD + t - win // 2)
                cols[rows, V_RATIO + 16 * m + t] = win / left
                cols[rows, V_RATIO + 16 * m + 8 + t] = win / right
    cols[:, V_EPS] = EPS
    return cols


def rope_tables():
    t = np.arange(NX)
    nf = ROPE // 4
    inv = (10000.0 ** (-np.arange(nf, dtype=np.float32) / nf)).astype(np.float32)
    ar = (t // GRID_W).astype(np.float32)[:, None] * inv
    ac = (t % GRID_W).astype(np.float32)[:, None] * inv
    ang = np.concatenate([ar, ar, ac, ac], axis=-1)
    sign = np.tile(np.repeat(np.array([-1.0, 1.0], np.float32), nf), 2)
    tab = np.zeros((2, NT, ROPE), np.float32)
    tab[0] = 1.0
    tab[0, :NX] = np.cos(ang)
    tab[1, :NX] = np.sin(ang) * sign
    return np.ascontiguousarray(tab.reshape(2, TOK, P, ROPE).transpose(2, 0, 1, 3))


def tiles(w):
    n = w.shape[1] // P
    return w.reshape(KD, P, n, P).transpose(2, 1, 0, 3).reshape(n, P, CH)


def layout(a):
    a = {n: np.asarray(x) for n, x in a.items()}
    main = np.zeros((DEPTH * NCH + SPARE, P, CH), np.float32)
    heads = np.zeros((DEPTH * HEADS, P, 2 * HQ + 2 * NOPE), np.float32)
    rgain = np.zeros((DEPTH, 4, ROPE), np.float32)
    partner = np.arange(ROPE).reshape(2, 2, ROPE // 4)[:, ::-1].reshape(-1)
    for L in range(DEPTH):
        w_in, m = a["w_in"][L], main[NCH * L:NCH * (L + 1)]
        lat = w_in[:, :LATW].reshape(4, 2, P, LATW).transpose(0, 2, 1, 3).reshape(4, P, 2 * LATW)
        m[C_LAT:C_LAT + 4, :, :2 * LATW] = lat
        rest = tiles(np.ascontiguousarray(w_in[:, LATW:]))
        m[C_A2:C_A2 + 8] = rest[[0, 4, 6, 2, 1, 5, 7, 3]]
        m[C_WO:C_WO + 8] = tiles(a["w_o"][L])
        up = tiles(a["ff_up"][L])
        down = a["ff_down"][L].reshape(FT, P, D)
        c = C_FF
        for p in range(FP + 1):
            if p < FP:
                m[c:c + 4] = up[[2 * p, FT + 2 * p, 2 * p + 1, FT + 2 * p + 1]]
                c += 4
            if p:
                m[c:c + 2] = down[2 * p - 2:2 * p]
                c += 2
        wq = a["w_q_up"][L].reshape(2, P, HEADS, HQ)
        wkv = a["w_kv_up"][L].reshape(P, HEADS, NOPE + P)
        for h in range(HEADS):
            w = heads[HEADS * L + h]
            w[:, :2 * HQ] = wq[:, :, h].transpose(1, 0, 2).reshape(P, 2 * HQ)
            w[:, 2 * HQ:] = wkv[:, h]
        rgain[L] = [a["qr_g"][L], a["qr_g"][L][partner], a["kr_g"][L], a["kr_g"][L][partner]]
    ada = a["ada_w"].reshape(DEPTH, KD, P, ADB, ADC).transpose(0, 3, 1, 2, 4).reshape(DEPTH * ADB, KD, P, ADC)
    order = list(range(ADB)) + [2 * ADB - 2, 2 * ADB - 1] + list(range(ADB, 2 * ADB - 2))
    ada = np.concatenate([ada[order].reshape(DEPTH * ADB * KD, P, ADC), np.zeros((ADA_SPARE, P, ADC), np.float32)])
    return {
        "x": a["x"][0].T.reshape(KD, P, NX).transpose(1, 0, 2), "ctx": a["ctx"][0].T.reshape(KD, P, NC).transpose(1, 0, 2),
        "vec": pack_vectors(a), "rope": rope_tables(), "rgain": rgain, "pool_w": a["pool_w"],
        "w_main": main, "w_head": heads, "w_ada": ada,
    }


def kernel(**inputs):
    import concourse.bacc as bacc
    from concourse.bass_utils import run_bass_kernel_spmd

    nc = bacc.Bacc("TRN2", target_bir_lowering=False, num_devices=1)
    arrays, dram = {}, {}
    for name, x in layout(inputs).items():
        arrays[f"in_{name}"] = np.ascontiguousarray(x)
        dram[name] = nc.dram_tensor(f"in_{name}", x.shape, F32, kind="ExternalInput").ap()
    dram["out"] = nc.dram_tensor("out_x", (KD, P, NX), F32, kind="ExternalOutput").ap()
    build(nc, dram)
    r = run_bass_kernel_spmd(nc, [arrays], core_ids=[0])
    return np.ascontiguousarray(r.results[0]["out_x"].reshape(D, NX).T)[None]
```

```python
import numpy as np
import concourse.bass as bass
from concourse import mybir
from contextlib import ExitStack

F32 = mybir.dt.float32
F32R = mybir.dt.float32r
ALU = mybir.AluOpType
ACT = mybir.ActivationFunctionType
AX = mybir.AxisListType

P = 128
D = 1024
KD = D // P
DEPTH = 2
NX, NC = 512, 256
NT = NX + NC
TOK = NT // P
XTOK = NX // P
GRID_W = 64
HEADS = 4
NOPE, ROPE = 128, 64
SCALE = (NOPE + ROPE) ** -0.5
QR, KVR = 256, 128
LATW = QR + KVR + ROPE
HQ = NOPE + ROPE
QKW = HQ + NOPE
DFF = 2816
FT = DFF // P
FP = FT // 2
EPS = 1e-6
CH = 1024
ADC = 512
ADB = 6 * D // ADC
ADB_X = ADB // 2 - 1
PAD = 8

C_LAT, C_A2, C_WO, C_FF = 0, 4, 12, 20
NCH = C_FF + 6 * FP
SPARE = 4
ADA0 = 4
ADA_SPARE = 4
V_N1, V_N2, V_ADAB, V_QC, V_KVC, V_QN, V_KN, V_PS, V_SC, V_FC = 0, 8, 16, 64, 66, 67, 68, 69, 71, 77
V_LAYER = V_FC + 3 * FT
V_C = DEPTH * V_LAYER
V_INVW = V_C + 16
V_RATIO = V_INVW + 2
V_EPS = V_RATIO + 32
NV = V_EPS + 1


ADA_FIRST, ADA_ROWS, ADA_TURN, ADA_NORM = (2, 3, 0, 1), (0, 1, 3, 7), (2, 4, 8, 9), 5


def job_plan():
    plan, n = {"ada": 0}, 2 * ADA0 + 2
    for L in range(DEPTH):
        for name, count in [("norm1", 2 * L), ("lat", 3), ("a2", 6), ("latT", 3), ("a2last", 2), ("b0", 3),
                            ("pool0", 1), ("krT", 1), ("pool1", 1), ("b0T", 3), ("v0", 1),
                            ("heads", 16 * (HEADS - 1)), ("last", 9), ("wo", 8), ("norm2", 2 - L), ("u0", 4),
                            ("ff", 24 * ((FP - 1) // 2)), ("dlast", 8)]:
            plan[name, L] = n
            n += count
    plan["norm1", 0] = ADA_NORM
    for L in range(DEPTH):
        plan["a2", L] = [plan["a2", L] + j for j in range(6)] + [plan["a2last", L] + j for j in range(2)]
        plan["pool", L] = [plan["pool0", L], plan["pool1", L]]
    assert all(plan["v0", L] == plan["heads", L] - 1 for L in range(DEPTH))
    return plan


JOB = job_plan()


def build(nc, dram):
    ctx = ExitStack()
    base = (nc.sbuf_base + 31) // 32 * 32

    def at(name, off, shape, dt=F32):
        return nc.alloc_sbuf_tensor_at(name, shape, dt, offset=base + off)

    class Place:
        def __init__(self, off):
            self.off = off

        def __call__(self, name, shape, dt=F32, extra=0):
            t = at(name, self.off, shape, dt)
            self.off += (4 * int(np.prod(shape[1:])) + extra + 31) // 32 * 32
            return t

    sb = Place(0)
    X = sb("X", [P, KD, NT])
    vec = sb("vec", [P, NV + (-NV) % 8])
    mod = [sb(f"mod{L}", [P, 2, 48]) for L in range(DEPTH)]
    csil = sb("csil", [P, 16])
    amul = sb("amul", [P, 2, 8])
    qg = sb("qg", [P, 8])
    lat_ss = sb("lat_ss", [P, 3, TOK])
    head_ss = sb("head_ss", [P, 3, TOK])
    head_sq = sb("head_sq", [P, TOK, 5])
    warm = sb("warm", [P, 8])
    nmax = sb("nmax", [P, 8])
    rsum = sb("rsum", [P, 8])
    ident = sb("ident", [P, P])
    ones = sb("ones", [P, P])
    poolw = sb("poolw", [P, 2, P])
    rgain = sb("rgain", [P, 4, ROPE])
    rtab = sb("rtab", [P, 4, TOK, ROPE])
    w_raw = [sb(f"w_raw{s}", [P, CH]) for s in range(2)]
    w_hi = [sb(f"w_hi{s}", [P, CH], F32R) for s in range(4)]
    w_lo = [sb(f"w_lo{s}", [P, CH], F32R) for s in range(4)]
    HWC = 2 * HQ + 2 * NOPE
    hw_raw = sb("hw_raw", [P, HWC])
    hw_hi = sb("hw_hi", [P, HWC], F32R)
    hw_lo = sb("hw_lo", [P, HWC], F32R)
    mid = Place(sb.off)
    ql = [mid(f"ql_{x}", [P, 2, NT], F32R) for x in ("hi", "lo")]
    kvl = [mid(f"kvl_{x}", [P, NT], F32R) for x in ("hi", "lo")]
    kr = [mid(f"kr_{x}", [P, NT], F32R) for x in ("hi", "lo")]
    ymix = [None] * 4
    for j in (0, 2, 3):
        ymix[j] = mid(f"ymix{j}", [P, NT])
    win_a = at("win_a", mid.off, [P, NT + 4 * PAD])
    ymix[1] = mid("ymix1", [P, NT], F32, extra=4 * 4 * PAD)
    cat_y = [at(f"cat_y_{x}", sb.off + 4 * 4 * NT * n, [P, 4, NT], F32R) for n, x in enumerate(("hi", "lo"))]
    ph = Place(mid.off)
    ada_raw = [ph(f"ada_raw{s}", [P, ADC]) for s in range(4)]
    ada_acc = ph("ada_acc", [P, 2, ADC])
    tmp = [ph(f"tmp{s}", [P, NT]) for s in range(2)]
    ss = ph("ss", [P, NT])
    lo_free = ph.off
    H = [ph(f"H_{x}", [P, KD, NT], F32R) for x in ("hi", "lo")]
    ada_acc2 = at("ada_acc2", ph.off, [P, 1, ADC])
    latr = ph("latr", [P, TOK, LATW])
    ada_first = [at(f"ada_first{b}", (sb.off, lo_free)[b // 2] + 4 * KD * ADC * (b % 2), [P, KD, ADC])
                 for b in range(ADA0)]
    assert 2 * 4 * KD * ADC <= min(mid.off - sb.off, 2 * 4 * KD * NT)
    win_p = ph("win_p", [P, NT + 4 * PAD])
    win_r = ph("win_r", [P, NT + 4 * PAD])
    hd = Place(mid.off)
    q = [hd(f"q_{x}", [P, NT], F32R) for x in ("hi", "lo")]
    qr = [hd(f"qr_{x}", [P, NT], F32R) for x in ("hi", "lo")]
    k = [hd(f"k_{x}", [P, NT], F32R) for x in ("hi", "lo")]
    v = [hd(f"v_{x}", [P, NT], F32R) for x in ("hi", "lo")]
    pt = [[hd(f"pt_{x}{s}", [P, NX], F32R) for s in range(4)] for x in ("hi", "lo")]
    prob = hd("prob", [P, XTOK, NT])
    probc = hd("probc", [P, 2, NC])
    qkt = hd("qkt", [P, TOK, QKW])
    rt = [hd(f"rt{s}", [P, TOK, ROPE]) for s in range(2)]
    assert hd.off >= lo_free
    cat_a = [hd(f"cat_a_{x}", [P, 4, NT], F32R) for x in ("hi", "lo")]
    ff = Place(sb.off)
    inner = [[ff(f"inner_{x}{b}", [P, 2, NT], F32R) for b in range(2)] for x in ("hi", "lo")]
    ff_v = ff("ff_v", [P, NT])
    assert ff.off <= mid.off

    ps_t = ctx.enter_context(nc.psum_tensor("ps", [P, 8, 512], F32))
    ps_all = ps_t[:].rearrange("p b n -> p (b n)")

    def sem(name):
        return ctx.enter_context(nc.semaphore(name))

    def sems(name, n=DEPTH):
        return [sem(f"{name}{i}") for i in range(n)]

    full, free = sems("psum_full", 4), sems("psum_free", 4)
    chunk_in = sems("chunk_in", 2)
    chunk_hi, chunk_lo, lat_used = sem("chunk_hi"), sem("chunk_lo"), sem("lat_used")
    hw_in, hw_hid, hw_lod = sem("hw_in"), sem("hw_hi_done"), sem("hw_lo_done")
    ada_in = sems("ada_in", 4)
    ada_first_in = sems("ada_first_in", 2 * ADA0)
    ada_op, mod_done = sem("ada_op"), sem("mod_done")
    vec_in, x_in, tab_in, csil_done = sem("vec_in"), sem("x_in"), sem("tab_in"), sem("csil_done")
    consts, poolw_zero, poolw_in, out_in = sem("consts"), sem("poolw_zero"), sem("poolw_in"), sem("out_in")
    sq_done, ss_done, scale_ok, rms_ok, t_done, h_hi, h_lo = (
        sems(n, 4) for n in ("sq_done", "ss_done", "scale_ok", "rms_ok", "t_done", "h_hi", "h_lo"))
    (lat_sq, lat_ms, lat_rt, lat_nm, lat_hi, kr_rot, tab_ok, win_st, win_ok, pdiff, cv, b_sq, b_ms, b_rt, b_rc, b_rot, b_hi, v_hi,
     s_max, s_rec, s_p, pt_hi, pv_used, ca_hi, cy_hi, cy_lo, ff_mid, ff_conv, ff_silu, ff_hi, ff_lo) = (
        sems(n) for n in ("lat_sq", "lat_ms", "lat_rt", "lat_nm", "lat_hi", "kr_rot", "tab_ok", "win_st", "win_ok",
                          "pdiff", "cv", "b_sq", "b_ms", "b_rt", "b_rc", "b_rot", "b_hi", "v_hi", "s_max", "s_rec", "s_p", "pt_hi",
                          "pv_used", "ca_hi", "cy_hi", "cy_lo", "ff_mid", "ff_conv", "ff_silu", "ff_hi", "ff_lo"))

    block = ctx.enter_context(nc.Block())

    ALL = [(0, 0, NX), (1, NX, NT)]

    def segs(L):
        return ALL if L == 0 else ALL[:1]

    def nsegs(nn):
        return ALL if nn < 3 else ALL[:1]

    def width(L):
        return NT if L == 0 else NX

    def qtok(L):
        return TOK if L == 0 else XTOK

    class Job:
        def __init__(self, n, i=0, per=0):
            self.slot, self.count, self.i, self.step = n % 4, n // 4, i, per // 4
            assert per % 4 == 0

        def times(self, extra):
            n = self.count + extra
            return n + self.i * self.step if self.step else n

        def ps(self, a=0, b=1024):
            return ps_all[:, self.slot * 1024 + a:self.slot * 1024 + b]

        def open(self, pe):
            if self.count:
                pe.wait_ge(free[self.slot], self.times(0))

        def filled(self, ins):
            ins.then_inc(full[self.slot], 1)

        def ready(self, eng):
            eng.wait_ge(full[self.slot], self.times(1))

        def last_read(self, ins):
            ins.then_inc(free[self.slot], 1)

        def taken(self, eng):
            eng.wait_ge(free[self.slot], self.times(1))

    def V(L, off, n=1):
        return vec[:, L * V_LAYER + off:L * V_LAYER + off + n]

    TJOBS = [[(0, 1), (2, 3), (4, 5), (6,)], [(0, 1), (2, 3), (4,), (5,)]]
    ENTRIES = [7, 6]
    LAT_SQ = [3 * qtok(L) + 2 * (TOK - qtok(L)) for L in range(DEPTH)]
    J_S, J_B, J_BT, J_T, J_PV, J_V, J_HEAD = (0, 1, 5, 6), 2, (7, 8, 10), (9, 11, 12, 14), 13, 15, 16
    J_LS = (0, 1, 2, 3)
    ROLES = ("pool", "gate_c", "conv_in", "gate_b")

    def spare_landed(eng):
        for n in range(4):
            eng.wait_ge(ada_in[n], 4 * ((DEPTH * ADB - ADA0) * KD + ADA_SPARE))

    def pieces(nn):
        halves = [ALL[0]] if nn % 2 else [(0, 0, NX // 2), (0, NX // 2, NX)]
        first = [(0, h) for h in halves] + [(1, ALL[0])]
        if nn == 3:
            return first + [(kk, ALL[0]) for kk in range(2, KD)]
        return first + [(0, ALL[1]), (1, ALL[1])] + [(kk, sg) for kk in range(2, KD) for sg in ALL]

    LAT_TURN = 6
    NORM_BREAK = 4

    ADA_WO = (range(8), range(0))
    ADA_UP = (((0, 1, 2), (3,)), ((4, 5), (6, 7)))

    @block.sync
    def _(sp):
        def load(c, i=0, per=0):
            if c >= 2:
                sp.wait_ge(chunk_lo, c - 1 + per * i if per else c - 1)
            src = dram["w_main"][c + per * i] if per else dram["w_main"][c]
            sp.dma_start(w_raw[c % 2][:], src).then_inc(chunk_in[c % 2], 16)

        def load_head(n):
            if n >= 1:
                sp.wait_ge(hw_lod, n)
            sp.dma_start(hw_raw[:], dram["w_head"][n]).then_inc(hw_in, 16)

        def load_ada(c, i=0, per=0):
            c -= ADA0 * KD
            if c >= 4:
                sp.wait_ge(ada_op, 2 * c - 6 + 2 * per * i if per else 2 * c - 6)
            n = c + ADA0 * KD
            src = dram["w_ada"][n + per * i] if per else dram["w_ada"][n]
            sp.dma_start(ada_raw[c % 4][:], src).then_inc(ada_in[c % 4], 16)

        def load_tables(L):
            for n in (0, 2):
                sp.dma_start(rtab[:, n:n + 2], dram["rope"]).then_inc(tab_in, 16)
            sp.dma_start(rgain[:], dram["rgain"][L].partition_broadcast(P)).then_inc(tab_in, 16)
            for g in range(4):
                p0 = 64 * (g % 2)
                sp.dma_start(poolw[p0:p0 + 64, g // 2, p0:p0 + 64], dram["pool_w"][L, g]).then_inc(poolw_in, 16)

        sp.dma_start(vec[:, 0:NV], dram["vec"]).then_inc(vec_in, 16)
        def load_first(n):
            b = ADA_FIRST[n]
            for kk in (0, KD // 2):
                src = dram["w_ada"][KD * b + kk:KD * b + kk + KD // 2].rearrange("k p n -> p k n")
                sp.dma_start(ada_first[b][:, kk:kk + KD // 2], src).then_inc(ada_first_in[2 * b + 2 * kk // KD], 16)
        load_first(0)
        sp.dma_start(X[:, :, 0:NX], dram["x"]).then_inc(x_in, 16)
        sp.dma_start(X[:, :, NX:NT], dram["ctx"]).then_inc(x_in, 16)
        load_first(1)
        load(0)
        load(1)
        load_first(2)
        load_first(3)
        load(2)
        load(3)
        load_head(0)
        for m in range(4):
            load_ada(ADA0 * KD + m)
        sp.wait_ge(poolw_zero, 1)
        load_tables(0)
        for L in range(DEPTH):
            c0 = NCH * L
            if L == 0:
                load(4)
                load(5)
            load_head(HEADS * L + 1)
            for j in range(4):
                load(c0 + 6 + j)
            if L == 0:
                for m in range(8):
                    load_ada(8 * 4 + m + 4)
            for j in range(8):
                if L == 0 and j in (2, 4, 6):
                    for m in range(8):
                        if 8 * (4 + j // 2) + m + 4 < 64:
                            load_ada(8 * (4 + j // 2) + m + 4)
                load(c0 + 10 + j)
            load_head(HEADS * L + 2)
            load_head(HEADS * L + 3)
            if L == 0:
                load_head(HEADS)
                Job(JOB["last", 0] + 3).ready(sp)
                for c in range(64, 68):
                    load_ada(c)
            with sp.Fori(0, 2) as i:
                for j in range(4):
                    if L == 0:
                        for m in ADA_WO[j % 2]:
                            load_ada(8 * (8 + j // 2) + m + 4, i, 16)
                    load(c0 + 18 + j, i, 4)
            if L == 0:
                for m in range(8):
                    load_ada(8 * 12 + m + 4)
            for j in range(4):
                if L == 0 and j == 0:
                    for m in range(8):
                        load_ada(8 * 13 + m + 4)
                load(c0 + 26 + j)
            if L == 0:
                b_rot_done = 3 * HEADS
                sp.wait_ge(b_rot[0], b_rot_done)
                load_tables(1)
            with sp.Fori(0, (FP - 1) // 2) as i:
                for d in range(2):
                    c = c0 + 30 + 6 * d
                    for t in range(2):
                        for x in range(2):
                            if L == 0:
                                for m in ADA_UP[t][x]:
                                    load_ada(8 * (14 + d) + m + 4, i, 16)
                            load(c + 2 * t + x, i, 12)
                    for x in range(2):
                        load(c + 4 + x, i, 12)
            if L == 0:
                for j in range(2):
                    load(c0 + NCH + 4 + j)
        for m in range(KD):
            Job(JOB["dlast", 1] + m).taken(sp)
            sp.dma_start(dram["out"][m], X[:, m, 0:NX]).then_inc(out_in, 16)
        sp.wait_ge(out_in, 16 * KD)
        for s in range(2):
            sp.wait_ge(chunk_in[s], 8 * (DEPTH * NCH + SPARE))

    @block.gpsimd
    def _(pool):
        pool.memset(poolw[:], 0.0).then_inc(poolw_zero, 1)
        pool.memset(ones[:], 1.0).then_inc(consts, 1)
        pool.memset(ident[:], 0.0).then_inc(consts, 1)
        pool.memset(lat_ss[:], 1.0).then_inc(consts, 1)
        pool.memset(head_sq[:], 1.0).then_inc(consts, 1)
        pool.wait_ge(consts, 4)
        pool.affine_select(out=ident[:], in_=ident[:], compare_op=ALU.not_equal, fill=1.0, base=0,
                           pattern=[[-1, P]], channel_multiplier=1).then_inc(consts, 1)

        def rotate(src, n, tab, done, before, scratch):
            def halves(x):
                return x.rearrange("p t (a h f) -> p t a h f", a=2, h=2)
            a, b = scratch[0][:, 0:n], scratch[1][:, 0:n]
            pool.tensor_tensor(a, src, rtab[:, tab, 0:n], ALU.mult).then_inc(done, 1)
            for h in range(2):
                for ax in range(2):
                    last = pool.tensor_tensor(halves(b)[:, :, ax, h], halves(src)[:, :, ax, 1 - h],
                                              halves(rtab[:, tab + 1, 0:n])[:, :, ax, h], ALU.mult)
            last.then_inc(done, 1)
            pool.wait_ge(done, before + 2)
            pool.tensor_tensor(src, a, b, ALU.add).then_inc(done, 1)

        for L in range(DEPTH):
            W = width(L) + (4 if L == 0 else 2) * PAD
            streams = [(PAD, NX)] + ([(NX + 3 * PAD, NC)] if L == 0 else [])
            st = 0

            def step(ins):
                nonlocal st
                st += 1
                ins.then_inc(win_st[L], 1)
            pool.wait_ge(h_lo[2 * L], len(pieces(2 * L)))
            for o, n in streams:
                pool.memset(win_p[:, o - PAD:o], 0.0)
                last = pool.memset(win_p[:, o + n:o + n + PAD], 0.0)
            step(last)
            for m in range(2):
                if m == 1:
                    pool.wait_ge(pdiff[L], 1)
                Job(JOB["a2", L][4 * m]).taken(pool)
                pool.wait_ge(win_st[L], st)
                if m == 0:
                    pool.tensor_tensor(win_r[0:64, 1:W], win_p[0:64, 0:W - 1], win_p[0:64, 1:W], ALU.add)
                    step(pool.tensor_tensor(win_a[64:P, 1:W], win_p[64:P, 0:W - 1], win_p[64:P, 1:W], ALU.add))
                    pool.wait_ge(win_st[L], st)
                    step(pool.tensor_tensor(win_r[64:P, 2:W - 1], win_a[64:P, 1:W - 2], win_a[64:P, 3:W], ALU.add))
                else:
                    step(pool.tensor_tensor(win_a[:, 1:W], win_p[:, 0:W - 1], win_p[:, 1:W], ALU.add))
                    pool.wait_ge(win_st[L], st)
                    step(pool.tensor_tensor(win_r[:, 2:W - 1], win_a[:, 1:W - 2], win_a[:, 3:W], ALU.add))
                    pool.wait_ge(win_st[L], st)
                    step(pool.tensor_tensor(win_a[:, 4:W - 3], win_r[:, 2:W - 5], win_r[:, 6:W - 1], ALU.add))
                    pool.wait_ge(win_st[L], st)
                    pool.tensor_copy(win_r[0:64, 8:W - 8], win_a[0:64, 8:W - 8])
                    step(pool.tensor_tensor(win_r[64:P, 8:W - 7], win_a[64:P, 4:W - 11], win_a[64:P, 12:W - 3],
                                            ALU.add))
                pool.wait_ge(win_st[L], st)
                for o, n in streams:
                    for e, c in ((0, o), (1, o + n - PAD)):
                        r = V_RATIO + 16 * m + 8 * e
                        last = pool.tensor_tensor(win_r[:, c:c + 8], win_r[:, c:c + 8], vec[:, r:r + 8], ALU.mult)
                last.then_inc(win_ok[L], 1)
            pool.wait_ge(pdiff[L], 2)
            pool.wait_ge(lat_nm[L], 3)
            pool.wait_ge(tab_ok[L], 5)
            scratch = [x[:, 0:TOK * ROPE].rearrange("p (t f) -> p t f", t=TOK) for x in (win_p, win_r)]
            rotate(latr[:, :, QR + KVR:LATW], TOK, 2, kr_rot[L], 0, scratch)

            def head_rope(j, i, per, h):
                Job(j, i, per).taken(pool)
                rotate(qkt[:, 0:qtok(L), NOPE:HQ], qtok(L), 0, b_rot[L], 3 * h, rt)
            head_rope(JOB["b0", L] + 2, 0, 0, 0)
            with pool.Fori(0, HEADS - 1) as h:
                head_rope(JOB["heads", L] + J_B + 2, h, J_HEAD, h + 1)

    @block.tensor
    def _(pe):
        def mm3(out, w, wsl, x, xsl, first, last):
            (wh, wl), (xh, xl) = w, x
            pe.matmul(out, wh[wsl], xh[xsl], start=first, stop=False)
            pe.matmul(out, wh[wsl], xl[xsl], start=False, stop=False)
            return pe.matmul(out, wl[wsl], xh[xsl], start=False, stop=last)

        def ada_rows(n):
            job, b = Job(JOB["ada"] + ADA_ROWS[n]), ADA_FIRST[n]
            job.open(pe)
            cs = csil[:].rearrange("p (s k) -> p k s", s=2)
            for kk in range(KD):
                if kk % (KD // 2) == 0:
                    pe.wait_ge(ada_first_in[2 * b + 2 * kk // KD], 16)
                last = pe.matmul(job.ps(0, ADC)[0:2], cs[:, kk], ada_first[b][:, kk], start=kk == 0,
                                 stop=kk == KD - 1)
            job.filled(last)

        def ada_turn(n):
            job = Job(JOB["ada"] + ADA_TURN[n])
            job.open(pe)
            Job(JOB["ada"] + ADA_ROWS[n]).taken(pe)
            for c in range(4):
                last = pe.transpose(job.ps(2 * c, 2 * c + 2), ada_acc[0:2, n % 2, P * c:P * (c + 1)],
                                    ident[0:2, 0:2])
            job.filled(last)

        def ada_reduce(job, b_op, acc=ada_acc, ns=2, o0=0):
            pe.wait_ge(ada_op, b_op - 2 * KD * ADA0)
            for s in range(ns):
                for c in range(4):
                    o = 768 + o0 + 4 * s + c
                    last = pe.matmul(job.ps(o, o + 1), acc[:, s, P * c:P * (c + 1)], ones[:, 0:1],
                                     start=True, stop=True)
            return last

        def norm_sum(nn, j):
            for sg, a, b in nsegs(nn):
                job = Job(j + sg)
                job.open(pe)
                pe.wait_ge(ss_done[nn], KD + 2)
                job.filled(pe.matmul(job.ps(a, b), ones[:], ss[:, a:b], start=True, stop=True))

        def part(job, sg, w, wc, x, xk, first, last):
            wsl = slice(wc, wc + P)
            for n, (ww, xx) in enumerate(((w[0], x[0]), (w[0], x[1]), (w[1], x[0]))):
                for _, a, b in sg:
                    ins = pe.matmul(job.ps(a, b), ww[:, wsl], xx[:, xk, a:b], start=first and n == 0,
                                    stop=last and n == 2)
            return ins

        def slot(c):
            return w_hi[c % 4], w_lo[c % 4]

        pe.wait_ge(consts, 5)
        pe.wait_ge(csil_done, 1)
        ada_rows(0)
        ada_rows(1)
        ada_turn(0)
        ada_rows(2)
        ada_turn(1)
        norm_sum(0, ADA_NORM)
        ada_rows(3)
        ada_turn(2)
        ada_turn(3)
        for L in range(DEPTH):
            sg, c0 = segs(L), NCH * L
            if L == 1:
                norm_sum(2 * L, JOB["norm1", L])
            jobs = [Job(JOB["lat", L] + j) for j in range(3)]
            for j in jobs:
                j.open(pe)
            for n, (kk, (sgn, ta, tb)) in enumerate(pieces(2 * L)):
                if sgn == 0 and kk % 2 == 0:
                    pe.wait_ge(chunk_lo, c0 + kk // 2 + 1)
                pe.wait_ge(h_lo[2 * L], n + 1)
                wo = (kk % 2) * LATW
                for t in range(ta // P, tb // P):
                    a = 0 if t < qtok(L) else QR
                    o = 512 * (t % 2)
                    last = mm3(jobs[t // 2].ps(o + a, o + LATW), H, (slice(None), kk, slice(P * t, P * (t + 1))),
                               slot(c0 + kk // 2), (slice(None), slice(wo + a, wo + LATW)), kk == 0, kk == KD - 1)
                    if kk == KD - 1 and t % 2 == 1:
                        jobs[t // 2].filled(last)
                if sgn == 1 and kk % 2 == 1 and kk < KD - 1:
                    last.then_inc(lat_used, 1)
            def lat_turn(job, a, b, nt):
                job.open(pe)
                for t in range(nt):
                    last = pe.transpose(job.ps(P * t, P * (t + 1))[0:b - a], latr[:, t, a:b], ident[:])
                job.filled(last)

            for j in range(8):
                if j == LAT_TURN:
                    pe.wait_ge(lat_nm[L], 3)
                    for n, nt in enumerate((qtok(L), qtok(L), TOK)):
                        lat_turn(Job(JOB["latT", L] + n), P * n, P * (n + 1), nt)
                job, c = Job(JOB["a2", L][j]), c0 + C_A2 + j
                pe.wait_ge(chunk_lo, c + 1)
                job.open(pe)
                for kk in range(KD):
                    last = part(job, sg, slot(c), P * kk, H, kk, kk == 0, kk == KD - 1)
                if L == 0 and j % 2 == 1:
                    last = ada_reduce(job, 16 * (5 + j // 2))
                job.filled(last)

            def pool_project(m):
                pe.wait_ge(poolw_in, 64 * (L + 1))
                job = Job(JOB["pool", L][m])
                job.open(pe)
                pe.wait_ge(pdiff[L], m + 1)
                for _, a, b in sg:
                    last = pe.matmul(job.ps(a, b), poolw[:, m], ymix[m][:, a:b], start=True, stop=True)
                job.filled(last)

            def b_tokens(j0, i, per, h):
                pe.wait_ge(hw_lod, HEADS * L + 1 + h)
                for j in range(3):
                    job = Job(j0 + j, i, per)
                    job.open(pe)
                    for t in (2 * j, 2 * j + 1):
                        o, tsl = 512 * (t % 2), slice(P * t, P * (t + 1))
                        for kk in range(2 if t < qtok(L) else 0):
                            mm3(job.ps(o, o + HQ), ql, (slice(None), kk, tsl), (hw_hi, hw_lo),
                                (slice(None), slice(HQ * kk, HQ * (kk + 1))), kk == 0, kk == 1)
                        last = mm3(job.ps(o + HQ, o + QKW), kvl, (slice(None), tsl), (hw_hi, hw_lo),
                                   (slice(None), slice(2 * HQ, 2 * HQ + NOPE)), True, True)
                    job.filled(last)

            def b_turn(n, j0, jt, i, per, h):
                a, b, nt = ((0, NOPE, qtok(L)), (HQ, QKW, TOK), (NOPE, NOPE + P, qtok(L)))[n]
                job = Job(jt, i, per)
                job.open(pe)
                if n == 0:
                    Job(j0 + 2, i, per).taken(pe)
                if n == 2:
                    pe.wait_ge(b_rot[L], 3 * h + 3)
                for t in range(nt):
                    last = pe.transpose(job.ps(P * t, P * (t + 1)), qkt[:, t, a:b], ident[:])
                job.filled(last)

            def b_v(j, i, per):
                job = Job(j, i, per)
                job.open(pe)
                for t in range(TOK):
                    last = mm3(job.ps(P * t, P * (t + 1)), kvl, (slice(None), slice(P * t, P * (t + 1))),
                               (hw_hi, hw_lo), (slice(None), slice(2 * HQ + NOPE, HWC)), True, True)
                job.filled(last)

            def score(t, j, i, per):
                job = Job(j, i, per)
                job.open(pe)
                parts = [(t, 0, NX, 0), (t, NX, NT, NX)]
                if L == 0 and t < 2:
                    parts.append((XTOK + t, NX, NT, NT))
                for qt, ka, kb, o in parts:
                    qs = slice(P * qt, P * (qt + 1))
                    mm3(job.ps(o, o + kb - ka), q, (slice(None), qs), k, (slice(None), slice(ka, kb)), True, False)
                    last = mm3(job.ps(o, o + kb - ka), qr, (slice(0, ROPE), qs), kr,
                               (slice(0, ROPE), slice(ka, kb)), False, True)
                job.filled(last)

            def attend(js, jpv, i, per, h, between=None):
                pv = Job(jpv, i, per)

                def turn(n):
                    job = Job(js[n], i, per)
                    job.open(pe)
                    for t in range(XTOK):
                        if n == 0:
                            pe.wait_ge(s_p[L], 4 * h + (t + 1))
                        for m, e in enumerate(TJOBS[L][n]):
                            if e < 6:
                                o = 512 * m + P * t
                                last = pe.transpose(job.ps(o, o + P), prob[:, t, P * e:P * (e + 1)], ident[:])
                    for m, e in enumerate(TJOBS[L][n]):
                        if e == 6:
                            for kt in range(2):
                                for t in range(2):
                                    o = NC * kt + P * t
                                    last = pe.transpose(job.ps(o, o + P), probc[:, t, P * kt:P * (kt + 1)], ident[:])
                    job.filled(last)

                def values(n):
                    Job(js[n], i, per).taken(pe)
                    for e in TJOBS[L][n]:
                        if e == 0:
                            pv.open(pe)
                        p = (pt[0][e % 4], pt[1][e % 4])
                        if e < 6:
                            last = mm3(pv.ps(0, NX), v, (slice(None), slice(P * e, P * (e + 1))), p,
                                       (slice(None), slice(0, NX)), e == 0, e == 5)
                        else:
                            for kt in range(2):
                                last = mm3(pv.ps(NX, NT), v, (slice(None), slice(P * (4 + kt), P * (5 + kt))), p,
                                           (slice(None), slice(NC * kt, NC * (kt + 1))), kt == 0, kt == 1)
                        if e < ENTRIES[L] - 1:
                            last.then_inc(pv_used[L], 1)
                        else:
                            pv.filled(last)
                turn(0)
                if between:
                    between()
                turn(1)
                values(0)
                turn(2)
                values(1)
                turn(3)
                values(2)
                values(3)

            b0, b0t = JOB["b0", L], JOB["b0T", L]
            Job(JOB["latT", L] + 2).taken(pe)
            b_tokens(b0, 0, 0, 0)
            pool_project(0)
            pe.wait_ge(kr_rot[L], 3)
            lat_turn(Job(JOB["krT", L]), QR + KVR, LATW, TOK)
            pool_project(1)
            for n in range(3):
                b_turn(n, b0, b0t + n, 0, 0, 0)
            b_v(JOB["v0", L], 0, 0)
            Job(b0t + 2).taken(pe)
            j0 = JOB["heads", L]
            with pe.Fori(0, HEADS - 1) as h:
                for t in range(2):
                    score(t, j0 + J_S[t], h, J_HEAD)
                b_tokens(j0 + J_B, h, J_HEAD, h + 1)
                for t in range(2, XTOK):
                    score(t, j0 + J_S[t], h, J_HEAD)
                for n in range(2):
                    b_turn(n, j0 + J_B, j0 + J_BT[n], h, J_HEAD, h + 1)
                attend([j0 + x for x in J_T], j0 + J_PV, h, J_HEAD, h,
                       lambda: b_turn(2, j0 + J_B, j0 + J_BT[2], h, J_HEAD, h + 1))
                b_v(j0 + J_V, h, J_HEAD)
                Job(j0 + J_BT[2], h, J_HEAD).taken(pe)
            j0 = JOB["last", L]
            for t in range(XTOK):
                score(t, j0 + J_LS[t], 0, 0)
            attend([j0 + 4, j0 + 5, j0 + 7, j0 + 8], j0 + 6, 0, 0, HEADS - 1)
            pe.wait_ge(cy_lo[L], 4)
            with pe.Fori(0, 2) as i:
                for j in range(4):
                    job = Job(JOB["wo", L] + j, i, 4)
                    c = c0 + C_WO + j
                    pe.wait_ge(chunk_lo, c + 1 + 4 * i)
                    job.open(pe)
                    for n, kk in enumerate((4, 5, 6, 7, 0, 1, 2, 3)):
                        if j == 0 and n == 4:
                            Job(JOB["last", L] + 6).taken(pe)
                        last = part(job, sg, slot(c), P * kk, cat_a if kk < 4 else cat_y, kk % 4, n == 0, n == 7)
                    if L == 0 and j % 2 == 1:
                        last = ada_reduce(job, 16 * (9 + j // 2) + 32 * i)
                    job.filled(last)
            norm_sum(2 * L + 1, JOB["norm2", L])

            def up_first(jn, c):
                jobs = [Job(jn + n) for n in range(4)]
                for j in jobs:
                    j.open(pe)
                pe.wait_ge(chunk_lo, c + 4)
                work = pieces(2 * L + 1)
                for m, (kk, stream) in enumerate(work):
                    if kk < KD // 2:
                        pe.wait_ge(h_lo[2 * L + 1], m + 1)
                        for n in range(4):
                            part(jobs[n], [stream], slot(c + n), P * kk, H, kk, kk == 0, False)
                for n in range(4):
                    for m, (kk, stream) in enumerate(work):
                        if kk >= KD // 2:
                            if n == 0:
                                pe.wait_ge(h_lo[2 * L + 1], m + 1)
                            last = part(jobs[n], [stream], slot(c + n), P * kk, H, kk, False, kk == KD - 1)
                    if L == 0 and n == 3:
                        ada_reduce(jobs[n], 16 * 14, ada_acc, 1)
                        last = ada_reduce(jobs[n], 16 * 14, ada_acc2, 1, 4)
                    jobs[n].filled(last)

            def up(jn, c, i):
                for n in range(4):
                    job = Job(jn + n, i, 24)
                    pe.wait_ge(chunk_lo, c + n + 1 + 12 * i)
                    job.open(pe)
                    for kk in range(KD):
                        last = part(job, sg, slot(c + n), P * kk, H, kk, kk == 0, kk == KD - 1)
                    job.filled(last)

            def down(jn, c, p, buf, i, per_j, per_c, ada=None, ns=0):
                pe.wait_ge(ff_lo[L], 2 * p + 2)
                pe.wait_ge(chunk_lo, c + 2 + per_c * i if per_c else c + 2)
                x = (inner[0][buf], inner[1][buf])
                for m in range(KD):
                    job = Job(jn + m, i, per_j)
                    job.open(pe)
                    for kk in range(2):
                        last = part(job, sg, slot(c + kk), P * m, x, kk, kk == 0, kk == 1)
                    if ada is not None and m == KD - 1:
                        last = ada_reduce(job, ada, ada_acc, ns)
                    job.filled(last)

            up_first(JOB["u0", L], c0 + C_FF)
            jf = JOB["ff", L]
            with pe.Fori(0, (FP - 1) // 2) as i:
                for d in range(2):
                    c = c0 + C_FF + 4 + 6 * d
                    up(jf + 12 * d, c, i)
                    down(jf + 12 * d + 4, c + 4, 2 * i + d, d, i, 24, 12, 16 * (15 + d) + 32 * i if L == 0 else None, 2 - d)
            down(JOB["dlast", L], c0 + NCH - 2, FP - 1, 0, 0, 0, 0)

    @block.scalar
    def _(act):
        def split_hi(c, user=None, i=0, per=0):
            if user is not None:
                user.ready(act)
            n = 16 * (c // 2 + 1)
            act.wait_ge(chunk_in[c % 2], n + 8 * per * i if per else n)
            act.activation(w_hi[c % 4][:], w_raw[c % 2][:], ACT.Copy).then_inc(chunk_hi, 1)

        def head_hi(n):
            act.wait_ge(hw_in, 16 * n + 16)
            act.activation(hw_hi[:], hw_raw[:], ACT.Copy).then_inc(hw_hid, 1)

        def square(nn, m, par, job=None):
            w = NT if nn < 3 else NX
            if job is not None:
                job.taken(act)
            act.wait_ge(ss_done[nn], m + 1)
            act.activation(tmp[par][:, 0:w], X[:, m, 0:w], ACT.Square).then_inc(sq_done[nn], 1)

        def norm_roots(nn, j):
            act.activation(warm[:, 0:1], ones[:, 0:1], ACT.Sqrt)
            for sg, a, b in nsegs(nn):
                job = Job(j + sg)
                job.ready(act)
                job.last_read(act.activation(ss[:, a:b], job.ps(a, b), ACT.Sqrt, bias=vec[:, V_EPS:V_EPS + 1],
                                             scale=1.0 / D))

        def norm(nn, between=None):
            L, which = nn // 2, nn % 2
            for n, (kk, (sg, a, b)) in enumerate(pieces(nn)):
                act.wait_ge(t_done[nn], n + 1)
                m = 24 * which + kk
                act.activation(H[0][:, kk, a:b], tmp[kk % 2][:, a:b], ACT.Identity,
                               bias=mod[L][:, sg, m:m + 1]).then_inc(h_hi[nn], 1)
                if n == NORM_BREAK and between:
                    between()

        act.wait_ge(vec_in, 16)
        act.activation(csil[:], vec[:, V_C:V_C + 16], ACT.Silu).then_inc(csil_done, 1)
        act.wait_ge(x_in, 32)
        for m in range(KD):
            square(0, m, m % 2)
        for c in range(2):
            split_hi(c)
        for n in range(ADA0):
            if n == 3:
                norm_roots(0, ADA_NORM)
            if n >= 2:
                Job(JOB["ada"] + ADA_TURN[n - 2]).ready(act)
            job = Job(JOB["ada"] + ADA_ROWS[n])
            job.ready(act)
            job.last_read(act.activation(ada_acc[0:2, n % 2], job.ps(0, ADC)[0:2], ACT.Copy))
        for L in range(DEPTH):
            c0, w = NCH * L, width(L)
            if L == 0:
                def between():
                    split_hi(2)
                    split_hi(3)
                norm(0, between)
                head_hi(0)
            else:
                norm_roots(2, JOB["norm1", 1])
                norm(2)
            for j in range(4):
                if j < 3:
                    act.wait_ge(lat_used, 3 * L + j + 1)
                split_hi(c0 + 4 + j, Job(JOB["lat", L] + 2) if j == 3 else None)
            n = 0
            for t in range(TOK):
                if t % 2 == 0:
                    Job(JOB["lat", L] + t // 2).taken(act)
                for g, (a, b) in enumerate(((0, QR), (QR, QR + KVR), (QR + KVR, LATW))):
                    if g > 0 or t < qtok(L):
                        if n:
                            act.wait_ge(lat_sq[L], n)
                        act.activation(tmp[1][:, 0:b - a], latr[:, t, a:b], ACT.Square,
                                       accum_out=lat_ss[:, g, t:t + 1]).then_inc(lat_sq[L], 1)
                        n += 1
            assert n == LAT_SQ[L]
            act.wait_ge(lat_ms[L], 4)
            act.activation(lat_ss[:], lat_ss[:], ACT.Sqrt).then_inc(lat_rt[L], 1)
            for j in range(8):
                job = Job(JOB["a2", L][j])
                if j % 4 == 0:
                    pdone = j // 4
                    if pdone:
                        act.wait_ge(pdiff[L], 1)
                    job.ready(act)
                    for s, a, b in segs(L):
                        o = PAD + a + 2 * PAD * s
                        last = act.activation(win_p[:, o:o + b - a], job.ps(a, b), ACT.Copy)
                    job.last_read(last)
                split_hi(c0 + 8 + j, job)
                if j == LAT_TURN - 1:
                    for n in range(3):
                        job = Job(JOB["latT", L] + n)
                        job.ready(act)
                        if n < 2:
                            ins = act.activation(ql[0][:, n, 0:w], job.ps(0, w), ACT.Copy, scale=V(L, V_QC + n))
                        else:
                            ins = act.activation(kvl[0][:], job.ps(0, NT), ACT.Copy, scale=V(L, V_KVC))
                        ins.then_inc(lat_hi[L], 1)

            def pool_out(m):
                job = Job(JOB["pool", L][m])
                job.ready(act)
                job.last_read(act.activation(ymix[m][:, 0:w], job.ps(0, w), ACT.Copy, scale=V(L, V_PS + m)))

            def b_stats(j0, i, per, h):
                for j in range(3):
                    job = Job(j0 + j, i, per)
                    job.ready(act)
                    a = 0 if 2 * j < qtok(L) else HQ
                    src = job.ps().rearrange("p (t c) -> p t c", t=2)[:, :, a:QKW]
                    act.activation(qkt[:, 2 * j:2 * j + 2, a:QKW], src, ACT.Square).then_inc(b_sq[L], 1)
                    if j:
                        n, t0, t1 = (None, (1, 0, 4), (2, 4, 6))[j]
                        act.wait_ge(b_ms[L], 5 * h + (3, 5)[n - 1])
                        eps = vec[:, V_EPS:V_EPS + 1]
                        act.activation(head_ss[:, 0:2, t0:t1], head_ss[:, 0:2, t0:t1], ACT.Sqrt, bias=eps,
                                       scale=1.0 / NOPE)
                        act.activation(head_ss[:, 2, t0:t1], head_sq[:, t0:t1, 2], ACT.Sqrt, bias=eps,
                                       scale=1.0 / ROPE).then_inc(b_rt[L], 1)

            def b_half(n, j, i, per):
                job = Job(j, i, per)
                job.ready(act)
                dst, rows, wn = ((q, P, w), (k, P, NT), (qr, ROPE, w))[n]
                kw = ({"scale": qg[:, 0:1]}, {"scale": V(L, V_KN)}, {})[n]
                act.activation(dst[0][0:rows, 0:wn], job.ps(0, wn)[0:rows], ACT.Copy, **kw).then_inc(b_hi[L], 1)

            def v_half(j, i, per):
                job = Job(j, i, per)
                job.ready(act)
                act.activation(v[0][:], job.ps(0, NT), ACT.Copy).then_inc(v_hi[L], 1)

            def exponentials(t, j, i, per, h):
                job = Job(j, i, per)
                act.wait_ge(s_max[L], 4 * h + (t + 1))
                ins = act.activation(prob[:, t], job.ps(0, NT), ACT.Exp, bias=nmax[:, t:t + 1],
                                     accum_out=rsum[:, t:t + 1])
                if L == 0 and t < 2:
                    ins = act.activation(probc[:, t], job.ps(NT, 1024), ACT.Exp, bias=nmax[:, 4 + t:5 + t],
                                         accum_out=rsum[:, 4 + t:5 + t])
                job.last_read(ins)

            def attend(js, i, per, h, extras, extra):
                for n in range(4):
                    job = Job(js[n], i, per)
                    job.ready(act)
                    for m, e in enumerate(TJOBS[L][n]):
                        if e >= 4:
                            act.wait_ge(pv_used[L], (ENTRIES[L] - 1) * h + (e - 3))
                        act.activation(pt[0][e % 4][:], job.ps(512 * m, 512 * (m + 1)),
                                       ACT.Copy).then_inc(pt_hi[L], 1)
                    if n < extras:
                        extra(n)

            def attended(jpv, i, per, h):
                job = Job(jpv, i, per)
                job.ready(act)
                act.activation(cat_a[0][:, h, 0:w], job.ps(0, w), ACT.Copy).then_inc(ca_hi[L], 1)

            b0 = JOB["b0", L]
            if L == 1:
                spare_landed(act)
            b_stats(b0, 0, 0, 0)
            pool_out(0)
            job = Job(JOB["krT", L])
            job.ready(act)
            act.activation(kr[0][0:ROPE], job.ps(0, NT)[0:ROPE], ACT.Copy).then_inc(lat_hi[L], 1)
            pool_out(1)
            for n in range(3):
                b_half(n, JOB["b0T", L] + n, 0, 0)
            j0 = JOB["heads", L]
            with act.Fori(0, HEADS - 1) as h:
                act.activation(warm[:, 0:1], ones[:, 0:1], ACT.Exp)
                Job(JOB["v0", L], h, J_HEAD).ready(act)
                head_hi(h + (HEADS * L + 1))
                v_half(JOB["v0", L], h, J_HEAD)
                for t in range(2):
                    exponentials(t, j0 + J_S[t], h, J_HEAD, h)
                b_stats(j0 + J_B, h, J_HEAD, h + 1)
                for t in range(2, XTOK):
                    exponentials(t, j0 + J_S[t], h, J_HEAD, h)
                for n in range(2):
                    b_half(n, j0 + J_BT[n], h, J_HEAD)
                attend([j0 + x for x in J_T], h, J_HEAD, h, 1,
                       lambda n: b_half(2, j0 + J_BT[2], h, J_HEAD))
                attended(j0 + J_PV, h, J_HEAD, h)
            v_half(JOB["last", L] - 1, 0, 0)
            if L == 0:
                head_hi(HEADS)
            j0 = JOB["last", L]
            for t in range(XTOK):
                exponentials(t, j0 + J_LS[t], 0, 0, HEADS - 1)
            Job(JOB["a2", L][7]).taken(act)
            Job(JOB["pool", L][1]).taken(act)

            def mix_hi(j):
                act.activation(cat_y[0][:, j, 0:w], ymix[j][:, 0:w], ACT.Copy).then_inc(cy_hi[L], 1)
            attend([j0 + 4, j0 + 5, j0 + 7, j0 + 8], 0, 0, HEADS - 1, 4, mix_hi)
            attended(j0 + 6, 0, 0, HEADS - 1)
            with act.Fori(0, 2) as i:
                for j in range(4):
                    job = Job(JOB["wo", L] + j, i, 4)
                    split_hi(c0 + 16 + j, job, i, 4)
                    square(2 * L + 1, 4 * i + j, j % 2, job)
            norm_roots(2 * L + 1, JOB["norm2", L])
            norm(2 * L + 1)

            def ff_tile(t, jn, c, par, buf, i, per_j, per_c):
                g, u = Job(jn, i, per_j), Job(jn + 1, i, per_j)
                g.ready(act)
                tap = vec[:, bass.ds(L * V_LAYER + V_FC + FT + t, 1)]
                act.activation(tmp[par][:, 0:w], g.ps(0, w), ACT.Copy, scale=tap).then_inc(ff_mid[L], 1)
                split_hi(c, g, i, per_c)
                g.taken(act)
                act.activation(tmp[par][:, 0:w], tmp[par][:, 0:w], ACT.Silu).then_inc(ff_silu[L], 1)
                split_hi(c + 1, u, i, per_c)
                u.taken(act)
                act.activation(inner[0][buf][:, par, 0:w], ff_v[:, 0:w], ACT.Copy).then_inc(ff_hi[L], 1)

            for t in range(2):
                ff_tile(t, JOB["u0", L] + 2 * t, c0 + C_FF + 4 + 2 * t, t, 0, 0, 0, 0)
            jf = JOB["ff", L]
            with act.Fori(0, (FP - 1) // 2) as i:
                for d in range(2):
                    c = c0 + C_FF + 4 + 6 * d
                    for t in range(2):
                        ff_tile(4 * i + (2 * (d + 1) + t), jf + 12 * d + 2 * t, c + 4 + 2 * t, t, 1 - d, i, 24, 12)
                    for x in range(2):
                        split_hi(c + 8 + x, Job(jf + 12 * d + 11, i, 24), i, 12)
            if L == 0:
                for m in range(KD):
                    square(2, m, m % 2, Job(JOB["dlast", 0] + m))
                for x in range(2):
                    split_hi(c0 + NCH + 2 + x, Job(JOB["dlast", 0] + 7))

    @block.vector
    def _(dve):
        def split_lo(c, i=0, per=0):
            dve.wait_ge(chunk_hi, c + 1 + per * i if per else c + 1)
            dve.tensor_tensor(w_lo[c % 4][:], w_raw[c % 2][:], w_hi[c % 4][:].bitcast(F32),
                              ALU.subtract).then_inc(chunk_lo, 1)

        def head_lo(n):
            dve.wait_ge(hw_hid, n + 1)
            dve.tensor_tensor(hw_lo[:], hw_raw[:], hw_hi[:].bitcast(F32), ALU.subtract).then_inc(hw_lod, 1)

        def ada_chunks(b, ks, i=0, per=0, acc=ada_acc, ns=2):
            for kk in ks:
                c = 8 * (b - ADA0) + kk
                n = 16 * (c // 4 + 1)
                dve.wait_ge(ada_in[c % 4], n + 32 * per * i if per else n)
                for s in range(ns):
                    cs = csil[:, 8 * s + kk:8 * s + kk + 1]
                    if kk == 0:
                        ins = dve.tensor_scalar(acc[:, s], ada_raw[c % 4][:], cs, None, ALU.mult)
                    else:
                        done = 2 * c + s - (ns - 1)
                        dve.wait_ge(ada_op, done + 16 * per * i if per else done)
                        ins = dve.scalar_tensor_tensor(acc[:, s], ada_raw[c % 4][:], cs, acc[:, s],
                                                       ALU.mult, ALU.add)
                    ins.then_inc(ada_op, 2 // ns)

        def ada_pair(b):
            for n in range(2 * KD):
                c, kk, acc = KD * (b - ADA0) + n, n // 2, (ada_acc, ada_acc2)[n % 2][:, 0]
                dve.wait_ge(ada_in[c % 4], 16 * (c // 4 + 1))
                if kk == 0:
                    ins = dve.tensor_scalar(acc, ada_raw[c % 4][:], csil[:, 0:1], None, ALU.mult)
                else:
                    dve.wait_ge(ada_op, 2 * c - 2)
                    ins = dve.scalar_tensor_tensor(acc, ada_raw[c % 4][:], csil[:, kk:kk + 1], acc, ALU.mult, ALU.add)
                ins.then_inc(ada_op, 2)

        def ada_out(L, b, job, ns=2):
            bias = vec[:, bass.ds(L * V_LAYER + V_ADAB + 4 * b, 4)].unsqueeze(1).to_broadcast([P, ns, 4])
            return dve.tensor_tensor(mod[L][:, 0:ns, bass.ds(4 * b, 4)],
                                     job.ps(768, 768 + 4 * ns).rearrange("p (s c) -> p s c", s=ns), bias, ALU.add)

        def clear_ss(nn):
            dve.memset(ss[:, 0:NT if nn < 3 else NX], 0.0).then_inc(ss_done[nn], 2)

        def add_squares(nn, m, par):
            w = NT if nn < 3 else NX
            dve.wait_ge(sq_done[nn], m + 1)
            dve.wait_ge(ss_done[nn], m + 2)
            dve.tensor_tensor(ss[:, 0:w], ss[:, 0:w], tmp[par][:, 0:w], ALU.add).then_inc(ss_done[nn], 1)

        def norm_inverse(nn, j, sg, a, b):
            Job(j + sg).taken(dve)
            dve.reciprocal(ss[:, a:b], ss[:, a:b]).then_inc(rms_ok[nn], 1)

        def norm(nn, j=None, between=None):
            L, which = nn // 2, nn % 2
            if nn == 0:
                Job(JOB["ada"] + ADA_TURN[ADA0 - 1]).taken(dve)
            else:
                dve.wait_ge(mod_done, ADB - 6 if L == 0 else 2 * ADB - 4)
            ns = len(nsegs(nn))
            g = V(L, V_N1 if which == 0 else V_N2, 8).unsqueeze(1).to_broadcast([P, ns, 8])
            dve.scalar_tensor_tensor(amul[:, 0:ns], mod[L][:, 0:ns, 24 * which + 8:24 * which + 16], 1.0, g, ALU.add,
                                     ALU.mult).then_inc(scale_ok[nn], 1)
            dve.wait_ge(scale_ok[nn], 1)
            work = pieces(nn)

            def scaled(n):
                kk, (sg, a, b) = work[n]
                if j is not None and kk == 0:
                    norm_inverse(nn, j, sg, a, b)
                if kk < 2:
                    dve.wait_ge(rms_ok[nn], sum(p[0] == 0 for p in work[:n + 1]))
                if n >= 2:
                    dve.wait_ge(h_lo[nn], n - 1)
                dve.scalar_tensor_tensor(tmp[kk % 2][:, a:b], X[:, kk, a:b], amul[:, sg, kk:kk + 1], ss[:, a:b],
                                         ALU.mult, ALU.mult).then_inc(t_done[nn], 1)
            scaled(0)
            for n, (kk, (sg, a, b)) in enumerate(work):
                if n + 1 < len(work):
                    scaled(n + 1)
                dve.wait_ge(h_hi[nn], n + 1)
                m = 24 * which + kk
                dve.scalar_tensor_tensor(H[1][:, kk, a:b], tmp[kk % 2][:, a:b], mod[L][:, sg, m:m + 1],
                                         H[0][:, kk, a:b].bitcast(F32), ALU.add, ALU.subtract).then_inc(h_lo[nn], 1)
                if n == NORM_BREAK and between:
                    between()

        def lo_half(dst, src, hi, scale=None):
            if scale is None:
                return dve.tensor_tensor(dst, src, hi.bitcast(F32), ALU.subtract)
            return dve.scalar_tensor_tensor(dst, src, scale, hi.bitcast(F32), ALU.mult, ALU.subtract)

        def update_x(m, L, job, gate, loop=False):
            for s, a, b in segs(L):
                xo = X[:, m, a:b]
                last = dve.scalar_tensor_tensor(xo, job.ps(a, b), mod[L][:, s, bass.ds(gate + m, 1)], xo,
                                                ALU.mult, ALU.add)
            job.last_read(last)

        clear_ss(0)
        dve.wait_ge(vec_in, 16)
        dve.wait_ge(csil_done, 1)
        for m in range(KD):
            add_squares(0, m, m % 2)
        for c in range(2):
            split_lo(c)
        for n, b in enumerate(ADA_FIRST):
            if n == 2:
                for kk, part in pieces(0):
                    if kk == 0:
                        norm_inverse(0, ADA_NORM, *part)
            job = Job(JOB["ada"] + ADA_TURN[n])
            job.ready(dve)
            bias = V(0, V_ADAB + 4 * b, 4).unsqueeze(1).to_broadcast([P, 2, 4])
            job.last_read(dve.tensor_tensor(mod[0][:, :, 4 * b:4 * b + 4],
                                            job.ps(0, 8).rearrange("p (c s) -> p s c", s=2), bias, ALU.add))
        for L in range(DEPTH):
            c0, w, sg = NCH * L, width(L), segs(L)
            if L == 0:
                def between():
                    split_lo(2)
                    split_lo(3)
                norm(0, None, between)
                head_lo(0)
            else:
                norm(2, JOB["norm1", 1])
            for j in range(4):
                split_lo(c0 + 4 + j)
            dve.wait_ge(tab_in, 48 * (L + 1))
            for n in range(4):
                gb = rgain[:, n:n + 1].to_broadcast([P, TOK, ROPE])
                dve.scalar_tensor_tensor(rtab[:, n], rtab[:, n], SCALE if n < 2 else 1.0, gb, ALU.mult,
                                         ALU.mult).then_inc(tab_ok[L], 1)
            dve.tensor_scalar(qg[:, 0:1], V(L, V_QN), SCALE, None, ALU.mult).then_inc(tab_ok[L], 1)
            for j in range(3):
                job = Job(JOB["lat", L] + j)
                job.ready(dve)
                a = 0 if 2 * j < qtok(L) else QR
                src = job.ps().rearrange("p (t c) -> p t c", t=2)[:, :, a:LATW]
                job.last_read(dve.tensor_copy(latr[:, 2 * j:2 * j + 2, a:LATW], src))
            if L == 0:
                ada_chunks(4, range(8))
            dve.wait_ge(lat_sq[L], LAT_SQ[L])
            for g, n in enumerate((QR, KVR, ROPE)):
                dve.tensor_scalar(lat_ss[:, g], lat_ss[:, g], 1.0 / n, EPS, ALU.mult, ALU.add).then_inc(lat_ms[L], 1)
            dve.wait_ge(lat_ms[L], 3)
            dve.reciprocal(lat_ss[:], lat_ss[:]).then_inc(lat_ms[L], 1)
            dve.wait_ge(lat_rt[L], 1)
            for g, (a, b) in enumerate(((0, QR), (QR, QR + KVR), (QR + KVR, LATW))):
                nt = TOK if g > 0 else qtok(L)
                r = lat_ss[:, g, 0:nt].unsqueeze(2).to_broadcast([P, nt, b - a])
                dve.tensor_tensor(latr[:, 0:nt, a:b], latr[:, 0:nt, a:b], r, ALU.mult).then_inc(lat_nm[L], 1)
            ncv = 1 + 2 * len(sg)
            for j in range(8):
                job, m, role = Job(JOB["a2", L][j]), j // 4, ROLES[j % 4]
                y = ymix[2 + m]
                if L == 0 and j in (2, 4, 6):
                    ada_chunks(4 + j // 2, range(8))
                if role != "pool":
                    job.ready(dve)
                if L == 0 and j % 2 == 1:
                    ada_out(0, 4 + j // 2, job).then_inc(mod_done, 1)
                if role == "gate_c":
                    job.last_read(dve.tensor_copy(tmp[0][:, 0:w], job.ps(0, w)))
                elif role == "conv_in":
                    Job(JOB["a2", L][j - 1]).taken(dve)
                    job.last_read(dve.tensor_tensor(tmp[1][:, 0:w], tmp[0][:, 0:w], job.ps(0, w), ALU.mult))
                    job.taken(dve)
                    dve.tensor_scalar(y[:, 0:w], tmp[1][:, 0:w], V(L, V_SC + 3 * m + 1), None,
                                      ALU.mult).then_inc(cv[L], 1)
                    n = ncv * m + 1
                    for tap, d0, s0 in ((0, 1, 0), (2, 0, 1)):
                        for _, a, b in sg:
                            dve.wait_ge(cv[L], n)
                            yo = y[:, a + d0:b - 1 + d0]
                            dve.scalar_tensor_tensor(yo, tmp[1][:, a + s0:b - 1 + s0], V(L, V_SC + 3 * m + tap), yo,
                                                     ALU.mult, ALU.add).then_inc(cv[L], 1)
                            n += 1
                elif role == "gate_b":
                    dve.wait_ge(cv[L], ncv * (m + 1))
                    job.last_read(dve.tensor_tensor(y[:, 0:w], y[:, 0:w], job.ps(0, w), ALU.mult))
                    dve.wait_ge(win_ok[L], m + 1)
                    for s, a, b in sg:
                        o = PAD + a + 2 * PAD * s
                        last = dve.scalar_tensor_tensor(ymix[m][:, a:b], win_r[:, o:o + b - a],
                                                        vec[:, V_INVW + m:V_INVW + m + 1], win_p[:, o:o + b - a],
                                                        ALU.mult, ALU.subtract)
                    last.then_inc(pdiff[L], 1)
                split_lo(c0 + 8 + j)
                if j == LAT_TURN - 1:
                    for n in range(3):
                        job = Job(JOB["latT", L] + n)
                        dve.wait_ge(lat_hi[L], n + 1)
                        if n < 2:
                            ins = lo_half(ql[1][:, n, 0:w], job.ps(0, w), ql[0][:, n, 0:w], V(L, V_QC + n))
                        else:
                            ins = lo_half(kvl[1][:], job.ps(0, NT), kvl[0][:], V(L, V_KVC))
                        job.last_read(ins)

            def b_norm(j0, i, per, h, meanwhile=None):
                def sums(j):
                    dve.wait_ge(b_sq[L], 3 * h + (j + 1))
                    a = 0 if 2 * j < qtok(L) else HQ
                    sq = qkt[:, 2 * j:2 * j + 2, a:QKW].rearrange("p t (g f) -> p t g f", f=ROPE)
                    dve.tensor_reduce(head_sq[:, 2 * j:2 * j + 2, a // ROPE:], sq, AX.X, ALU.add).then_inc(b_ms[L], 1)

                parts = head_sq[:].rearrange("p t g -> p g t")
                groups = (slice(0, 4), slice(4, 6))

                def halves(n):
                    tt = groups[n]
                    dve.wait_ge(b_ms[L], 5 * h + (2, 4)[n])
                    dve.tensor_tensor(head_ss[:, 0:2, tt], parts[:, 0:4:3, tt], parts[:, 1:5:3, tt],
                                      ALU.add).then_inc(b_ms[L], 1)

                def inverses(n):
                    tt = groups[n]
                    dve.wait_ge(b_rt[L], 2 * h + (n + 1))
                    dve.reciprocal(head_ss[:, :, tt], head_ss[:, :, tt]).then_inc(b_rc[L], 1)
                    dve.wait_ge(b_rc[L], 2 * h + (n + 1))

                def scaled(j):
                    job = Job(j0 + j, i, per)
                    src = job.ps().rearrange("p (t c) -> p t c", t=2)
                    for g, a, b in ((0, 0, NOPE), (2, NOPE, HQ), (1, HQ, QKW)):
                        if g == 1 or 2 * j < qtok(L):
                            r = head_ss[:, g, 2 * j:2 * j + 2].unsqueeze(2).to_broadcast([P, 2, b - a])
                            last = dve.tensor_tensor(qkt[:, 2 * j:2 * j + 2, a:b], src[:, :, a:b], r, ALU.mult)
                    job.last_read(last)

                sums(0)
                sums(1)
                halves(0)
                if meanwhile:
                    meanwhile()
                inverses(0)
                scaled(0)
                sums(2)
                halves(1)
                scaled(1)
                inverses(1)
                scaled(2)

            def b_half(n, j, i, per, h):
                job = Job(j, i, per)
                dve.wait_ge(b_hi[L], 3 * h + (n + 1))
                dst, rows, wn = ((q, P, w), (k, P, NT), (qr, ROPE, w))[n]
                scale = (qg[:, 0:1], V(L, V_KN), None)[n]
                job.last_read(lo_half(dst[1][0:rows, 0:wn], job.ps(0, wn)[0:rows], dst[0][0:rows, 0:wn], scale))

            def v_half(j, i, per, h):
                dve.wait_ge(v_hi[L], h + 1)
                job = Job(j, i, per)
                job.last_read(lo_half(v[1][:], job.ps(0, NT), v[0][:]))

            def maxima(t, j, i, per):
                job = Job(j, i, per)
                job.ready(dve)
                last = dve.tensor_reduce(nmax[:, t:t + 1], job.ps(0, NT), AX.X, ALU.max, negate=True)
                if L == 0 and t < 2:
                    last = dve.tensor_reduce(nmax[:, 4 + t:5 + t], job.ps(NT, 1024), AX.X, ALU.max, negate=True)
                last.then_inc(s_max[L], 1)

            def probabilities(t, j, i, per, h):
                Job(j, i, per).taken(dve)
                if L == 0 and t < 2:
                    dve.reciprocal(rsum[:, 4 + t:5 + t], rsum[:, 4 + t:5 + t])
                dve.reciprocal(rsum[:, t:t + 1], rsum[:, t:t + 1]).then_inc(s_rec[L], 1)
                dve.wait_ge(s_rec[L], 4 * h + (t + 1))
                if L == 0 and t < 2:
                    dve.tensor_scalar(probc[:, t], probc[:, t], rsum[:, 4 + t:5 + t], None, ALU.mult)
                dve.tensor_scalar(prob[:, t], prob[:, t], rsum[:, t:t + 1], None, ALU.mult).then_inc(s_p[L], 1)

            def attend(js, i, per, h, extras, extra):
                for n in range(4):
                    job = Job(js[n], i, per)
                    for m, e in enumerate(TJOBS[L][n]):
                        dve.wait_ge(pt_hi[L], ENTRIES[L] * h + (e + 1))
                        ins = lo_half(pt[1][e % 4][:], job.ps(512 * m, 512 * (m + 1)), pt[0][e % 4][:])
                    job.last_read(ins)
                    if n < extras:
                        extra(n)

            def attended(jpv, i, per, h):
                job = Job(jpv, i, per)
                dve.wait_ge(ca_hi[L], h + 1)
                job.last_read(lo_half(cat_a[1][:, h, 0:w], job.ps(0, w), cat_a[0][:, h, 0:w]))

            b0 = JOB["b0", L]
            if L == 1:
                spare_landed(dve)
            b_norm(b0, 0, 0, 0)
            dve.wait_ge(lat_hi[L], 4)
            job = Job(JOB["krT", L])
            job.last_read(lo_half(kr[1][0:ROPE], job.ps(0, NT)[0:ROPE], kr[0][0:ROPE]))
            for n in range(3):
                b_half(n, JOB["b0T", L] + n, 0, 0, 0)
            j0 = JOB["heads", L]
            with dve.Fori(0, HEADS - 1) as h:
                head_lo(h + (HEADS * L + 1))
                v_half(JOB["v0", L], h, J_HEAD, h)
                maxima(0, j0 + J_S[0], h, J_HEAD)
                maxima(1, j0 + J_S[1], h, J_HEAD)
                probabilities(0, j0 + J_S[0], h, J_HEAD, h)
                b_norm(j0 + J_B, h, J_HEAD, h + 1, lambda: probabilities(1, j0 + J_S[1], h, J_HEAD, h))
                for t in range(2, XTOK):
                    maxima(t, j0 + J_S[t], h, J_HEAD)
                    if t > 2:
                        probabilities(t - 1, j0 + J_S[t - 1], h, J_HEAD, h)
                probabilities(XTOK - 1, j0 + J_S[XTOK - 1], h, J_HEAD, h)
                b_half(0, j0 + J_BT[0], h, J_HEAD, h + 1)
                attend([j0 + x for x in J_T], h, J_HEAD, h, 2,
                       lambda n: b_half(n + 1, j0 + J_BT[n + 1], h, J_HEAD, h + 1))
                attended(j0 + J_PV, h, J_HEAD, h)
            v_half(JOB["last", L] - 1, 0, 0, HEADS - 1)
            if L == 0:
                head_lo(HEADS)
            j0 = JOB["last", L]
            for t in range(XTOK):
                maxima(t, j0 + J_LS[t], 0, 0)
                if t:
                    probabilities(t - 1, j0 + J_LS[t - 1], 0, 0, HEADS - 1)
            probabilities(XTOK - 1, j0 + J_LS[XTOK - 1], 0, 0, HEADS - 1)

            def mix_lo(j):
                dve.wait_ge(cy_hi[L], j + 1)
                lo_half(cat_y[1][:, j, 0:w], ymix[j][:, 0:w], cat_y[0][:, j, 0:w]).then_inc(cy_lo[L], 1)
            attend([j0 + 4, j0 + 5, j0 + 7, j0 + 8], 0, 0, HEADS - 1, 4, mix_lo)
            attended(j0 + 6, 0, 0, HEADS - 1)
            nn = 2 * L + 1
            clear_ss(nn)
            with dve.Fori(0, 2) as i:
                for j in range(4):
                    job = Job(JOB["wo", L] + j, i, 4)
                    if L == 0:
                        ada_chunks(8 + j // 2, ADA_WO[j % 2], i, 2)
                    job.ready(dve)
                    if L == 0 and j % 2 == 1:
                        ada_out(0, 2 * i + (8 + j // 2), job).then_inc(mod_done, 1)
                    update_x(4 * i + j, L, job, 16)
                    split_lo(c0 + 16 + j, i, 4)
                    add_squares(nn, 4 * i + j, j % 2)
            norm(nn, JOB["norm2", L])
            if L == 0:
                ada_pair(12)

            def ff_tile(t, jn, c, par, buf, i, per_j, per_c, ada=None):
                g, u = Job(jn, i, per_j), Job(jn + 1, i, per_j)
                if ada is not None:
                    ada_chunks(ada, ADA_UP[par][0], i, 2, ada_acc, 16 - ada)
                dve.wait_ge(ff_mid[L], t + 1)
                n, per_tile = 0, 2 * len(sg) - 1
                for tap, d0, s0 in ((0, 1, 0), (2, 0, 1)):
                    for _, a, b in sg:
                        if n:
                            dve.wait_ge(ff_conv[L], per_tile * t + n)
                        y = tmp[par][:, a + d0:b - 1 + d0]
                        ins = dve.scalar_tensor_tensor(y, g.ps(a + s0, b - 1 + s0),
                                                       vec[:, bass.ds(L * V_LAYER + V_FC + FT * tap + t, 1)], y,
                                                       ALU.mult, ALU.add)
                        n += 1
                        if n <= per_tile:
                            ins.then_inc(ff_conv[L], 1)
                        else:
                            g.last_read(ins)
                split_lo(c, i, per_c)
                if ada is not None:
                    ada_chunks(ada, ADA_UP[par][1], i, 2, ada_acc, 16 - ada)
                u.ready(dve)
                dve.wait_ge(ff_silu[L], t + 1)
                return u

            def ff_value(t, u, c, par, buf, i, per_c):
                u.last_read(dve.tensor_tensor(ff_v[:, 0:w], tmp[par][:, 0:w], u.ps(0, w), ALU.mult))
                split_lo(c + 1, i, per_c)
                dve.wait_ge(ff_hi[L], t + 1)
                lo_half(inner[1][buf][:, par, 0:w], ff_v[:, 0:w],
                        inner[0][buf][:, par, 0:w]).then_inc(ff_lo[L], 1)

            for t in range(2):
                u = ff_tile(t, JOB["u0", L] + 2 * t, c0 + C_FF + 4 + 2 * t, t, 0, 0, 0, 0)
                if L == 0 and t == 1:
                    o = 4 * (ADB - 2)
                    dve.tensor_tensor(mod[1][:, 0, o:o + 8], u.ps(768, 776), V(1, V_ADAB + o, 8),
                                      ALU.add).then_inc(mod_done, 2)
                ff_value(t, u, c0 + C_FF + 4 + 2 * t, t, 0, 0, 0)
            jf = JOB["ff", L]
            with dve.Fori(0, (FP - 1) // 2) as i:
                for d in range(2):
                    c = c0 + C_FF + 4 + 6 * d
                    for t in range(2):
                        tile, cc = 4 * i + (2 * (d + 1) + t), c + 4 + 2 * t
                        u = ff_tile(tile, jf + 12 * d + 2 * t, cc, t, 1 - d, i, 24, 12, 14 + d if L == 0 else None)
                        ff_value(tile, u, cc, t, 1 - d, i, 12)
                    for m in range(KD):
                        job = Job(jf + 12 * d + 4 + m, i, 24)
                        job.ready(dve)
                        if L == 0 and m == KD - 1:
                            ada_out(1, i + ADB_X * d, job, 2 - d).then_inc(mod_done, 1)
                        update_x(m, L, job, 40)
                    for x in range(2):
                        split_lo(c + 8 + x, i, 12)
            if L == 0:
                clear_ss(2)
            for m in range(KD):
                job = Job(JOB["dlast", L] + m)
                job.ready(dve)
                update_x(m, L, job, 40)
                if L == 0 and m:
                    add_squares(2, m - 1, (m - 1) % 2)
            if L == 0:
                add_squares(2, KD - 1, (KD - 1) % 2)
                for x in range(2):
                    split_lo(c0 + NCH + 2 + x)

    ctx.close()


def pack_vectors(a):
    cols = np.zeros((P, NV), np.float32)

    def put(c, x):
        x = np.asarray(x, np.float32).reshape(-1, P).T
        cols[:, c:c + x.shape[1]] = x
    for L in range(DEPTH):
        o = L * V_LAYER
        for c, name in ((V_N1, "norm1_g"), (V_N2, "norm2_g"), (V_ADAB, "ada_b"), (V_QC, "qc_g"), (V_KVC, "kvc_g"),
                        (V_QN, "qn_g"), (V_KN, "kn_g"), (V_PS, "pool_scale")):
            put(o + c, a[name][L])
        for m in range(2):
            for tap in range(3):
                put(o + V_SC + 3 * m + tap, a["sconv_w"][L][tap, P * m:P * (m + 1)])
        for tap in range(3):
            put(o + V_FC + FT * tap, a["ff_conv"][L][tap])
    put(V_C, a["c"][0])
    put(V_C + 8, a["c_ctx"])
    for m, pair in enumerate(((2, 4), (8, 16))):
        for half, win in enumerate(pair):
            rows = slice(64 * half, 64 * half + 64)
            cols[rows, V_INVW + m] = 1.0 / win
            for t in range(PAD):
                left = min(t + win // 2, NC) - max(t - win // 2, 0)
                right = min(NC - PAD + t + win // 2, NC) - (NC - PAD + t - win // 2)
                cols[rows, V_RATIO + 16 * m + t] = win / left
                cols[rows, V_RATIO + 16 * m + 8 + t] = win / right
    cols[:, V_EPS] = EPS
    return cols


def rope_tables():
    t = np.arange(NX)
    nf = ROPE // 4
    inv = (10000.0 ** (-np.arange(nf, dtype=np.float32) / nf)).astype(np.float32)
    ar = (t // GRID_W).astype(np.float32)[:, None] * inv
    ac = (t % GRID_W).astype(np.float32)[:, None] * inv
    ang = np.concatenate([ar, ar, ac, ac], axis=-1)
    sign = np.tile(np.repeat(np.array([-1.0, 1.0], np.float32), nf), 2)
    tab = np.zeros((2, NT, ROPE), np.float32)
    tab[0] = 1.0
    tab[0, :NX] = np.cos(ang)
    tab[1, :NX] = np.sin(ang) * sign
    return np.ascontiguousarray(tab.reshape(2, TOK, P, ROPE).transpose(2, 0, 1, 3))


def tiles(w):
    n = w.shape[1] // P
    return w.reshape(KD, P, n, P).transpose(2, 1, 0, 3).reshape(n, P, CH)


def layout(a):
    a = {n: np.asarray(x) for n, x in a.items()}
    main = np.zeros((DEPTH * NCH + SPARE, P, CH), np.float32)
    heads = np.zeros((DEPTH * HEADS, P, 2 * HQ + 2 * NOPE), np.float32)
    rgain = np.zeros((DEPTH, 4, ROPE), np.float32)
    partner = np.arange(ROPE).reshape(2, 2, ROPE // 4)[:, ::-1].reshape(-1)
    for L in range(DEPTH):
        w_in, m = a["w_in"][L], main[NCH * L:NCH * (L + 1)]
        lat = w_in[:, :LATW].reshape(4, 2, P, LATW).transpose(0, 2, 1, 3).reshape(4, P, 2 * LATW)
        m[C_LAT:C_LAT + 4, :, :2 * LATW] = lat
        rest = tiles(np.ascontiguousarray(w_in[:, LATW:]))
        m[C_A2:C_A2 + 8] = rest[[0, 4, 6, 2, 1, 5, 7, 3]]
        m[C_WO:C_WO + 8] = tiles(a["w_o"][L])
        up = tiles(a["ff_up"][L])
        down = a["ff_down"][L].reshape(FT, P, D)
        c = C_FF
        for p in range(FP + 1):
            if p < FP:
                m[c:c + 4] = up[[2 * p, FT + 2 * p, 2 * p + 1, FT + 2 * p + 1]]
                c += 4
            if p:
                m[c:c + 2] = down[2 * p - 2:2 * p]
                c += 2
        wq = a["w_q_up"][L].reshape(2, P, HEADS, HQ)
        wkv = a["w_kv_up"][L].reshape(P, HEADS, NOPE + P)
        for h in range(HEADS):
            w = heads[HEADS * L + h]
            w[:, :2 * HQ] = wq[:, :, h].transpose(1, 0, 2).reshape(P, 2 * HQ)
            w[:, 2 * HQ:] = wkv[:, h]
        rgain[L] = [a["qr_g"][L], a["qr_g"][L][partner], a["kr_g"][L], a["kr_g"][L][partner]]
    ada = a["ada_w"].reshape(DEPTH, KD, P, ADB, ADC).transpose(0, 3, 1, 2, 4).reshape(DEPTH * ADB, KD, P, ADC)
    order = list(range(ADB)) + [2 * ADB - 2, 2 * ADB - 1]
    order += [ADB + i + ADB_X * d for i in range(ADB_X) for d in range(2)]
    ada = ada[order]
    ada[ADB:ADB + 2] = ada[ADB:ADB + 2].transpose(1, 0, 2, 3).reshape(2, KD, P, ADC)
    ada = np.concatenate([ada.reshape(DEPTH * ADB * KD, P, ADC), np.zeros((ADA_SPARE, P, ADC), np.float32)])
    return {
        "x": a["x"][0].T.reshape(KD, P, NX).transpose(1, 0, 2), "ctx": a["ctx"][0].T.reshape(KD, P, NC).transpose(1, 0, 2),
        "vec": pack_vectors(a), "rope": rope_tables(), "rgain": rgain, "pool_w": a["pool_w"],
        "w_main": main, "w_head": heads, "w_ada": ada,
    }


def kernel(**inputs):
    import concourse.bacc as bacc
    from concourse.bass_utils import run_bass_kernel_spmd

    nc = bacc.Bacc("TRN2", target_bir_lowering=False, num_devices=1)
    arrays, dram = {}, {}
    for name, x in layout(inputs).items():
        arrays[f"in_{name}"] = np.ascontiguousarray(x)
        dram[name] = nc.dram_tensor(f"in_{name}", x.shape, F32, kind="ExternalInput").ap()
    dram["out"] = nc.dram_tensor("out_x", (KD, P, NX), F32, kind="ExternalOutput").ap()
    build(nc, dram)
    r = run_bass_kernel_spmd(nc, [arrays], core_ids=[0])
    return np.ascontiguousarray(r.results[0]["out_x"].reshape(D, NX).T)[None]
```
